# Optimizing a Trainium2 kernel written in Bass

```python
import jax, jax.numpy as jnp
from jax import lax
import numpy as np

D_MODEL = 1024
BATCH = 1
SEQ = 128
DEPTH = 1
DEC_BATCH = 1
DEC_SEQ = 512
PAST_LEN = 128

GRID_W = 64
N_BRANCH = 4
BRANCH_WIDTH = D_MODEL // 4
FT_GROUPS = 4
FT_GROUP = BRANCH_WIDTH // FT_GROUPS
RW_HEAD = 64
RW_HEADS = BRANCH_WIDTH // RW_HEAD
RW_LORA_W = 32
RW_LORA_A = 32
RW_LORA_G = 64
RW_GN_EPS = 64e-5
GLA_HEADS = 4
GLA_DV = BRANCH_WIDTH // GLA_HEADS
GLA_DK = GLA_DV // 2
GLA_KEY_WIDTH = GLA_HEADS * GLA_DK
GLA_RANK = 16
GLA_TAU = 16.0
GLA_CHUNK = 64
CONV_W = 3
N_EXPERTS = 64
EXPERT_FF = 256
SHARED_FF = 256
TOP_K = 8
N_GROUPS = 8
TOPK_GROUPS = 4
ROUTED_SCALE = 2.5
MOE_BLOCK = 128
NORM_EPS = 1e-6

IN_SIZES = (BRANCH_WIDTH,
            BRANCH_WIDTH, BRANCH_WIDTH, BRANCH_WIDTH,
            2 * RW_LORA_W, 2 * RW_LORA_A, RW_LORA_G,
            GLA_KEY_WIDTH, GLA_KEY_WIDTH, BRANCH_WIDTH,
            2 * GLA_RANK, BRANCH_WIDTH,
            BRANCH_WIDTH, BRANCH_WIDTH, BRANCH_WIDTH,
            N_BRANCH * D_MODEL)
IN_WIDTH = sum(IN_SIZES)

kernel_name = 'hybrid_fourier_rwkv7_gla_conv_moe_dit_step'

def rmsnorm(x, g):
    xf = x.astype(jnp.float32)
    y = xf * lax.rsqrt(jnp.mean(xf * xf, axis=-1, keepdims=True) + NORM_EPS)
    return (y * g).astype(x.dtype)

def swiglu(x, w_gate, w_up, w_down):
    return (jax.nn.silu(x @ w_gate) * (x @ w_up)) @ w_down

def ada_modulation(cvec, w_mod, b_mod):
    m = jax.nn.silu(cvec) @ w_mod + b_mod
    return jnp.split(m[:, None, :], 6, axis=-1)

def fourier_mixer(u, grid):
    B, L, _ = u.shape
    uf = u.astype(jnp.float32).reshape(B, L, FT_GROUPS, FT_GROUP)
    if grid:
        rows = L // GRID_W
        y = jnp.fft.fftn(uf.reshape(B, rows, GRID_W, FT_GROUPS, FT_GROUP), axes=(1, 2, 4), norm='ortho').real
    else:
        y = jnp.fft.fftn(uf, axes=(1, 3), norm='ortho').real
    return y.reshape(B, L, BRANCH_WIDTH)

def rwkv7_scan(r, w, k, v, a, b, s0):
    def step(S, xs):
        rt, wt, kt, vt, at, bt = xs
        sa = jnp.einsum('bhvk,bhk->bhv', S, at)
        S = S * wt[:, :, None, :] + sa[..., None] * bt[:, :, None, :] + vt[..., None] * kt[:, :, None, :]
        return S, jnp.einsum('bhvk,bhk->bhv', S, rt)
    xs = tuple(jnp.swapaxes(t, 0, 1) for t in (r, w, k, v, a, b))
    s_final, y = lax.scan(step, s0, xs)
    return jnp.swapaxes(y, 0, 1), s_final

def rwkv7_mixer(r, k, v, w_dn, a_dn, g_dn, p, s0):
    B, L, _ = r.shape
    f32 = jnp.float32
    heads = lambda t: t.reshape(B, L, RW_HEADS, RW_HEAD)
    r, k, v = r.astype(f32), k.astype(f32), v.astype(f32)
    w_dn = w_dn.astype(f32).reshape(B, L, 2, RW_LORA_W)
    a_dn = a_dn.astype(f32).reshape(B, L, 2, RW_LORA_A)
    kk = heads(k * p['rw_k_k'])
    kk = kk / jnp.maximum(jnp.sqrt(jnp.sum(kk * kk, axis=-1, keepdims=True)), 1e-12)
    rh, vh = heads(r), heads(v)
    ys, bonus, finals = [], [], []
    for d in range(2):
        log_w = -jax.nn.softplus(-(p['rw_w0'][d] + jnp.tanh(w_dn[:, :, d]) @ p['rw_w_up'][d])) - 0.5
        decay = heads(jnp.exp(-jnp.exp(log_w)))
        a = jax.nn.sigmoid(p['rw_a0'][d] + a_dn[:, :, d] @ p['rw_a_up'][d])
        kd = heads(k * (1.0 + (a - 1.0) * p['rw_k_a']))
        seq = (rh, decay, kd, vh, -kk, kk * heads(a))
        if d == 1:
            seq = tuple(jnp.flip(t, axis=1) for t in seq)
        y, s_final = rwkv7_scan(*seq, s0[:, d])
        ys.append(jnp.flip(y, axis=1) if d == 1 else y)
        bonus.append(jnp.sum(rh * kd * p['rw_r_k'], axis=-1, keepdims=True) * vh)
        finals.append(s_final)
    y = ys[0] + ys[1]
    mu = jnp.mean(y, axis=-1, keepdims=True)
    var = jnp.mean(jnp.square(y - mu), axis=-1, keepdims=True)
    y = ((y - mu) * lax.rsqrt(var + RW_GN_EPS)).reshape(B, L, BRANCH_WIDTH) * p['rw_ln_w'] + p['rw_ln_b']
    y = y + (bonus[0] + bonus[1]).reshape(B, L, BRANCH_WIDTH)
    g = jax.nn.sigmoid(g_dn.astype(f32)) @ p['rw_g_up']
    return y * g, jnp.stack(finals, axis=1)

def to_chunks(t):
    B, L, H, X = t.shape
    return jnp.transpose(t.reshape(B, L // GLA_CHUNK, GLA_CHUNK, H, X), (1, 0, 3, 2, 4))

def gla_chunked(q, k, v, log_a, s0):
    B, L, H, _ = q.shape
    qc, kc, vc, lc = to_chunks(q), to_chunks(k), to_chunks(v), to_chunks(log_a)
    b = jnp.cumsum(lc, axis=3)
    causal = jnp.tril(jnp.ones((GLA_CHUNK, GLA_CHUNK), dtype=bool))
    rel = jnp.where(causal[:, :, None], b[..., :, None, :] - b[..., None, :, :], -jnp.inf)
    scores = jnp.einsum('nbhik,nbhjk,nbhijk->nbhij', qc, kc, jnp.exp(rel))
    o_intra = jnp.einsum('nbhij,nbhjv->nbhiv', scores, vc)
    b_last = b[..., -1:, :]
    q_dec = qc * jnp.exp(b)
    k_dec = kc * jnp.exp(b_last - b)
    chunk_decay = jnp.exp(b_last[..., 0, :])

    def step(S, xs):
        qd, kd, vv, cd = xs
        o = jnp.einsum('bhik,bhkv->bhiv', qd, S)
        S = S * cd[..., None] + jnp.einsum('bhjk,bhjv->bhkv', kd, vv)
        return S, o

    s_final, o_inter = lax.scan(step, s0, (q_dec, k_dec, vc, chunk_decay))
    o = o_intra + o_inter
    return jnp.transpose(o, (1, 0, 3, 2, 4)).reshape(B, L, H, -1), s_final

def gla_mixer(q, k, v, a_dn, g, p, s0):
    B, L, _ = q.shape
    f32 = jnp.float32
    q = q.astype(f32).reshape(B, L, GLA_HEADS, GLA_DK) * (GLA_DK ** -0.5)
    k = k.astype(f32).reshape(B, L, GLA_HEADS, GLA_DK)
    v = v.astype(f32).reshape(B, L, GLA_HEADS, GLA_DV)
    a_dn = a_dn.astype(f32).reshape(B, L, 2, GLA_RANK)
    outs, finals = [], []
    for d in range(2):
        log_a = jax.nn.log_sigmoid(a_dn[:, :, d] @ p['gla_a_up'][d] + p['gla_a_b'][d]) / GLA_TAU
        seq = (q, k, v, log_a.reshape(B, L, GLA_HEADS, GLA_DK))
        if d == 1:
            seq = tuple(jnp.flip(t, axis=1) for t in seq)
        o, s_final = gla_chunked(*seq, s0[:, d])
        outs.append(jnp.flip(o, axis=1) if d == 1 else o)
        finals.append(s_final)
    o = outs[0] + outs[1]
    o = o * lax.rsqrt(jnp.mean(o * o, axis=-1, keepdims=True) + NORM_EPS)
    o = o.reshape(B, L, BRANCH_WIDTH) * p['gla_norm'] * jax.nn.silu(g.astype(f32))
    return o, jnp.stack(finals, axis=1)

def short_conv_mixer(b, c, x, w):
    z = c * x
    zp = jnp.pad(z, ((0, 0), (1, 1), (0, 0)))
    return b * (w[0] * zp[:, :-2] + w[1] * zp[:, 1:-1] + w[2] * zp[:, 2:])

def token_mixing(h, p, s_rwkv, s_gla, grid):
    B, L, _ = h.shape
    cuts = np.cumsum(IN_SIZES)[:-1].tolist()
    (ft_u, rw_r, rw_k, rw_v, rw_wd, rw_ad, rw_gd,
     gl_q, gl_k, gl_v, gl_ad, gl_g,
     sc_b, sc_c, sc_x, merge_logits) = jnp.split(h @ p['w_in'], cuts, axis=-1)
    y_ft = fourier_mixer(ft_u, grid)
    y_rw, fin_rwkv = rwkv7_mixer(rw_r, rw_k, rw_v, rw_wd, rw_ad, rw_gd, p, s_rwkv)
    y_gl, fin_gla = gla_mixer(gl_q, gl_k, gl_v, gl_ad, gl_g, p, s_gla)
    y_sc = short_conv_mixer(sc_b, sc_c, sc_x, p['conv_w'])
    branches = jnp.stack([t.astype(h.dtype) for t in (y_ft, y_rw, y_gl, y_sc)], axis=2)
    proj = jnp.einsum('blnc,ncd->blnd', branches, p['w_branch'])
    gates = jax.nn.sigmoid(merge_logits.reshape(B, L, N_BRANCH, D_MODEL))
    merged = jnp.sum(gates * proj, axis=2)
    return merged @ p['w_out'], fin_rwkv, fin_gla

def routed_experts(t, idx, gate, wg, wu, wd):
    T, K = idx.shape
    D = t.shape[-1]
    A = T * K
    flat_e = idx.reshape(A)
    order = jnp.argsort(flat_e)
    e_sorted = flat_e[order]
    counts = jnp.bincount(flat_e, length=N_EXPERTS)
    starts = jnp.cumsum(counts) - counts
    padded = (counts + MOE_BLOCK - 1) // MOE_BLOCK * MOE_BLOCK
    pad_end = jnp.cumsum(padded)
    pad_start = pad_end - padded
    slot = pad_start[e_sorted] + (jnp.arange(A) - starts[e_sorted])
    n_blocks = -(-A // MOE_BLOCK) + N_EXPERTS
    P = n_blocks * MOE_BLOCK
    slot_tok = jnp.full((P,), T, jnp.int32).at[slot].set((order // K).astype(jnp.int32))
    slot_gate = jnp.zeros((P,), t.dtype).at[slot].set(gate.reshape(A)[order])
    blk_expert = jnp.minimum(jnp.searchsorted(pad_end, jnp.arange(n_blocks) * MOE_BLOCK, side='right'), N_EXPERTS - 1)
    t_pad = jnp.concatenate([t, jnp.zeros((1, D), t.dtype)], axis=0)

    def block(args):
        tok, g, e = args
        xb = t_pad[tok]
        hb = jax.nn.silu(xb @ wg[e]) * (xb @ wu[e])
        return (hb @ wd[e]) * g[:, None]

    yb = lax.map(block, (slot_tok.reshape(n_blocks, MOE_BLOCK), slot_gate.reshape(n_blocks, MOE_BLOCK), blk_expert))
    out = jnp.zeros((T + 1, D), yb.dtype).at[slot_tok].add(yb.reshape(P, D))
    return out[:T]

def moe_ffn(h, p):
    B, L, D = h.shape
    t = h.reshape(B * L, D)
    T = t.shape[0]
    scores = jax.nn.sigmoid((t @ p['w_router']).astype(jnp.float32))
    sel = scores + p['b_router'].astype(jnp.float32)
    grp_score = jnp.sum(lax.top_k(sel.reshape(T, N_GROUPS, N_EXPERTS // N_GROUPS), 2)[0], axis=-1)
    _, top_g = lax.top_k(grp_score, TOPK_GROUPS)
    gmask = jnp.sum(jax.nn.one_hot(top_g, N_GROUPS, dtype=jnp.float32), axis=1) > 0
    emask = jnp.repeat(gmask, N_EXPERTS // N_GROUPS, axis=-1)
    _, idx = lax.top_k(jnp.where(emask, sel, -jnp.inf), TOP_K)
    w = jnp.take_along_axis(scores, idx, axis=-1)
    w = w / jnp.sum(w, axis=-1, keepdims=True) * ROUTED_SCALE
    routed = routed_experts(t, idx, w.astype(t.dtype), p['we_gate'], p['we_up'], p['we_down'])
    shared = swiglu(t, p['ws_gate'], p['ws_up'], p['ws_down'])
    return (routed + shared).reshape(B, L, D)

def trunk_layer(x, mods, p, s_rwkv, s_gla, grid):
    shift_a, scale_a, gate_a, shift_f, scale_f, gate_f = mods
    h = rmsnorm(x, p['g_norm_mix']) * (1.0 + scale_a) + shift_a
    mix, fin_rwkv, fin_gla = token_mixing(h, p, s_rwkv, s_gla, grid)
    x = x + (gate_a * mix).astype(x.dtype)
    h = rmsnorm(x, p['g_norm_ffn']) * (1.0 + scale_f) + shift_f
    x = x + (gate_f * moe_ffn(h, p)).astype(x.dtype)
    return x, fin_rwkv, fin_gla

def setup_inputs(seed: int = 0) -> dict:
    key = jax.random.key(seed)
    ks = iter(jax.random.split(key, 48))
    nrm = lambda shape, s: jax.random.normal(next(ks), shape, jnp.float32) * s
    D = D_MODEL
    BW = BRANCH_WIDTH
    return {
        'x_prompt': nrm((BATCH, SEQ, D), 1.0),
        'x_sample': nrm((DEC_BATCH, DEC_SEQ, D), 1.0),
        'state_rwkv': nrm((DEC_BATCH, DEPTH, 2, RW_HEADS, RW_HEAD, RW_HEAD), 0.1),
        'state_gla': nrm((DEC_BATCH, DEPTH, 2, GLA_HEADS, GLA_DK, GLA_DV), 0.1),
        'c': nrm((DEC_BATCH, D), 1.0),
        'c_ctx': nrm((D,), 1.0),
        'w_mod': nrm((DEPTH, D, 6 * D), 0.5 * D ** -0.5),
        'b_mod': nrm((DEPTH, 6 * D), 0.02),
        'g_norm_mix': 1.0 + nrm((DEPTH, D), 0.05),
        'g_norm_ffn': 1.0 + nrm((DEPTH, D), 0.05),
        'w_in': nrm((DEPTH, D, IN_WIDTH), D ** -0.5),
        'rw_w0': nrm((DEPTH, 2, BW), 0.5),
        'rw_w_up': nrm((DEPTH, 2, RW_LORA_W, BW), RW_LORA_W ** -0.5),
        'rw_a0': nrm((DEPTH, 2, BW), 0.5),
        'rw_a_up': nrm((DEPTH, 2, RW_LORA_A, BW), RW_LORA_A ** -0.5),
        'rw_g_up': nrm((DEPTH, RW_LORA_G, BW), RW_LORA_G ** -0.5),
        'rw_k_k': 0.85 + nrm((DEPTH, BW), 0.05),
        'rw_k_a': 1.0 + nrm((DEPTH, BW), 0.05),
        'rw_r_k': nrm((DEPTH, RW_HEADS, RW_HEAD), 0.1),
        'rw_ln_w': 1.0 + nrm((DEPTH, BW), 0.05),
        'rw_ln_b': nrm((DEPTH, BW), 0.02),
        'gla_a_up': nrm((DEPTH, 2, GLA_RANK, GLA_KEY_WIDTH), GLA_RANK ** -0.5),
        'gla_a_b': nrm((DEPTH, 2, GLA_KEY_WIDTH), 0.5),
        'gla_norm': 1.0 + nrm((DEPTH, BW), 0.05),
        'conv_w': nrm((DEPTH, CONV_W, BW), 0.5),
        'w_branch': nrm((DEPTH, N_BRANCH, BW, D), BW ** -0.5),
        'w_out': nrm((DEPTH, D, D), D ** -0.5),
        'w_router': nrm((DEPTH, D, N_EXPERTS), D ** -0.5),
        'b_router': nrm((DEPTH, N_EXPERTS), 0.01),
        'we_gate': nrm((DEPTH, N_EXPERTS, D, EXPERT_FF), D ** -0.5),
        'we_up': nrm((DEPTH, N_EXPERTS, D, EXPERT_FF), D ** -0.5),
        'we_down': nrm((DEPTH, N_EXPERTS, EXPERT_FF, D), EXPERT_FF ** -0.5),
        'ws_gate': nrm((DEPTH, D, SHARED_FF), D ** -0.5),
        'ws_up': nrm((DEPTH, D, SHARED_FF), D ** -0.5),
        'ws_down': nrm((DEPTH, SHARED_FF, D), SHARED_FF ** -0.5),
        'g_final': 1.0 + nrm((D,), 0.05),
    }

def reference(x_prompt, x_sample, state_rwkv, state_gla, c, c_ctx,
              w_mod, b_mod, g_norm_mix, g_norm_ffn, w_in,
              rw_w0, rw_w_up, rw_a0, rw_a_up, rw_g_up, rw_k_k, rw_k_a, rw_r_k, rw_ln_w, rw_ln_b,
              gla_a_up, gla_a_b, gla_norm, conv_w, w_branch, w_out,
              w_router, b_router, we_gate, we_up, we_down, ws_gate, ws_up, ws_down, g_final):
    f32 = jnp.float32
    layers = [dict(w_mod=w_mod[l], b_mod=b_mod[l], g_norm_mix=g_norm_mix[l], g_norm_ffn=g_norm_ffn[l],
                   w_in=w_in[l], rw_w0=rw_w0[l], rw_w_up=rw_w_up[l], rw_a0=rw_a0[l], rw_a_up=rw_a_up[l],
                   rw_g_up=rw_g_up[l], rw_k_k=rw_k_k[l], rw_k_a=rw_k_a[l], rw_r_k=rw_r_k[l],
                   rw_ln_w=rw_ln_w[l], rw_ln_b=rw_ln_b[l], gla_a_up=gla_a_up[l], gla_a_b=gla_a_b[l],
                   gla_norm=gla_norm[l], conv_w=conv_w[l], w_branch=w_branch[l], w_out=w_out[l],
                   w_router=w_router[l], b_router=b_router[l], we_gate=we_gate[l], we_up=we_up[l],
                   we_down=we_down[l], ws_gate=ws_gate[l], ws_up=ws_up[l], ws_down=ws_down[l])
              for l in range(DEPTH)]

    B = x_prompt.shape[0]
    zero_rwkv = jnp.zeros((B, 2, RW_HEADS, RW_HEAD, RW_HEAD), f32)
    zero_gla = jnp.zeros((B, 2, GLA_HEADS, GLA_DK, GLA_DV), f32)
    h = x_prompt
    ctx_rwkv, ctx_gla = [], []
    for l in range(DEPTH):
        p = layers[l]
        mods = ada_modulation(c_ctx[None, :], p['w_mod'], p['b_mod'])
        h, fin_rwkv, fin_gla = trunk_layer(h, mods, p, zero_rwkv, zero_gla, False)
        ctx_rwkv.append(fin_rwkv)
        ctx_gla.append(fin_gla)
    y_prompt = rmsnorm(h, g_final)
    new_state_rwkv = jnp.stack(ctx_rwkv, axis=1)
    new_state_gla = jnp.stack(ctx_gla, axis=1)

    z = x_sample
    for l in range(DEPTH):
        p = layers[l]
        mods = ada_modulation(c, p['w_mod'], p['b_mod'])
        z, _, _ = trunk_layer(z, mods, p, state_rwkv[:, l].astype(f32), state_gla[:, l].astype(f32), True)
    y_sample = rmsnorm(z, g_final)

    return (y_prompt, y_sample, new_state_rwkv, new_state_gla)


_drawn_inputs = setup_inputs


def setup_inputs(seed=0):
    import zlib

    import numpy as np

    out = dict(_drawn_inputs(seed))
    spreads = {}
    factors = {'state_rwkv': 33.621,
     'state_gla': 36.167,
     'rw_k_k': 32.534,
     'rw_ln_w': 3.079,
     'rw_ln_b': 14.486,
     'gla_norm': 2.875}
    for name, (base, spread) in spreads.items():
        noise = np.random.default_rng([zlib.crc32(name.encode()), seed]).standard_normal(out[name].shape)
        drawn = base * np.exp(spread * noise) if base else spread * noise
        out[name] = __import__('jax').numpy.asarray(drawn.astype(out[name].dtype))
    for name, factor in factors.items():
        out[name] = (out[name] * factor).astype(out[name].dtype)
    return out
```

```python
from contextlib import ExitStack

import numpy as np

import concourse.bass as bass
from concourse import mybir

F32, U32, I32 = mybir.dt.float32, mybir.dt.uint32, mybir.dt.int32
ALU = mybir.AluOpType
ACT = mybir.ActivationFunctionType
AX = mybir.AxisListType

P = 128
D = 1024
KD = D // P
T_LAT, T_CTX = 512, 128
T = T_LAT + T_CTX
NT = T // P
CTX = NT - 1
BW = 256
NB = 4
EPS = 1e-6

(U_, R_, K_, V_, WA, GDGA, GQ, GK, GV, GG, SB_, SC_, SX) = (0, 2, 4, 6, 8, 9, 10, 11, 12, 14, 16, 18, 20)
N_MIX = 22
GA = 64

(W0, A0, KK, KA, RK, LNW, LNB, GAB, GNORM, CONV) = (0, 4, 8, 10, 12, 14, 16, 18, 20, 22)
N_VEC = 28

LEVELS = (1, 2, 4, 8, 16, 32, 64)
(IDENT, HEADS, LT, GT, LE, GE, LEV_F, LEV_B) = (0, 1, 2, 3, 4, 5, 6, 13)
(ONES, GBLK, C_END) = (20, 21, 23)


class Chain:

    def __init__(self, eng, sem):
        self.eng, self.sem, self.base, self.k = eng, sem, 0, 0

    def link(self, ins):
        ins.then_inc(self.sem, 1)
        self.k += 1
        self.eng.wait_ge(self.sem, self.base + self.k)

    def laps(self, n, per):
        return _Laps(self, n, per)


class _Laps:
    def __init__(self, chain, n, per):
        self.chain, self.n, self.per = chain, n, per

    def __enter__(self):
        c = self.chain
        self.start = c.k
        self.fori = c.eng.Fori(0, self.n)
        i = self.fori.__enter__()
        c.base, c.k = i * self.per + self.start, 0
        return i

    def __exit__(self, *e):
        c = self.chain
        if e[0] is None:
            assert c.k == self.per, (c.k, self.per)
        c.base = 0
        c.k = self.start + self.n * self.per if isinstance(self.n, int) else 0
        return self.fori.__exit__(*e)


def flat(ap):
    return ap.rearrange("p a b -> p (a b)")


class Tools:

    def __init__(self, nc, stage=""):
        self.nc, self.stage, self.ctx, self.used = nc, stage, ExitStack(), []

    def __enter__(self):
        return self

    def __exit__(self, *e):
        if e[0] is None and self.used:
            self.nc.clear_and_free_semaphores(self.used)
            self.nc.all_engine_barrier()
        return self.ctx.__exit__(*e)

    def sb(self, name, shape, dt=F32):
        return self.ctx.enter_context(self.nc.sbuf_tensor(name, shape, dt, allow_name_mangling=True))

    def ps(self, name, shape):
        return self.ctx.enter_context(self.nc.psum_tensor(name, shape, F32, allow_name_mangling=True))

    def sem(self, name):
        self.used.append(self.nc.alloc_semaphore(f"{self.stage}_{name}"))
        return self.used[-1]

    def sems(self, *names):
        return [self.sem(n) for n in names]

    def ring(self, name, n):
        return [self.sem(f"{name}{i}") for i in range(n)]


def norm_and_project(nc, m):
    RING = 4
    N_COL = 6 * D // 512
    N_FIRST = 2 * D // 512
    with Tools(nc, "norm_and_project") as a:
        hT = a.sb("hT", [P, KD, T])
        c_act, c_raw = a.sb("c_act", [P, KD, 2]), a.sb("c_raw", [P, KD, 2])
        wmod = a.sb("wmod", [P, RING, KD, 512])
        g_row = a.sb("g_row", [2, 2, D])
        rows = a.sb("mod_rows", [2, 6, D])
        w = a.sb("w_tiles", [P, 2, KD * P])
        mean_sq, rms, rstd = (a.sb(n, [P, NT]) for n in ("mean_sq", "rms", "rstd"))
        mod_c = a.sb("mod_c", [P, 2, KD, 2])
        spare = flat(m.proj[:])
        x = spare[:, 0:NT * D].rearrange("p (t d) -> p t d", t=NT)
        xn = spare[:, NT * D:(NT + 2) * D].rearrange("p (b d) -> p b d", b=2)
        square = spare[:, (NT + 2) * D:(NT + 3) * D]
        ps_mod = a.ps("ps_mod", [2, 2, 512])
        ps_cols = a.ps("ps_cols", [P, 2 * KD * 2])
        ps = a.ps("ps_turn_and_in", [P, 2, 1024])
        (vecs_in, rows_in, x_in, mod_mm, mod_added, mod_out, hT_out, act_chain, dve_chain, c_ready, ssq_ready,
         rms_ready, rows_ready, cols_mm, xn_ready, xn_turned, hT_ready) = a.sems(
            "vecs_in", "rows_in", "x_in", "mod_mm", "mod_added", "mod_out", "hT_out", "act_chain", "dve_chain",
            "c_ready", "ssq_ready", "rms_ready", "rows_ready", "cols_mm", "xn_ready", "xn_turned", "hT_ready")
        wmod_in = a.ring("wmod_in", RING)
        w_in, done, out = a.ring("w_in", 2), a.ring("in_done", 2), a.ring("in_out", 2)
        w_mod = m.w_mod[0].rearrange("(p k) n -> p k n", k=KD)
        with nc.Block() as block:

            @block.sync
            def _(sp):
                def chunk(n):
                    sp.dma_start(wmod[:, n % RING], w_mod[:, :, n * 512:(n + 1) * 512]
                                 ).then_inc(wmod_in[n % RING], 16)

                def tile(i, b):
                    sp.dma_start(w[:, b, :], m.w_mix[bass.ds(i * 2 + b, 1)].rearrange("a p n -> (a p) n")
                                 ).then_inc(w_in[b], 16)

                sp.dma_start(c_raw[:], m.cond).then_inc(vecs_in, 16)
                chunk(0)
                chunk(1)
                sp.dma_start(x[:, 0:CTX, :], m.x_sample[0].rearrange("(t p) d -> p t d", p=P)).then_inc(x_in, 16)
                sp.dma_start(x[:, CTX, :], m.x_prompt[0]).then_inc(x_in, 16)
                sp.dma_start(flat(rows[:]), m.b_mod.to_broadcast([2, 6 * D])).then_inc(rows_in, 16)
                sp.dma_start(g_row[:, 0, :], m.g_norm_mix.to_broadcast([2, D])).then_inc(rows_in, 16)
                sp.dma_start(g_row[:, 1, :], m.g_norm_ffn.to_broadcast([2, D])).then_inc(rows_in, 16)
                sp.dma_start(m.const[:], m.constants).then_inc(rows_in, 16)
                sp.dma_start(m.vec[:], m.vectors).then_inc(rows_in, 16)
                chunk(2)
                chunk(3)
                for n in range(RING, N_COL):
                    sp.wait_ge(mod_mm, n - RING + 1)
                    chunk(n)
                    if n == N_COL - 2:
                        for b in range(2):
                            tile(0, b)
                sp.wait_ge(hT_ready, NT)
                sp.dma_start(m.hT_dram, hT[:]).then_inc(hT_out, 16)
                sp.wait_ge(rows_ready, 2)
                sp.dma_start(m.mod_dram, rows[:]).then_inc(mod_out, 16)
                with sp.Fori(1, N_MIX // 2) as i:
                    for b in range(2):
                        sp.wait_ge(done[b], i)
                        tile(i, b)
                sp.wait_ge(mod_out, 16)
                sp.wait_ge(hT_out, 16)

            @block.scalar
            def _(act):
                ch = Chain(act, act_chain)
                act.wait_ge(vecs_in, 16)
                act.activation(c_act[:], c_raw[:], ACT.Sigmoid).then_inc(c_ready, 1)
                act.wait_ge(x_in, 32)
                for t in range(NT):
                    ch.link(act.activation(square, x[:, t, :], ACT.Square, accum_out=mean_sq[:, t:t + 1]))
                act.activation(square[:, 0:1], mean_sq[:, 0:1], ACT.Copy).then_inc(ssq_ready, 1)
                act.wait_ge(ssq_ready, 2)
                act.activation(rms[:], mean_sq[:], ACT.Sqrt).then_inc(rms_ready, 1)
                with act.Fori(0, N_MIX // 2) as i:
                    for b in range(2):
                        act.wait_ge(done[b], i + 1)
                        act.activation(m.proj[:, bass.ds(i * 2 + b, 1), :].rearrange("p a t -> p (a t)"),
                                       ps[:, b, 0:T], ACT.Copy).then_inc(out[b], 1)

            @block.vector
            def _(dve):
                ch = Chain(dve, dve_chain)
                flat_rows = flat(rows[:])

                def add(n):
                    dve.wait_ge(mod_mm, n + 1)
                    cut = flat_rows[:, n * 512:(n + 1) * 512]
                    dve.tensor_add(cut, ps_mod[:, n % 2, :], cut).then_inc(mod_added, 1)

                def scaled(r, g):
                    ch.link(dve.tensor_scalar(rows[:, r, :], rows[:, r, :], 1.0, None, ALU.add))
                    dve.tensor_mul(rows[:, r, :], rows[:, r, :], g_row[:, g, :]).then_inc(rows_ready, 1)

                dve.wait_ge(c_ready, 1)
                dve.tensor_mul(c_act[:], c_act[:], c_raw[:]).then_inc(c_ready, 1)
                dve.wait_ge(rows_in, 80)
                dve.wait_ge(ssq_ready, 1)
                dve.tensor_scalar(mean_sq[:], mean_sq[:], 1.0 / D, EPS, ALU.mult, ALU.add).then_inc(ssq_ready, 1)
                dve.wait_ge(rms_ready, 1)
                ch.link(dve.reciprocal(rstd[:], rms[:]))
                for n in range(N_FIRST):
                    add(n)
                dve.wait_ge(mod_added, N_FIRST)
                scaled(1, 0)
                dve.wait_ge(cols_mm, 1)
                ch.link(dve.tensor_copy(mod_c[:].rearrange("p v k g -> p (v k g)"), ps_cols[:]))
                for t in range(NT + 1):
                    if t < NT:
                        if t >= 2:
                            dve.wait_ge(xn_turned, t - 1)
                        dve.tensor_scalar(xn[:, t % 2, :], x[:, t, :], rstd[:, t:t + 1], None, ALU.mult
                                          ).then_inc(xn_ready, 1)
                    if t >= 1:
                        u, g = t - 1, 0 if t - 1 == CTX else 1
                        dve.wait_ge(xn_turned, u + 1)
                        to = hT[:, :, u * P:(u + 1) * P]
                        ch.link(dve.tensor_mul(to, ps[:, u % 2, :].rearrange("p (k t) -> p k t", k=KD),
                                               mod_c[:, 1, :, g:g + 1].to_broadcast([P, KD, P])))
                        dve.tensor_add(to, to, mod_c[:, 0, :, g:g + 1].to_broadcast([P, KD, P])
                                       ).then_inc(hT_ready, 1)
                        add(N_FIRST + u)
                for n in range(N_FIRST + NT, N_COL):
                    add(n)
                dve.wait_ge(mod_added, N_COL)
                scaled(4, 1)

            @block.tensor
            def _(pe):
                def modulation(n):
                    pe.wait_ge(wmod_in[n % RING], 16 * (n // RING + 1))
                    if n >= 2:
                        pe.wait_ge(mod_added, n - 1)
                    for k in range(KD):
                        mm = pe.matmul(ps_mod[:, n % 2, :], c_act[:, k, :], wmod[:, n % RING, k, :],
                                       start=(k == 0), stop=(k == KD - 1))
                    mm.then_inc(mod_mm, 1)

                pe.wait_ge(c_ready, 2)
                for n in range(N_FIRST):
                    modulation(n)
                pe.wait_ge(rows_ready, 1)
                for v in range(2):
                    for k in range(KD):
                        mm = pe.matmul(ps_cols[:, (v * KD + k) * 2:(v * KD + k) * 2 + 2], rows[:, v, k::KD],
                                       m.const[0:2, 0:2], start=True, stop=True)
                mm.then_inc(cols_mm, 1)
                for t in range(NT):
                    pe.wait_ge(xn_ready, t + 1)
                    if t >= 2:
                        pe.wait_ge(hT_ready, t - 1)
                    for k in range(KD):
                        mm = pe.transpose(ps[:, t % 2, k * P:(k + 1) * P], xn[:, t % 2, k::KD], m.const[:, 0:P])
                    mm.then_inc(xn_turned, 1)
                    modulation(N_FIRST + t)
                for n in range(N_FIRST + NT, N_COL):
                    modulation(n)
                pe.wait_ge(hT_ready, NT)

                def lap(i):
                    for b in range(2):
                        pe.wait_ge(w_in[b], 16 * i + 16)
                        pe.wait_ge(out[b], i)
                        for k in range(KD):
                            for lo, hi in ((0, 512), (512, T)):
                                mm = pe.matmul(ps[:, b, lo:hi], w[:, b, k * P:(k + 1) * P], hT[:, k, lo:hi],
                                               start=(k == 0), stop=(k == KD - 1))
                        mm.then_inc(done[b], 1)

                lap(0)
                with pe.Fori(1, N_MIX // 2) as i:
                    lap(i)


def fourier_and_conv(nc, m):
    with Tools(nc, "fourier_and_conv") as a:
        ch_dft = a.sb("ch_dft", [P, 2 * P])
        lat_dft = a.sb("lat_dft", [P, CTX, 2, T_LAT])
        ctx_dft = a.sb("ctx_dft", [P, 2, T_CTX])
        mixed = a.sb("ch_mixed", [P, NT, 2, 2 * P])
        z = a.sb("conv_z", [P, 2, T])
        y = a.sb("conv_y", [P, 2, T])
        ps_ch = a.ps("ps_ch", [P, 2, 512])
        ps_lat = a.ps("ps_lat", [P, 2, 512])
        ps_ctx = a.ps("ps_ctx", [P, 512])
        tables_in, ch_mm, ch_out, tok_mm, conv = a.sems("tables_in", "ch_mm", "ch_out", "tok_mm", "conv")
        with nc.Block() as block:

            @block.sync
            def _(sp):
                sp.dma_start(ch_dft[:], m.dft_channel).then_inc(tables_in, 16)
                sp.dma_start(lat_dft[:], m.dft_lat).then_inc(tables_in, 16)
                sp.dma_start(ctx_dft[:], m.dft_ctx).then_inc(tables_in, 16)

            @block.tensor
            def _(pe):
                pe.wait_ge(tables_in, 48)
                for n in range(2 * NT):
                    t, c = n // 2, n % 2
                    if n >= 2:
                        pe.wait_ge(ch_out, n - 1)
                    pe.matmul(ps_ch[:, n % 2, 0:2 * P], m.proj[:, U_ + c, t * P:(t + 1) * P], ch_dft[:],
                              start=True, stop=True).then_inc(ch_mm, 1)
                pe.wait_ge(ch_out, 2 * NT)
                for c in range(2):
                    for t in range(CTX):
                        for part in range(2):
                            mm = pe.matmul(ps_lat[:, c, :], mixed[:, t, c, part * P:(part + 1) * P],
                                           lat_dft[:, t, part, :], start=(t + part == 0),
                                           stop=(t == CTX - 1 and part == 1))
                    mm.then_inc(tok_mm, 1)
                for c in range(2):
                    for part in range(2):
                        mm = pe.matmul(ps_ctx[:, c * P:(c + 1) * P], mixed[:, CTX, c, part * P:(part + 1) * P],
                                       ctx_dft[:, part, :], start=(part == 0), stop=(part == 1))
                mm.then_inc(tok_mm, 1)

            @block.scalar
            def _(act):
                for n in range(2 * NT):
                    act.wait_ge(ch_mm, n + 1)
                    act.activation(mixed[:, n // 2, n % 2, :], ps_ch[:, n % 2, 0:2 * P], ACT.Copy).then_inc(ch_out, 1)
                for c in range(2):
                    act.wait_ge(tok_mm, c + 1)
                    act.activation(m.branch[:, c, 0:T_LAT], ps_lat[:, c, :], ACT.Copy)
                act.wait_ge(tok_mm, 3)
                act.activation(m.branch[:, 0:2, T_LAT:T], ps_ctx[:, 0:2 * P].rearrange("p (c t) -> p c t", c=2),
                               ACT.Copy)

            @block.vector
            def _(dve):
                ch = Chain(dve, conv)
                ch.link(dve.tensor_mul(z[:], m.proj[:, SC_:SC_ + 2, :], m.proj[:, SX:SX + 2, :]))
                w = lambda tap, c: m.vec[:, CONV + 2 * tap + c:CONV + 2 * tap + c + 1]
                for c in range(2):
                    ch.link(dve.tensor_scalar(y[:, c, :], z[:, c, :], w(1, c), None, ALU.mult))
                for lo, hi in ((0, T_LAT), (T_LAT, T)):
                    for c in range(2):
                        ch.link(dve.scalar_tensor_tensor(
                            out=y[:, c, lo + 1:hi], in0=z[:, c, lo:hi - 1], scalar=w(0, c),
                            in1=y[:, c, lo + 1:hi], op0=ALU.mult, op1=ALU.add))
                        ch.link(dve.scalar_tensor_tensor(
                            out=y[:, c, lo:hi - 1], in0=z[:, c, lo + 1:hi], scalar=w(2, c),
                            in1=y[:, c, lo:hi - 1], op0=ALU.mult, op1=ALU.add))
                dve.tensor_mul(m.branch[:, 6:8, :], y[:], m.proj[:, SB_:SB_ + 2, :])


def head_sum(pe, m, ps, src):
    for c in range(2):
        for lo, hi in ((0, 512), (512, T)):
            mm = pe.matmul(ps[:, c, lo:hi], m.const[:, HEADS * P:(HEADS + 1) * P], src[:, c, lo:hi],
                           start=True, stop=True)
    return mm


def rwkv_prepare(nc, m, r):
    C0 = -float(np.exp(-0.5))
    with Tools(nc, "rwkv_prepare") as a:
        lora = a.sb("lora_w", [P, BW])
        g_up = a.sb("g_up_w", [64, BW])
        keep = a.sb("keep", [P, T])
        kk, rec, sg, ag, L, b, ce, ci = (a.sb(n, [P, 2, T]) for n in ("kk", "rec", "sg", "ag", "L", "b", "ce", "ci"))
        bonus = a.sb("bonus", [P, 2, T])
        half = a.sb("half_tot", [P, 2, NT])
        zw = a.ps("ps_zw", [P, 2, 1024])
        za = a.ps("ps_za", [P, 2, 1024])
        (w_in, keep_set, squashed, sq, sq_mm, nrm, nrm_mul, zw_mm, za_mm, sg_ok, ag_ok, cum, kd_ok, exps, prods,
         bon, bon_mm, g_mm, act_chain, dve_chain) = a.sems(
            "w_in", "keep_set", "squashed", "sq", "sq_mm", "nrm", "nrm_mul", "zw_mm", "za_mm", "sg_ok", "ag_ok",
            "cum", "kd_ok", "exps", "prods", "bon", "bon_mm", "g_mm", "act_chain", "dve_chain")
        tiles = lambda ap: ap.rearrange("p c (t i) -> p c t i", i=P)
        pr = m.proj
        with nc.Block() as block:

            @block.sync
            def _(sp):
                sp.dma_start(lora[:], m.lora).then_inc(w_in, 16)
                sp.dma_start(g_up[:], m.rw_g_up[0]).then_inc(w_in, 16)

            @block.gpsimd
            def _(pool):
                pool.memset(keep[:], 1.0).then_inc(keep_set, 1)
                pool.wait_ge(keep_set, 1)
                pool.memset(keep[:, ::P], 0.0).then_inc(keep_set, 1)

            @block.scalar
            def _(act):
                ch = Chain(act, act_chain)
                act.activation(pr[0:64, WA, :], pr[0:64, WA, :], ACT.Tanh)
                act.activation(pr[0:64, GDGA, :], pr[0:64, GDGA, :], ACT.Sigmoid).then_inc(squashed, 1)
                act.wait_ge(sq_mm, 1)
                act.activation(rec[:], zw[:, :, 0:T], ACT.Sqrt).then_inc(nrm, 1)
                for d in range(2):
                    act.wait_ge(zw_mm, d + 1)
                    for c in range(2):
                        s = act.activation(sg[:, c, :], zw[:, c, 0:T], ACT.Sigmoid,
                                           bias=m.vec[:, W0 + 2 * d + c:W0 + 2 * d + c + 1])
                    s.then_inc(sg_ok, 1)
                    act.wait_ge(za_mm, d + 1)
                    for c in range(2):
                        s = act.activation(ag[:, c, :], za[:, c, 0:T], ACT.Sigmoid,
                                           bias=m.vec[:, A0 + 2 * d + c:A0 + 2 * d + c + 1])
                    s.then_inc(ag_ok, 1)
                    act.wait_ge(cum, d + 1)
                    act.activation(r.mid[d][:], half[:], ACT.Exp)
                    act.activation(L[:], ci[:], ACT.Exp, scale=-1.0)
                    act.activation(b[:], ce[:], ACT.Exp)
                    act.wait_ge(kd_ok, d + 1)
                    act.activation(ag[:], ci[:], ACT.Exp).then_inc(exps, 1)
                    act.wait_ge(prods, d + 1)
                act.wait_ge(g_mm, 1)
                act.wait_ge(prods, 2)
                act.activation(pr[:, K_:K_ + 2, :], za[:, :, 0:T], ACT.Copy)

            @block.vector
            def _(dve):
                ch = Chain(dve, dve_chain)
                dve.wait_ge(keep_set, 2)
                for c in range(2):
                    ch.link(dve.tensor_scalar(kk[:, c, :], pr[:, K_ + c, :], m.vec[:, KK + c:KK + c + 1], None,
                                              ALU.mult))
                dve.tensor_mul(b[:], kk[:], kk[:]).then_inc(sq, 1)
                dve.wait_ge(nrm, 1)
                ch.link(dve.tensor_scalar(rec[:], rec[:], 1e-12, None, ALU.max))
                ch.link(dve.reciprocal(rec[:], rec[:]))
                ch.link(dve.tensor_mul(kk[:], kk[:], rec[:]))
                for d in range(2):
                    dve.wait_ge(sg_ok, d + 1)
                    ch.link(dve.tensor_scalar(L[:], sg[:], C0, None, ALU.mult))
                    for c in range(2):
                        ch.link(dve.tensor_tensor_scan(b[:, c, :], keep[:], L[:, c, :], 0.0, ALU.mult, ALU.add))
                    ch.link(dve.tensor_scalar(half[:], tiles(b[:])[:, :, :, P - 1], 0.5, None, ALU.mult))
                    for c in range(2):
                        mid = half[:, c, :].unsqueeze(2).to_broadcast([P, NT, P])
                        bt = b[:, c, :].rearrange("p (t i) -> p t i", i=P)
                        if d == 0:
                            ch.link(dve.tensor_sub(ci[:, c, :].rearrange("p (t i) -> p t i", i=P), bt, mid))
                        else:
                            ch.link(dve.tensor_sub(ce[:, c, :].rearrange("p (t i) -> p t i", i=P), mid, bt))
                    if d == 0:
                        dve.tensor_sub(ce[:], ci[:], L[:]).then_inc(cum, 1)
                    else:
                        dve.tensor_add(ci[:], ce[:], L[:]).then_inc(cum, 1)
                    dve.wait_ge(ag_ok, d + 1)
                    ch.link(dve.tensor_mul(rec[:], kk[:], ag[:]))
                    for c in range(2):
                        ch.link(dve.tensor_scalar(sg[:, c, :], ag[:, c, :], 1.0, m.vec[:, KA + c:KA + c + 1],
                                                  ALU.subtract, ALU.mult))
                    ch.link(dve.scalar_tensor_tensor(out=sg[:], in0=sg[:], scalar=1.0, in1=pr[:, K_:K_ + 2, :],
                                                     op0=ALU.add, op1=ALU.mult))
                    if d == 0:
                        dve.tensor_copy(bonus[:], sg[:]).then_inc(kd_ok, 1)
                    else:
                        dve.tensor_add(bonus[:], bonus[:], sg[:]).then_inc(kd_ok, 1)
                    dve.wait_ge(exps, d + 1)
                    dve.tensor_mul(r.rt[d][:], pr[:, R_:R_ + 2, :], ag[:])
                    dve.tensor_mul(r.kt[d][:], sg[:], L[:])
                    dve.tensor_mul(r.bt[d][:], rec[:], L[:])
                    ch.link(dve.scalar_tensor_tensor(out=r.at[d][:], in0=kk[:], scalar=-1.0, in1=b[:],
                                                     op0=ALU.mult, op1=ALU.mult))
                    dve.tensor_copy(half[:, 0, 0:1], half[:, 0, 0:1]).then_inc(prods, 1)
                ch.link(dve.tensor_mul(bonus[:], bonus[:], pr[:, R_:R_ + 2, :]))
                for c in range(2):
                    s = dve.tensor_scalar(bonus[:, c, :], bonus[:, c, :], m.vec[:, RK + c:RK + c + 1], None, ALU.mult)
                s.then_inc(bon, 1)
                dve.wait_ge(bon_mm, 1)
                dve.tensor_mul(pr[:, R_:R_ + 2, :], zw[:, :, 0:T], pr[:, V_:V_ + 2, :])

            @block.tensor
            def _(pe):
                pe.wait_ge(sq, 1)
                head_sum(pe, m, zw, b).then_inc(sq_mm, 1)
                pe.wait_ge(w_in, 32)
                pe.wait_ge(squashed, 1)
                pe.wait_ge(nrm, 1)
                for d in range(2):
                    for ps, first, done, free in ((zw, 0, zw_mm, sg_ok), (za, 64, za_mm, ag_ok)):
                        pe.wait_ge(free, d)
                        at = first + 32 * d
                        for c in range(2):
                            for lo, hi in ((0, 512), (512, T)):
                                mm = pe.matmul(ps[:, c, lo:hi], lora[at:at + 32, c * P:(c + 1) * P],
                                               pr[at:at + 32, WA, lo:hi], start=True, stop=True)
                        mm.then_inc(done, 1)
                pe.wait_ge(ag_ok, 2)
                for c in range(2):
                    for lo, hi in ((0, 512), (512, T)):
                        mm = pe.matmul(za[:, c, lo:hi], g_up[:, c * P:(c + 1) * P], pr[0:64, GDGA, lo:hi],
                                       start=True, stop=True)
                mm.then_inc(g_mm, 1)
                pe.wait_ge(bon, 1)
                head_sum(pe, m, zw, bonus).then_inc(bon_mm, 1)


def turn_to_tokens(nc, m, items, name):
    with Tools(nc, f"turn_{name}") as a:
        ps = a.ps("ps_turn", [P, 8, 512])
        turned, out = a.sems(f"{name}_turned", f"{name}_out")
        with nc.Block() as block:

            @block.tensor
            def _(pe):
                for n, (_, src) in enumerate(items):
                    if n >= 8:
                        pe.wait_ge(out, n - 7)
                    pe.transpose(ps[:, n % 8, 0:P], src, m.const[:, 0:P]).then_inc(turned, 1)

            @block.scalar
            def _(act):
                for n, (dst, _) in enumerate(items):
                    act.wait_ge(turned, n + 1)
                    for k, (to, lo, hi) in enumerate(dst):
                        s = act.activation(to, ps[:, n % 8, lo:hi], ACT.Copy)
                    s.then_inc(out, 1)


def rwkv_scan(nc, m, r):
    NL = len(LEVELS) - 1
    H = 4
    tile_of = ((CTX, 0, 1, 2, 3), (CTX, 3, 2, 1, 0))
    cs = lambda n: m.const[:, n * P:(n + 1) * P]
    lev, strict, causal = (LEV_F, LEV_B), (LT, GT), (LE, GE)
    with Tools(nc, "rwkv_scan") as a:
        two = lambda n, shape: [a.sb(f"{n}_{d}", shape) for d in range(2)]
        X, XT, NTm, OFF, Y, MT, QB, QK, Upad = (two(n, [P, H, P]) for n in (
            "X", "XT", "NTm", "OFF", "Y", "MT", "QB", "QK", "Upad"))
        Rsb, Usb = two("Rsb", [P, BW]), two("Usb", [P, BW])
        S, Sc, S0, Snat = two("S", [P, 2, P]), two("Sc", [P, 2, P]), two("S0", [P, 2, P]), two("Snat", [P, 2, P])
        ps = [a.ps(f"ps_scan{d}", [P, 4, 512]) for d in range(2)]
        sem2 = lambda n: [a.sem(f"{n}_{d}") for d in range(2)]
        (sc_mm, m_mm, q_mm, Y_mm, dX_mm, R_mm, U_mm, S_mm, y_mm, x_set, m_set, q_set, X_upd, u_set, sc_set,
         Y_out, R_out, u_out, y_out, eye, off, S0_mm, S0_out, fin_mm, fin_out) = (sem2(n) for n in (
            "sc_mm", "m_mm", "q_mm", "Y_mm", "dX_mm", "R_mm", "U_mm", "S_mm", "y_mm", "x_set", "m_set", "q_set",
            "X_upd", "u_set", "sc_set", "Y_out", "R_out", "u_out", "y_out", "eye", "off", "S0_mm", "S0_out",
            "fin_mm", "fin_out"))
        zeroed, states_in, states_out, dve_chain = a.sems("zeroed", "states_in", "states_out", "dve_chain")
        split = lambda ap: ap.rearrange("p (hh par) t -> p par hh t", par=2)
        bank2 = lambda d, first, half: ps[d][:, first:first + 2, half * 256:half * 256 + 256].rearrange(
            "p b (hh t) -> p b hh t", hh=2)
        full = lambda d, b: ps[d][:, b, :].rearrange("p (h t) -> p h t", h=H)
        pair = lambda d, b, half=0: ps[d][:, b, half * 256:half * 256 + 256].rearrange("p (c v) -> p c v", c=2)
        many = lambda mask: mask.bitcast(U32).unsqueeze(1).unsqueeze(1).to_broadcast([P, 2, 2, P])
        with nc.Block() as block:

            @block.sync
            def _(sp):
                sp.wait_ge(zeroed, 1)
                for d in range(2):
                    for par in range(2):
                        sp.dma_start(Snat[d][64 * par:64 * par + 64, :, 64 * par:64 * par + 64],
                                     m.state_rwkv[0, 0, d, par::2].rearrange("h v k -> v h k")
                                     ).then_inc(states_in, 16)
                for d in range(2):
                    sp.wait_ge(fin_out[d], 1)
                    for par in range(2):
                        sp.dma_start(m.new_rwkv[0, 0, d, par::2].rearrange("h v k -> v h k"),
                                     Snat[d][64 * par:64 * par + 64, :, 64 * par:64 * par + 64]
                                     ).then_inc(states_out, 16)
                sp.wait_ge(states_out, 64)

            @block.gpsimd
            def _(pool):
                for d in range(2):
                    for t in (Snat, NTm, MT, QB, QK, Upad, Sc):
                        z = pool.memset(t[d][:], 0.0)
                z.then_inc(zeroed, 1)
                for s in range(NT):
                    for d in range(2):
                        pool.wait_ge(U_mm[d], s)
                        for t in (X, XT):
                            z = pool.tensor_copy(t[d][:], cs(IDENT).unsqueeze(1).to_broadcast([P, H, P]))
                        z.then_inc(eye[d], 1)
                    for li in range(1, NL + 1):
                        for d in range(2):
                            pool.wait_ge(x_set[d], s + 1)
                            pool.wait_ge(Y_mm[d], NL * s + li - 1)
                            pool.tensor_mul(OFF[d][:], NTm[d][:],
                                            cs(lev[d] + li).unsqueeze(1).to_broadcast([P, H, P])
                                            ).then_inc(off[d], 1)

            @block.tensor
            def _(pe):
                def head(d, arr, h, t):
                    lo = 64 * (h % 2)
                    return arr[d][lo:lo + 64, h // 2, t * P:(t + 1) * P]

                def scores(d, bank, half, lhs, rhs, t):
                    for h in range(H):
                        at = half * 256 + (h // 2) * P
                        mm = pe.matmul(ps[d][:, bank + h % 2, at:at + P], head(d, lhs, h, t), head(d, rhs, h, t),
                                       start=True, stop=True)
                    return mm

                pe.wait_ge(states_in, 64)
                for d in range(2):
                    for c in range(2):
                        mm = pe.transpose(ps[d][:, 3, c * P:(c + 1) * P], Snat[d][:, c, :], cs(IDENT))
                    mm.then_inc(S0_mm[d], 1)
                for s in range(NT):
                    for d in range(2):
                        t = tile_of[d][s]
                        pe.wait_ge(sc_set[d], s + 1)
                        pe.wait_ge(y_out[d], s)
                        scores(d, 0, 0, r.at, r.bt, t)
                        scores(d, 0, 1, r.bt, r.at, t).then_inc(sc_mm[d], 1)
                        pe.wait_ge(X_upd[d], NL * s)
                        pe.wait_ge(S0_out[d], 1)
                        pe.wait_ge(u_out[d], s)
                        pe.wait_ge(u_set[d], s)
                        scores(d, 2, 0, r.kt, r.at, t)
                        scores(d, 2, 1, r.bt, r.rt, t).then_inc(m_mm[d], 1)
                    for d in range(2):
                        pe.wait_ge(x_set[d], s + 1)
                        scores(d, 0, 0, r.kt, r.rt, tile_of[d][s]).then_inc(q_mm[d], 1)
                    for li in range(1, NL + 1):
                        n = NL * s + li
                        for d in range(2):
                            pe.wait_ge(off[d], n)
                            if li == 1:
                                pe.wait_ge(q_set[d], s + 1)
                            else:
                                pe.wait_ge(X_upd[d], n - 1)
                            for h in range(H):
                                mm = pe.matmul(full(d, 0)[:, h, :], OFF[d][:, h, :], X[d][:, h, :],
                                               start=True, stop=True)
                            mm.then_inc(Y_mm[d], 1)
                        for d in range(2):
                            pe.wait_ge(Y_out[d], n)
                            if li == 1:
                                pe.wait_ge(m_set[d], s + 1)
                            if li < NL:
                                for h in range(H):
                                    pe.matmul(full(d, 1)[:, h, :], XT[d][:, h, :], Y[d][:, h, :],
                                              start=True, stop=True)
                            for h in range(H):
                                mm = pe.matmul(full(d, 2)[:, h, :], Y[d][:, h, :], XT[d][:, h, :],
                                               start=True, stop=True)
                            mm.then_inc(dX_mm[d], 1)
                    for d in range(2):
                        t = tile_of[d][s]
                        for c in range(2):
                            for h in (2 * c, 2 * c + 1):
                                pe.matmul(ps[d][:, 3, 64 * h:64 * h + 64], MT[d][:, h, :],
                                          r.vtok[:, t, 64 * h:64 * h + 64], start=(h % 2 == 0), stop=False)
                            mm = pe.matmul(pair(d, 3)[:, c, :], r.at[d][:, c, t * P:(t + 1) * P], Sc[d][:, c, :],
                                           start=False, stop=True)
                        mm.then_inc(R_mm[d], 1)
                    for d in range(2):
                        pe.wait_ge(R_out[d], s + 1)
                        pe.wait_ge(X_upd[d], NL * s + NL)
                        for h in range(H):
                            mm = pe.matmul(ps[d][:, 3, 256 + 64 * h:320 + 64 * h], XT[d][:, h, :],
                                           Rsb[d][:, 64 * h:64 * h + 64], start=True, stop=True)
                        mm.then_inc(U_mm[d], 1)
                    for d in range(2):
                        t = tile_of[d][s]
                        pe.wait_ge(u_out[d], s + 1)
                        for c in range(2):
                            cols = slice(c * P, (c + 1) * P)
                            pe.matmul(pair(d, 0)[:, c, :], r.btok[d][:, t, cols], Usb[d][:, cols],
                                      start=True, stop=False)
                            mm = pe.matmul(pair(d, 0)[:, c, :], r.ktok[d][:, t, cols], r.vtok[:, t, cols],
                                           start=False, stop=True)
                        mm.then_inc(S_mm[d], 1)
                        pe.wait_ge(u_set[d], s + 1)
                        for c in range(2):
                            out = pair(d, 1)[:, c, :]
                            pe.matmul(out, Sc[d][:, c, :], r.rt[d][:, c, t * P:(t + 1) * P], start=True, stop=False)
                            for h in (2 * c, 2 * c + 1):
                                pe.matmul(out, r.vpad[:, t, h, :], QK[d][:, h, :], start=False, stop=False)
                                mm = pe.matmul(out, Upad[d][:, h, :], QB[d][:, h, :], start=False,
                                               stop=(h % 2 == 1))
                        mm.then_inc(y_mm[d], 1)
                for d in range(2):
                    for c in range(2):
                        mm = pe.transpose(ps[d][:, 3, c * P:(c + 1) * P], S[d][:, c, :], cs(IDENT))
                    mm.then_inc(fin_mm[d], 1)

            @block.scalar
            def _(act):
                for d in range(2):
                    act.wait_ge(S0_mm[d], 1)
                    act.activation(S0[d][:], pair(d, 3), ACT.Copy).then_inc(S0_out[d], 1)
                for s in range(NT):
                    for li in range(1, NL + 1):
                        for d in range(2):
                            act.wait_ge(Y_mm[d], NL * s + li)
                            act.wait_ge(dX_mm[d], NL * s + li - 1)
                            act.activation(Y[d][:], full(d, 0), ACT.Copy).then_inc(Y_out[d], 1)
                    for d in range(2):
                        act.wait_ge(R_mm[d], s + 1)
                        act.activation(Rsb[d][:], ps[d][:, 3, 0:BW], ACT.Copy).then_inc(R_out[d], 1)
                    for d in range(2):
                        act.wait_ge(U_mm[d], s + 1)
                        act.wait_ge(u_set[d], s)
                        act.activation(Usb[d][:], ps[d][:, 3, BW:2 * BW], ACT.Copy).then_inc(u_out[d], 1)
                    for d in range(2):
                        t = tile_of[d][s]
                        act.wait_ge(y_mm[d], s + 1)
                        act.activation(r.y[d][:, :, t * P:(t + 1) * P], pair(d, 1), ACT.Copy).then_inc(y_out[d], 1)
                for d in range(2):
                    act.wait_ge(fin_mm[d], 1)
                    act.activation(Snat[d][:], pair(d, 3), ACT.Copy).then_inc(fin_out[d], 1)

            @block.vector
            def _(dve):
                ch = Chain(dve, dve_chain)
                dve.wait_ge(zeroed, 1)
                for d in range(2):
                    dve.tensor_copy(S[d][:, 0, 0:1], cs(ONES)[:, 0:1]).then_inc(sc_set[d], 1)
                for s in range(NT):
                    for d in range(2):
                        dve.wait_ge(sc_mm[d], s + 1)
                        dve.wait_ge(eye[d], s + 1)
                        dve.wait_ge(off[d], NL * s)
                        dve.copy_predicated(split(X[d][:]), many(cs(lev[1 - d])), bank2(d, 0, 0))
                        dve.copy_predicated(split(XT[d][:]), many(cs(lev[d])), bank2(d, 0, 1))
                        dve.copy_predicated(split(NTm[d][:]), many(cs(strict[d])), bank2(d, 0, 1)
                                            ).then_inc(x_set[d], 1)
                        dve.wait_ge(m_mm[d], s + 1)
                        dve.wait_ge(y_mm[d], s)
                        dve.copy_predicated(split(MT[d][:]), many(cs(strict[d])), bank2(d, 2, 0))
                        dve.copy_predicated(split(QB[d][:]), many(cs(causal[d])), bank2(d, 2, 1)
                                            ).then_inc(m_set[d], 1)
                    for d in range(2):
                        dve.wait_ge(q_mm[d], s + 1)
                        dve.copy_predicated(split(QK[d][:]), many(cs(causal[d])), bank2(d, 0, 0)
                                            ).then_inc(q_set[d], 1)
                    for li in range(1, NL + 1):
                        for d in range(2):
                            dve.wait_ge(dX_mm[d], NL * s + li)
                            if li < NL:
                                dve.tensor_add(X[d][:], full(d, 1), X[d][:])
                            dve.tensor_add(XT[d][:], full(d, 2), XT[d][:]).then_inc(X_upd[d], 1)
                    for d in range(2):
                        dve.wait_ge(u_out[d], s + 1)
                        for par in range(2):
                            u = dve.tensor_copy(
                                Upad[d][:, par::2, 64 * par:64 * par + 64],
                                Usb[d][:].rearrange("p (hh par v) -> p par hh v", hh=2, par=2)[:, par])
                        u.then_inc(u_set[d], 1)
                    for d in range(2):
                        dve.wait_ge(S_mm[d], s + 1)
                        dve.wait_ge(y_mm[d], s + 1)
                        t = tile_of[d][s]
                        wide = lambda t: r.mid[d][:, :, t:t + 1].to_broadcast([P, 2, P])
                        ch.link(dve.tensor_mul(S0[d][:] if s else S[d][:], pair(d, 0),
                                               cs(HEADS).unsqueeze(1).to_broadcast([P, 2, P])))
                        if s == 0:
                            ch.link(dve.tensor_mul(S[d][:], S[d][:], wide(t)))
                            dve.wait_ge(S0_out[d], 1)
                            dve.tensor_mul(Sc[d][:], S0[d][:], wide(tile_of[d][1])).then_inc(sc_set[d], 1)
                        elif s < NT - 1:
                            ch.link(dve.tensor_add(Sc[d][:], Sc[d][:], S0[d][:]))
                            ch.link(dve.tensor_mul(Sc[d][:], Sc[d][:], wide(t)))
                            dve.tensor_mul(Sc[d][:], Sc[d][:], wide(tile_of[d][s + 1])).then_inc(sc_set[d], 1)


def rwkv_finish(nc, m, r):
    with Tools(nc, "rwkv_finish") as a:
        y, y2 = a.sb("y_sum", [P, 2, T]), a.sb("y_sq", [P, 2, T])
        ps = a.ps("ps_mean", [P, 2, 1024])
        ready, mm_s, rms, chain = a.sems("fin_ready", "fin_sum", "fin_rms", "fin_chain")
        with nc.Block() as block:

            @block.tensor
            def _(pe):
                pe.wait_ge(ready, 1)
                head_sum(pe, m, ps, y).then_inc(mm_s, 1)
                pe.wait_ge(ready, 2)
                head_sum(pe, m, ps, y2).then_inc(mm_s, 1)

            @block.scalar
            def _(act):
                act.wait_ge(ready, 3)
                act.activation(y2[:], y2[:], ACT.Sqrt).then_inc(rms, 1)

            @block.vector
            def _(dve):
                ch = Chain(dve, chain)
                dve.tensor_add(y[:], r.y[0][:], r.y[1][:]).then_inc(ready, 1)
                dve.wait_ge(mm_s, 1)
                dve.wait_ge(ready, 1)
                ch.link(dve.scalar_tensor_tensor(out=y[:], in0=ps[:, :, 0:T], scalar=-1.0 / 64, in1=y[:],
                                                 op0=ALU.mult, op1=ALU.add))
                dve.tensor_mul(y2[:], y[:], y[:]).then_inc(ready, 1)
                dve.wait_ge(mm_s, 2)
                dve.tensor_scalar(y2[:], ps[:, :, 0:T], 1.0 / 64, 64e-5, ALU.mult, ALU.add).then_inc(ready, 1)
                dve.wait_ge(rms, 1)
                ch.link(dve.reciprocal(y2[:], y2[:]))
                ch.link(dve.tensor_mul(y[:], y[:], y2[:]))
                for c in range(2):
                    ch.link(dve.tensor_scalar(y[:, c, :], y[:, c, :], m.vec[:, LNW + c:LNW + c + 1],
                                              m.vec[:, LNB + c:LNB + c + 1], ALU.mult, ALU.add))
                ch.link(dve.tensor_add(y[:], y[:], m.proj[:, R_:R_ + 2, :]))
                dve.tensor_mul(m.branch[:, 2:4, :], y[:], m.proj[:, K_:K_ + 2, :])


def rwkv(nc, m):
    spare = lambda lo, n: m.proj[:, lo:lo + n, :].rearrange("p a t -> p (a t)")
    with Tools(nc, "rwkv") as a:
        two = lambda n, shape: [a.sb(f"{n}{d}", shape) for d in range(2)]
        r = Stage()
        r.rt, r.kt, r.at, r.bt = (two(n, [P, 2, T]) for n in ("rt", "kt", "at", "bt"))
        r.mid = two("mid", [P, 2, NT])
        rwkv_prepare(nc, m, r)
        r.vtok = a.sb("vtok", [P, NT, BW])
        r.vpad = a.sb("vpad", [P, NT, 4, P])
        tok = lambda ap: ap.rearrange("p (t n) -> p t n", t=NT)
        r.ktok = [tok(spare(SB_, 2)), tok(spare(SC_, 2))]
        r.btok = [tok(spare(SX, 2)), tok(spare(U_, 2))]
        r.y = [m.branch[:, 2:4, :], m.branch[:, 4:6, :]]
        zero_pads(nc, a, r.vpad)
        items = []
        for t in range(NT):
            cut = slice(t * P, (t + 1) * P)
            for c in range(2):
                cols = slice(c * P, (c + 1) * P)
                items.append(([(r.vtok[:, t, cols], 0, P), (r.vpad[:, t, 2 * c, 0:64], 0, 64),
                               (r.vpad[:, t, 2 * c + 1, 64:P], 64, P)], m.proj[:, V_ + c, cut]))
                for d in range(2):
                    items.append(([(r.ktok[d][:, t, cols], 0, P)], r.kt[d][:, c, cut]))
                    items.append(([(r.btok[d][:, t, cols], 0, P)], r.bt[d][:, c, cut]))
        turn_to_tokens(nc, m, items, "rwkv")
        rwkv_scan(nc, m, r)
    with Tools(nc, "rwkv_end") as a:
        rwkv_finish(nc, m, r)


class Stage:
    pass


def zero_pads(nc, a, pad):
    cleared = a.sem("pads_cleared")
    with nc.Block() as block:

        @block.gpsimd
        def _(pool):
            pool.memset(pad[:], 0.0).then_inc(cleared, 1)
            pool.wait_ge(cleared, 1)


def gla_prepare(nc, m, r):
    with Tools(nc, "gla_prepare") as a:
        up = a.sb("gla_up", [P, P])
        keep = a.sb("gkeep", [P, T])
        x, l, b, tail, e1, e2 = (a.sb(f"g_{n}", [P, T]) for n in ("x", "l", "b", "tail", "e1", "e2"))
        ps = a.ps("ps_gate", [P, 2, 1024])
        w_in, keep_set, up_mm, soft, cum, exps, prods, act_chain, dve_chain = a.sems(
            "gw_in", "gkeep_set", "gup_mm", "gsoft", "gcum", "gexps", "gprods", "gact_chain", "gdve_chain")
        tiles = lambda ap: ap.rearrange("p (t i) -> p t i", i=P)
        with nc.Block() as block:

            @block.sync
            def _(sp):
                for d in range(2):
                    lo = GA + 32 * d
                    sp.dma_start(up[lo:lo + 16, :], m.gla_a_up[0, d]).then_inc(w_in, 16)

            @block.gpsimd
            def _(pool):
                pool.memset(keep[:], 1.0).then_inc(keep_set, 1)
                pool.wait_ge(keep_set, 1)
                pool.memset(keep[:, ::P], 0.0).then_inc(keep_set, 1)

            @block.tensor
            def _(pe):
                pe.wait_ge(w_in, 32)
                for d in range(2):
                    rows = slice(GA + 32 * d, GA + 32 * d + 16)
                    for lo, hi in ((0, 512), (512, T)):
                        mm = pe.matmul(ps[:, d, lo:hi], up[rows, :], m.proj[rows, GDGA, lo:hi], start=True, stop=True)
                    mm.then_inc(up_mm, 1)

            @block.scalar
            def _(act):
                ch = Chain(act, act_chain)
                for d in range(2):
                    act.wait_ge(up_mm, d + 1)
                    act.wait_ge(prods, d)
                    ch.link(act.activation(x[:], ps[:, d, 0:T], ACT.Identity, bias=m.vec[:, GAB + d:GAB + d + 1]))
                    ch.link(act.activation(l[:], x[:], ACT.Abs))
                    ch.link(act.activation(l[:], l[:], ACT.Exp, scale=-1.0))
                    act.activation(l[:], l[:], ACT.Ln, bias=1.0).then_inc(soft, 1)
                    act.wait_ge(cum, d + 1)
                    act.activation(e1[:], r.cum[d][:], ACT.Exp)
                    act.activation(r.end[d][:], r.end[d][:], ACT.Exp)
                    act.activation(e2[:], tail[:], ACT.Exp).then_inc(exps, 1)

            @block.vector
            def _(dve):
                ch = Chain(dve, dve_chain)
                dve.wait_ge(keep_set, 2)
                ch.link(dve.tensor_scalar(r.q[:], m.proj[:, GQ, :], 32.0 ** -0.5, None, ALU.mult))
                for d in range(2):
                    dve.wait_ge(soft, d + 1)
                    ch.link(dve.scalar_tensor_tensor(out=x[:], in0=x[:], scalar=0.0, in1=l[:], op0=ALU.min,
                                                     op1=ALU.subtract))
                    ch.link(dve.tensor_scalar(x[:], x[:], 1.0 / 16.0, None, ALU.mult))
                    ch.link(dve.tensor_tensor_scan(b[:], keep[:], x[:], 0.0, ALU.mult, ALU.add))
                    ch.link(dve.tensor_copy(r.end[d][:], tiles(b[:])[:, :, P - 1]))
                    whole = tiles(b[:])[:, :, P - 1:P].to_broadcast([P, NT, P])
                    if d == 0:
                        ch.link(dve.tensor_copy(r.cum[0][:], b[:]))
                        dve.tensor_sub(tiles(tail[:]), whole, tiles(b[:])).then_inc(cum, 1)
                    else:
                        ch.link(dve.tensor_sub(tail[:], b[:], x[:]))
                        dve.tensor_sub(tiles(r.cum[1][:]), whole, tiles(tail[:])).then_inc(cum, 1)
                    dve.wait_ge(exps, d + 1)
                    dve.tensor_mul(r.qd[d][:], r.q[:], e1[:])
                    dve.tensor_mul(r.kd[d][:], m.proj[:, GK, :], e2[:]).then_inc(prods, 1)


def gla_scores(nc, m, r):
    H = 4
    cs = lambda n: m.const[:, n * P:(n + 1) * P]
    rounds = [(None, d) for d in range(2)] + [(li, d) for li in range(len(LEVELS)) for d in range(2)]
    with Tools(nc, "gla_scores") as a:
        two = lambda n: [a.sb(f"{n}_{b}", [P, T]) for b in range(2)]
        diff, ql, kl = two("diff"), two("ql"), two("kl")
        ps = a.ps("ps_gsc", [P, 8, 512])
        zeroed, from_mid, decay, ql_ok, kl_ok, sc_mm, copied, act_chain = a.sems(
            "gzeroed", "from_mid", "gdecay", "ql_ok", "kl_ok", "gsc_mm", "gcopied", "gs_act")
        with nc.Block() as block:

            @block.gpsimd
            def _(pool):
                for d in range(2):
                    z = pool.memset(r.sc[d][:], 0.0)
                z.then_inc(zeroed, 1)
                for n, (li, d) in enumerate(rounds[2:]):
                    pool.wait_ge(decay, n + 1)
                    if n >= 2:
                        pool.wait_ge(sc_mm, n + 1)
                    pool.tensor_mul(kl[n % 2][:], m.proj[:, GK, :], diff[n % 2][:]).then_inc(kl_ok, 1)

            @block.scalar
            def _(act):
                ch = Chain(act, act_chain)
                for n in range(len(rounds) - 2):
                    act.wait_ge(from_mid, n + 1)
                    ch.link(act.activation(diff[n % 2][:], diff[n % 2][:], ACT.Abs))
                    act.activation(diff[n % 2][:], diff[n % 2][:], ACT.Exp, scale=-1.0).then_inc(decay, 1)

            @block.vector
            def _(dve):
                def start(n):
                    li, d = rounds[2 + n]
                    h = LEVELS[li]
                    if n >= 2:
                        dve.wait_ge(ql_ok, n - 1)
                        dve.wait_ge(kl_ok, n - 1)
                    c = r.cum[d][:].rearrange("p (n w) -> p n w", w=2 * h)
                    at = h - 1 if d == 0 else h
                    dve.tensor_sub(diff[n % 2][:].rearrange("p (n w) -> p n w", w=2 * h), c,
                                   c[:, :, at:at + 1].to_broadcast([P, T // (2 * h), 2 * h])).then_inc(from_mid, 1)

                def copy(n):
                    li, d = rounds[n]
                    mask = cs(IDENT if li is None else (LEV_F, LEV_B)[d] + li).bitcast(U32)
                    dve.wait_ge(sc_mm, n + 1)
                    dve.copy_predicated(r.sc[d][:, :, 0:CTX, :],
                                        mask.unsqueeze(1).unsqueeze(1).to_broadcast([P, H, CTX, P]),
                                        ps[:, 0:4, :].rearrange("p h (t i) -> p h t i", t=CTX))
                    dve.copy_predicated(r.sc[d][:, :, CTX, :], mask.unsqueeze(1).to_broadcast([P, H, P]),
                                        ps[:, 4:8, 0:P]).then_inc(copied, 1)

                start(0)
                start(1)
                dve.wait_ge(zeroed, 1)
                copy(0)
                for n in range(len(rounds) - 2):
                    dve.wait_ge(decay, n + 1)
                    if n >= 2:
                        dve.wait_ge(sc_mm, n + 1)
                    dve.tensor_mul(ql[n % 2][:], r.q[:], diff[n % 2][:]).then_inc(ql_ok, 1)
                    copy(n + 1)
                    if n + 2 < len(rounds) - 2:
                        start(n + 2)
                copy(len(rounds) - 1)

            @block.tensor
            def _(pe):
                for n, (li, d) in enumerate(rounds):
                    if li is None:
                        q, k = r.q, m.proj[:, GK, :]
                    else:
                        q, k = ql[n % 2], kl[n % 2][:]
                        pe.wait_ge(ql_ok, n - 1)
                        pe.wait_ge(kl_ok, n - 1)
                    pe.wait_ge(copied, n)
                    for t in range(NT):
                        for h in range(H):
                            out = ps[:, h, t * P:(t + 1) * P] if t < CTX else ps[:, 4 + h, 0:P]
                            cut = slice(t * P, (t + 1) * P)
                            mm = pe.matmul(out, k[32 * h:32 * h + 32, cut], q[32 * h:32 * h + 32, cut],
                                           start=True, stop=True)
                    mm.then_inc(sc_mm, 1)


def gla_scan(nc, m, r):
    tile_of = ((CTX, 0, 1, 2, 3), (CTX, 3, 2, 1, 0))
    with Tools(nc, "gla_scan") as a:
        two = lambda n, shape: [a.sb(f"{n}_{d}", shape) for d in range(2)]
        S, Sfin, inc = two("gS", [P, BW]), two("gSfin", [P, BW]), two("ginc", [P, BW])
        S0 = two("gS0", [P, BW])
        ps_o = [a.ps(f"ps_go{d}", [P, 2, P]) for d in range(2)]
        ps_S = [a.ps(f"ps_gS{d}", [P, BW]) for d in range(2)]
        sem2 = lambda n: [a.sem(f"{n}_{d}") for d in range(2)]
        o_mm, S_mm, S_set, o_out, ctx_ok = (sem2(n) for n in ("go_mm", "gS_mm", "gS_set", "go_out", "gctx"))
        zeroed, states_in, states_out, chain = a.sems("gs_zeroed", "gstates_in", "gstates_out", "gs_chain")
        mask = m.const[:, GBLK * P:(GBLK + 2) * P]
        with nc.Block() as block:

            @block.sync
            def _(sp):
                sp.wait_ge(zeroed, 1)
                for d in range(2):
                    for h in range(4):
                        sp.dma_start(S0[d][32 * h:32 * h + 32, 64 * h:64 * h + 64], m.state_gla[0, 0, d, h]
                                     ).then_inc(states_in, 16)
                for d in range(2):
                    sp.wait_ge(ctx_ok[d], 1)
                    for h in range(4):
                        sp.dma_start(m.new_gla[0, 0, d, h], Sfin[d][32 * h:32 * h + 32, 64 * h:64 * h + 64]
                                     ).then_inc(states_out, 16)
                sp.wait_ge(states_out, 128)

            @block.gpsimd
            def _(pool):
                for d in range(2):
                    z = pool.memset(S0[d][:], 0.0)
                z.then_inc(zeroed, 1)

            @block.tensor
            def _(pe):
                for s in range(NT):
                    for d in range(2):
                        t = tile_of[d][s]
                        if s:
                            pe.wait_ge(S_set[d], s)
                        pe.matmul(ps_S[d][:], r.kdtok[d][:, t, :], r.vtok[:, t, :], start=True, stop=True
                                  ).then_inc(S_mm[d], 1)
                        pe.wait_ge(o_out[d], s)
                        for c in range(2):
                            if s:
                                pe.matmul(ps_o[d][:, c, :], S[d][:, c * P:(c + 1) * P],
                                          r.qd[d][:, t * P:(t + 1) * P], start=True, stop=False)
                            for h in (2 * c, 2 * c + 1):
                                mm = pe.matmul(ps_o[d][:, c, :], r.vpad[:, t, h, :], r.sc[d][:, h, t, :],
                                               start=(s == 0 and h % 2 == 0), stop=(h % 2 == 1))
                        mm.then_inc(o_mm[d], 1)

            @block.scalar
            def _(act):
                for s in range(NT):
                    for d in range(2):
                        t = tile_of[d][s]
                        act.wait_ge(o_mm[d], s + 1)
                        act.activation(r.o[d][:, :, t * P:(t + 1) * P], ps_o[d][:], ACT.Copy).then_inc(o_out[d], 1)

            @block.vector
            def _(dve):
                ch = Chain(dve, chain)
                for s in range(NT - 1):
                    for d in range(2):
                        t = tile_of[d][s]
                        dve.wait_ge(S_mm[d], s + 1)
                        if s == 0:
                            dve.tensor_mul(Sfin[d][:], ps_S[d][:], mask).then_inc(ctx_ok[d], 1)
                            dve.wait_ge(states_in, 128)
                            dve.tensor_copy(S[d][:], S0[d][:]).then_inc(S_set[d], 1)
                        else:
                            ch.link(dve.tensor_mul(inc[d][:], ps_S[d][:], mask))
                            dve.wait_ge(o_mm[d], s + 1)
                            dve.scalar_tensor_tensor(out=S[d][:], in0=S[d][:], scalar=r.end[d][:, t:t + 1],
                                                     in1=inc[d][:], op0=ALU.mult, op1=ALU.add
                                                     ).then_inc(S_set[d], 1)


def gla_finish(nc, m, r):
    with Tools(nc, "gla_finish") as a:
        o, o2, sg = (a.sb(n, [P, 2, T]) for n in ("o_sum", "o_sq", "o_gate"))
        ps = a.ps("ps_oms", [P, 2, 1024])
        ready, mm_s, rms, gate, chain = a.sems("gf_ready", "gf_sum", "gf_rms", "gf_gate", "gf_chain")
        with nc.Block() as block:

            @block.tensor
            def _(pe):
                pe.wait_ge(ready, 1)
                head_sum(pe, m, ps, o2).then_inc(mm_s, 1)

            @block.scalar
            def _(act):
                act.activation(sg[:], m.proj[:, GG:GG + 2, :], ACT.Sigmoid).then_inc(gate, 1)
                act.wait_ge(ready, 2)
                act.activation(o2[:], o2[:], ACT.Sqrt).then_inc(rms, 1)

            @block.vector
            def _(dve):
                ch = Chain(dve, chain)
                ch.link(dve.tensor_add(o[:], r.o[0][:], r.o[1][:]))
                dve.tensor_mul(o2[:], o[:], o[:]).then_inc(ready, 1)
                dve.wait_ge(gate, 1)
                ch.link(dve.tensor_mul(sg[:], sg[:], m.proj[:, GG:GG + 2, :]))
                for c in range(2):
                    ch.link(dve.tensor_scalar(sg[:, c, :], sg[:, c, :], m.vec[:, GNORM + c:GNORM + c + 1], None,
                                              ALU.mult))
                dve.wait_ge(mm_s, 1)
                dve.tensor_scalar(o2[:], ps[:, :, 0:T], 1.0 / 64, EPS, ALU.mult, ALU.add).then_inc(ready, 1)
                dve.wait_ge(rms, 1)
                ch.link(dve.reciprocal(o2[:], o2[:]))
                ch.link(dve.tensor_mul(o[:], o[:], o2[:]))
                dve.tensor_mul(m.branch[:, 4:6, :], o[:], sg[:])


def gla(nc, m):
    with Tools(nc, "gla") as a:
        two = lambda n, shape: [a.sb(f"{n}{d}", shape) for d in range(2)]
        r = Stage()
        r.q = a.sb("g_q", [P, T])
        r.cum, r.qd, r.kd = two("g_cum", [P, T]), two("g_qd", [P, T]), two("g_kd", [P, T])
        r.end = two("g_end", [P, NT])
        gla_prepare(nc, m, r)
        r.vtok, r.vpad = a.sb("g_vtok", [P, NT, BW]), a.sb("g_vpad", [P, NT, 4, P])
        r.kdtok = two("g_kdtok", [P, NT, P])
        r.sc = two("g_sc", [P, 4, NT, P])
        r.o = two("g_o", [P, 2, T])
        zero_pads(nc, a, r.vpad)
        items = []
        for t in range(NT):
            cut = slice(t * P, (t + 1) * P)
            for c in range(2):
                items.append(([(r.vtok[:, t, c * P:(c + 1) * P], 0, P), (r.vpad[:, t, 2 * c, 0:64], 0, 64),
                               (r.vpad[:, t, 2 * c + 1, 64:P], 64, P)], m.proj[:, GV + c, cut]))
            for d in range(2):
                items.append(([(r.kdtok[d][:, t, :], 0, P)], r.kd[d][:, cut]))
        turn_to_tokens(nc, m, items, "gla")
        gla_scores(nc, m, r)
        gla_scan(nc, m, r)
        gla_finish(nc, m, r)


def merge_branches(nc, m):
    with Tools(nc, "merge_branches") as a:
        hT = a.sb("hT_back", [P, KD, T])
        w = a.sb("w_merge_tiles", [P, 2, (KD + 2) * P])
        gate = a.sb("merge_gate", [P, 2, T])
        part = a.sb("merge_part", [P, 2, T])
        acc = a.sb("merge_acc", [P, T])
        ps_l = a.ps("ps_logit", [P, 2, 1024])
        ps_p = a.ps("ps_proj", [P, 2, 1024])
        hT_in, w_in = a.sem("hT_in"), a.ring("wm_in", 2)
        done, gated, multiplied = a.ring("wm_done", 2), a.ring("wm_gate", 2), a.ring("wm_mul", 2)
        chain = a.sem("wm_chain")
        with nc.Block() as block:

            @block.sync
            def _(sp):
                sp.dma_start(hT[:], m.hT_dram).then_inc(hT_in, 16)
                def lap(i):
                    for b in range(2):
                        sp.wait_ge(done[b], i)
                        sp.dma_start(w[:, b, :], m.w_merge[bass.ds(2 * i + b, 1)].rearrange("a p n -> (a p) n")
                                     ).then_inc(w_in[b], 16)

                lap(0)
                with sp.Fori(1, KD * NB // 2) as i:
                    lap(i)

            @block.tensor
            def _(pe):
                pe.wait_ge(hT_in, 16)
                def step(i):
                    for n in range(NB):
                        b, lap = n % 2, 2 * i + n // 2
                        pe.wait_ge(w_in[b], 16 * lap + 16)
                        pe.wait_ge(multiplied[b], lap)
                        for k in range(KD):
                            for lo, hi in ((0, 512), (512, T)):
                                pe.matmul(ps_l[:, b, lo:hi], w[:, b, k * P:(k + 1) * P], hT[:, k, lo:hi],
                                          start=(k == 0), stop=(k == KD - 1))
                        for k in range(2):
                            for lo, hi in ((0, 512), (512, T)):
                                mm = pe.matmul(ps_p[:, b, lo:hi], w[:, b, (KD + k) * P:(KD + k + 1) * P],
                                               m.branch[:, 2 * n + k, lo:hi], start=(k == 0), stop=(k == 1))
                        mm.then_inc(done[b], 1)

                step(0)
                with pe.Fori(1, KD) as i:
                    step(i)

            @block.scalar
            def _(act):
                def step(i):
                    for n in range(NB):
                        b, lap = n % 2, 2 * i + n // 2
                        act.wait_ge(done[b], lap + 1)
                        act.wait_ge(multiplied[b], lap)
                        act.activation(gate[:, b, :], ps_l[:, b, 0:T], ACT.Sigmoid).then_inc(gated[b], 1)

                step(0)
                with act.Fori(1, KD) as i:
                    step(i)

            @block.vector
            def _(dve):
                ch = Chain(dve, chain)
                with ch.laps(KD, 4) as i:
                    for n in range(NB):
                        b, lap = n % 2, 2 * i + n // 2
                        dve.wait_ge(gated[b], lap + 1)
                        dve.tensor_mul(part[:, b, :], gate[:, b, :], ps_p[:, b, 0:T]).then_inc(multiplied[b], 1)
                        dve.wait_ge(multiplied[b], lap + 1)
                        if n == 0:
                            ch.link(dve.tensor_copy(acc[:], part[:, b, :]))
                        elif n < NB - 1:
                            ch.link(dve.tensor_add(acc[:], acc[:], part[:, b, :]))
                        else:
                            ch.link(dve.tensor_add(m.merged[:, bass.ds(i, 1), :].rearrange("p a t -> p (a t)"),
                                                   acc[:], part[:, b, :]))


N_EXP, N_GRP, TOP_K, TOP_G, FF = 64, 8, 8, 4, 256
MAX_BLOCKS = N_EXP + T * TOP_K // P
TAB = 3


def group(t):
    return 0 if t == CTX else 1


def output_and_route(nc, m):
    with Tools(nc, "output_and_route") as a:
        w_out = a.sb("w_out_sb", [P, KD, D])
        w_r = a.sb("w_router_sb", [P, KD, N_EXP])
        w_gu = a.sb("ws_gu", [P, KD, 2 * FF])
        w_dn = a.sb("ws_dn", [P, 2, D])
        mod = a.sb("mod_rows_b", [P, 2, 3, D])
        sq = a.sb("sq_e", [P, D])
        h2 = a.sb("h2", [P, 2, D])
        h2T = a.sb("h2T", [P, 2, KD, P])
        ss, rms = a.sb("ss_e", [P, NT]), a.sb("rms_e", [P, NT])
        sg, hs, hsT = a.sb("sg_e", [P, FF]), a.sb("hs_e", [P, 2, FF]), a.sb("hsT_e", [P, 2, FF])
        bias = a.sb("b_router_b", [P, N_EXP])
        rc = a.sb("route_c", [P, N_EXP + 1 + NT])
        score = a.sb("score", [P, NT, N_EXP])
        sel, selm, chosen = a.sb("sel", [P, N_EXP]), a.sb("selm", [P, N_EXP]), a.sb("chosen", [P, NT, N_EXP])
        top, gs, g8, gm, pen = (a.sb(n, s) for n, s in (("top", [P, N_GRP, 8]), ("gs", [P, 8]), ("g8", [P, 8]),
                                                       ("gm", [P, 8]), ("pen", [P, 8])))
        idx_u, idx_g, eq_g = a.sb("idx_u", [P, 8], U32), a.sb("idx_g", [P, 8]), a.sb("eq_g", [P, TOP_G, N_GRP])
        e8, idx_e = a.sb("e8", [P, 8]), a.sb("idx_e", [P, NT, 8])
        eq = a.sb("eq_e", [P, NT, TOP_K, N_EXP])
        wide = a.sb("wide_e", [P, TOP_K, N_EXP])
        pos_in, pos8, addr = a.sb("pos_in", [P, N_EXP]), a.sb("pos8", [P, NT, 8]), a.sb("addr", [P, NT, 8])
        addr_u, tok_u = a.sb("addr_u", [P, NT, 8], U32), a.sb("tok_u", [P, NT], U32)
        zero_u = a.sb("zero_u", [P, N_EXP * T // P], U32)
        wsum = a.sb("wsum", [P, 1])
        cnt, nb, end, base, tmp = (a.sb(n, [P, N_EXP]) for n in ("cnt", "nblk", "end", "basee", "tmpe"))
        col = a.sb("col_e", [P, 8])
        tab = a.sb("tab", [P, TAB], I32)
        ps_mix, ps_t, ps_r = a.ps("ps_mix", [P, D]), a.ps("ps_t2", [P, D]), a.ps("ps_r", [P, 512])
        ps_gu, ps_y = a.ps("ps_gu", [P, 2 * FF]), a.ps("ps_y", [P, D])
        (w_in, r_in, mix_mm, mix_out, sq_ok, ms_ok, rms_ok, h2_ok, h2_store, turned, h2T_ok, r_mm, r_out, gu_mm, sig_ok,
         hs_ok, hs_turned, hsT_ok, y_mm, y_out, m_ok, pos_mm, pos_ok, zeroed, list_zero, addr_ok, scattered, cnt_mm,
         tab_ok, tab_store, tab_in, e_chain) = a.sems(*(f"e_{n}" for n in (
            "w_in", "r_in", "mix_mm", "mix_out", "sq_ok", "ms_ok", "rms_ok", "h2_ok", "h2_store", "turned", "h2T_ok", "r_mm",
            "r_out", "gu_mm", "sig_ok", "hs_ok", "hs_turned", "hsT_ok", "y_mm", "y_out", "m_ok", "pos_mm", "pos_ok",
            "zeroed", "list_zero", "addr_ok", "scattered", "cnt_mm", "tab_ok", "tab_store", "tab_in", "chain")))
        iota_e, iota_p = rc[:, 0:N_EXP], rc[:, N_EXP:N_EXP + 1]
        ident, ones, before = (m.const[:, n * P:(n + 1) * P] for n in (IDENT, ONES, LT))
        row = lambda ap, n: ap.unsqueeze(1).to_broadcast([P, n, ap.shape[1]])
        with nc.Block() as block:

            @block.sync
            def _(sp):
                sp.dma_start(w_out[:], m.w_out[0].rearrange("(k p) n -> p k n", p=P)).then_inc(w_in, 16)
                for i, g in enumerate((0, 1)):
                    for j, r in enumerate((2, 3, 4)):
                        sp.dma_start(mod[:, g, j, :], m.mod_dram[g, r:r + 1, :].to_broadcast([P, D])
                                     ).then_inc(w_in, 16)
                sp.dma_start(m.x[:, 0:CTX, :], m.x_sample[0].rearrange("(t p) d -> p t d", p=P)).then_inc(w_in, 16)
                sp.dma_start(m.x[:, CTX, :], m.x_prompt[0]).then_inc(w_in, 16)
                sp.dma_start(w_r[:], m.w_router[0].rearrange("(p k) n -> p k n", k=KD)).then_inc(r_in, 16)
                sp.dma_start(bias[:], m.b_router.to_broadcast([P, N_EXP])).then_inc(r_in, 16)
                sp.dma_start(rc[:], m.route_constants).then_inc(r_in, 16)
                sp.dma_start(w_gu[:, :, 0:FF], m.ws_gate[0].rearrange("(p k) n -> p k n", k=KD)).then_inc(r_in, 16)
                sp.dma_start(w_gu[:, :, FF:], m.ws_up[0].rearrange("(p k) n -> p k n", k=KD)).then_inc(r_in, 16)
                sp.dma_start(w_dn[:], m.ws_down[0].rearrange("(k p) n -> p k n", p=P)).then_inc(r_in, 16)
                for t in range(NT):
                    sp.wait_ge(h2_ok, t + 1)
                    if t >= 1:
                        sp.wait_ge(h2_store, 16 * t)
                    sp.dma_start(m.h2_dram[t * P:(t + 1) * P, :], h2[:, t % 2, :]).then_inc(h2_store, 16)
                sp.wait_ge(tab_ok, 1)
                sp.dma_start(m.tab_dram, tab[:]).then_inc(tab_store, 16)
                sp.wait_ge(tab_store, 16)
                sp.dma_start(m.table[:], m.tab_dram.rearrange("b c -> (b c)").unsqueeze(0)).then_inc(tab_in, 16)
                sp.wait_ge(tab_in, 16)
                sp.wait_ge(h2_store, 16 * NT)

            @block.gpsimd
            def _(pool):
                pool.memset(zero_u[:], 0).then_inc(zeroed, 1)
                pool.wait_ge(zeroed, 1)
                pool.dma_start(m.list_dram.rearrange("(p n) a -> p (n a)", p=P), zero_u[:]).then_inc(list_zero, 16)
                pool.wait_ge(list_zero, 16)
                for t in range(NT):
                    pool.wait_ge(addr_ok, t + 1)
                    for j in range(TOP_K):
                        pool.indirect_dma_start(
                            m.list_dram, bass.IndirectOffsetOnAxis(ap=addr_u[:, t, j:j + 1], axis=0),
                            tok_u[:, t:t + 1], None).then_inc(scattered, 16)
                        pool.wait_ge(scattered, 16 * (t * TOP_K + j + 1))

            @block.tensor
            def _(pe):
                def mix(t):
                    pe.wait_ge(mix_out, t)
                    for n in range(2):
                        for k in range(KD):
                            mm = pe.matmul(ps_mix[:, n * 512:(n + 1) * 512], m.merged[:, k, t * P:(t + 1) * P],
                                           w_out[:, k, n * 512:(n + 1) * 512], start=(k == 0), stop=(k == KD - 1))
                    mm.then_inc(mix_mm, 1)

                def turn(t):
                    pe.wait_ge(h2_ok, t + 1)
                    pe.wait_ge(hsT_ok, t - 1) if t >= 2 else None
                    for k in range(KD):
                        mm = pe.transpose(ps_t[:, k * P:(k + 1) * P], h2[:, t % 2, k::KD], ident)
                    mm.then_inc(turned, 1)

                def route(t):
                    pe.wait_ge(h2T_ok, t + 1)
                    pe.wait_ge(pos_ok, t)
                    for k in range(KD):
                        mm = pe.matmul(ps_r[:, 0:N_EXP], h2T[:, t % 2, k, :], w_r[:, k, :],
                                       start=(k == 0), stop=(k == KD - 1))
                    mm.then_inc(r_mm, 1)
                    pe.wait_ge(hs_ok, t)
                    for k in range(KD):
                        mm = pe.matmul(ps_gu[:], h2T[:, t % 2, k, :], w_gu[:, k, :],
                                       start=(k == 0), stop=(k == KD - 1))
                    mm.then_inc(gu_mm, 1)

                def place(t):
                    pe.wait_ge(m_ok, t + 1)
                    pe.matmul(ps_r[:, 128:128 + N_EXP], before, chosen[:, t, :], start=True, stop=(t == 0))
                    for u in range(t):
                        pe.matmul(ps_r[:, 128:128 + N_EXP], ones, chosen[:, u, :], start=False, stop=(u == t - 1))
                    pe.matmul(ps_r[:, 256:257], ones, chosen[:, t, 0:1], start=True, stop=True).then_inc(pos_mm, 1)

                def down(t):
                    pe.wait_ge(hs_ok, t + 1)
                    pe.wait_ge(h2T_ok, min(t + 2, NT))
                    for k in range(2):
                        mm = pe.transpose(ps_t[:, k * P:(k + 1) * P], hs[:, t % 2, k * P:(k + 1) * P], ident)
                    mm.then_inc(hs_turned, 1)
                    pe.wait_ge(hsT_ok, t + 1)
                    pe.wait_ge(y_out, t)
                    for n in range(2):
                        for k in range(2):
                            mm = pe.matmul(ps_y[:, n * 512:(n + 1) * 512], hsT[:, t % 2, k * P:(k + 1) * P],
                                           w_dn[:, k, n * 512:(n + 1) * 512], start=(k == 0), stop=(k == 1))
                    mm.then_inc(y_mm, 1)

                pe.wait_ge(w_in, 16 * 9)
                mix(0)
                pe.wait_ge(r_in, 16 * 6)
                for t in range(NT):
                    if t + 1 < NT:
                        mix(t + 1)
                    turn(t)
                    route(t)
                    if t >= 1:
                        down(t - 1)
                    place(t)
                down(NT - 1)
                pe.wait_ge(pos_ok, NT)
                for t in range(NT):
                    mm = pe.matmul(ps_r[:, 0:N_EXP], ones, chosen[:, t, :], start=(t == 0), stop=(t == NT - 1))
                mm.then_inc(cnt_mm, 1)

            @block.scalar
            def _(act):
                for t in range(NT + 1):
                    if t < NT:
                        act.wait_ge(mix_out, t + 1)
                        act.activation(sq[:], m.x[:, t, :], ACT.Square, accum_out=ss[:, t:t + 1]).then_inc(sq_ok, 1)
                        act.wait_ge(ms_ok, t + 1)
                        act.activation(rms[:, t:t + 1], ss[:, t:t + 1], ACT.Sqrt).then_inc(rms_ok, 1)
                        act.wait_ge(turned, t + 1)
                        act.activation(h2T[:, t % 2].rearrange("p k t -> p (k t)"), ps_t[:], ACT.Copy
                                       ).then_inc(h2T_ok, 1)
                        act.wait_ge(r_mm, t + 1)
                        act.activation(score[:, t, :], ps_r[:, 0:N_EXP], ACT.Sigmoid).then_inc(r_out, 1)
                        act.wait_ge(gu_mm, t + 1)
                        act.wait_ge(hs_ok, t)
                        act.activation(sg[:], ps_gu[:, 0:FF], ACT.Sigmoid).then_inc(sig_ok, 1)
                    if t >= 1:
                        u = t - 1
                        act.wait_ge(hs_turned, u + 1)
                        act.activation(hsT[:, u % 2, :], ps_t[:, 0:FF], ACT.Copy).then_inc(hsT_ok, 1)
                        act.wait_ge(y_mm, u + 1)
                        act.activation(m.acc[:, u, :], ps_y[:], ACT.Copy).then_inc(y_out, 1)

            @block.vector
            def _(dve):
                ch = Chain(dve, e_chain)

                def norm(t):
                    g = group(t)
                    dve.wait_ge(mix_mm, t + 1)
                    if t >= 2:
                        dve.wait_ge(h2_store, 16 * (t - 1))
                        dve.wait_ge(turned, t - 1)
                    ch.link(dve.tensor_mul(h2[:, t % 2, :], ps_mix[:], mod[:, g, 0, :]))
                    dve.tensor_add(m.x[:, t, :], m.x[:, t, :], h2[:, t % 2, :]).then_inc(mix_out, 1)
                    dve.wait_ge(sq_ok, t + 1)
                    dve.tensor_scalar(ss[:, t:t + 1], ss[:, t:t + 1], 1.0 / D, EPS, ALU.mult, ALU.add
                                      ).then_inc(ms_ok, 1)
                    dve.wait_ge(rms_ok, t + 1)
                    ch.link(dve.reciprocal(rms[:, t:t + 1], rms[:, t:t + 1]))
                    ch.link(dve.scalar_tensor_tensor(out=h2[:, t % 2, :], in0=m.x[:, t, :], scalar=rms[:, t:t + 1],
                                                     in1=mod[:, g, 2, :], op0=ALU.mult, op1=ALU.mult))
                    dve.tensor_add(h2[:, t % 2, :], h2[:, t % 2, :], mod[:, g, 1, :]).then_inc(h2_ok, 1)

                def silu(t):
                    dve.wait_ge(sig_ok, t + 1)
                    if t >= 2:
                        dve.wait_ge(hs_turned, t - 1)
                    ch.link(dve.tensor_mul(hs[:, t % 2, :], sg[:], ps_gu[:, 0:FF]))
                    dve.tensor_mul(hs[:, t % 2, :], hs[:, t % 2, :], ps_gu[:, FF:]).then_inc(hs_ok, 1)

                def choose(t):
                    dve.wait_ge(r_out, t + 1)
                    ch.link(dve.tensor_add(sel[:], score[:, t, :], bias[:]))
                    for g in range(N_GRP):
                        s = dve.max(top[:, g, :], sel[:, g * 8:(g + 1) * 8])
                    ch.link(s)
                    ch.link(dve.tensor_add(gs[:], top[:, :, 0], top[:, :, 1]))
                    ch.link(dve.max(g8[:], gs[:]))
                    ch.link(dve.max_index(idx_u[:], g8[:], gs[:]))
                    ch.link(dve.tensor_copy(idx_g[:], idx_u[:]))
                    ch.link(dve.tensor_tensor(eq_g[:], iota_e[:, 0:N_GRP].unsqueeze(1).to_broadcast([P, TOP_G, N_GRP]),
                                              idx_g[:, 0:TOP_G].unsqueeze(2).to_broadcast([P, TOP_G, N_GRP]),
                                              ALU.is_equal))
                    ch.link(dve.tensor_reduce(gm[:], eq_g[:].rearrange("p j g -> p g j"), AX.X, ALU.add))
                    ch.link(dve.tensor_scalar(pen[:], gm[:], 1.0, 1e30, ALU.subtract, ALU.mult))
                    members = lambda ap: ap.rearrange("p (g e) -> p g e", e=8)
                    of_group = lambda ap: ap.unsqueeze(2).to_broadcast([P, N_GRP, 8])
                    ch.link(dve.tensor_mul(members(selm[:]), members(sel[:]), of_group(gm[:])))
                    ch.link(dve.tensor_add(members(selm[:]), members(selm[:]), of_group(pen[:])))
                    ch.link(dve.max(e8[:], selm[:]))
                    ch.link(dve.max_index(idx_u[:], e8[:], selm[:]))
                    ch.link(dve.tensor_copy(idx_e[:, t, :], idx_u[:]))
                    ch.link(dve.tensor_tensor(eq[:, t], row(iota_e, TOP_K),
                                              idx_e[:, t, :].unsqueeze(2).to_broadcast([P, TOP_K, N_EXP]),
                                              ALU.is_equal))
                    dve.tensor_reduce(chosen[:, t, :], eq[:, t].rearrange("p j e -> p e j"), AX.X, ALU.add
                                      ).then_inc(m_ok, 1)
                    ch.link(dve.tensor_mul(wide[:], eq[:, t], row(score[:, t, :], TOP_K)))
                    ch.link(dve.tensor_reduce(m.weight[:, t, :], wide[:], AX.X, ALU.add))
                    ch.link(dve.tensor_reduce(wsum[:], m.weight[:, t, :], AX.X, ALU.add))
                    ch.link(dve.reciprocal(wsum[:], wsum[:]))
                    ch.link(dve.tensor_scalar(m.weight[:, t, :], m.weight[:, t, :], wsum[:], 2.5, ALU.mult, ALU.mult))

                def places(t):
                    dve.wait_ge(pos_mm, t + 1)
                    dve.tensor_copy(pos_in[:], ps_r[:, 128:128 + N_EXP]).then_inc(pos_ok, 1)
                    dve.wait_ge(pos_ok, t + 1)
                    ch.link(dve.tensor_mul(wide[:], eq[:, t], row(pos_in[:], TOP_K)))
                    ch.link(dve.tensor_reduce(pos8[:, t, :], wide[:], AX.X, ALU.add))
                    ch.link(dve.scalar_tensor_tensor(out=addr[:, t, :], in0=idx_e[:, t, :], scalar=float(T),
                                                     in1=pos8[:, t, :], op0=ALU.mult, op1=ALU.add))
                    dve.tensor_copy(addr_u[:, t, :], addr[:, t, :]).then_inc(addr_ok, 1)

                dve.wait_ge(w_in, 16 * 9)
                norm(0)
                dve.wait_ge(r_in, 16 * 6)
                ch.link(dve.tensor_copy(tok_u[:], rc[:, N_EXP + 1:N_EXP + 1 + NT]))
                for t in range(NT):
                    if t + 1 < NT:
                        norm(t + 1)
                    choose(t)
                    silu(t)
                    places(t)
                dve.wait_ge(cnt_mm, 1)
                ch.link(dve.tensor_copy(cnt[:], ps_r[:, 0:N_EXP]))
                ch.link(dve.tensor_scalar(nb[:], cnt[:], 0.0, None, ALU.is_gt))
                for b in range(1, NT):
                    ch.link(dve.scalar_tensor_tensor(out=nb[:], in0=cnt[:], scalar=float(P * b), in1=nb[:],
                                                     op0=ALU.is_gt, op1=ALU.add))
                ch.link(dve.tensor_tensor_scan(end[:], ones[:, 0:N_EXP], nb[:], 0.0, ALU.mult, ALU.add))
                ch.link(dve.tensor_sub(base[:], end[:], nb[:]))
                ch.link(dve.tensor_scalar(tmp[:], end[:], iota_p, None, ALU.is_le))
                ch.link(dve.tensor_reduce(col[:, 0:1], tmp[:], AX.X, ALU.add))
                ch.link(dve.tensor_scalar(col[:, 0:1], col[:, 0:1], float(N_EXP - 1), None, ALU.min))
                ch.link(dve.tensor_scalar(tmp[:], iota_e, col[:, 0:1], None, ALU.is_equal))
                ch.link(dve.tensor_mul(tmp[:], tmp[:], base[:]))
                ch.link(dve.tensor_reduce(col[:, 1:2], tmp[:], AX.X, ALU.add))
                ch.link(dve.tensor_sub(col[:, 1:2], iota_p, col[:, 1:2]))
                ch.link(dve.tensor_scalar(col[:, 1:2], col[:, 1:2], 0.0, float(NT - 1), ALU.max, ALU.min))
                ch.link(dve.tensor_scalar(col[:, 3:4], col[:, 1:2], float(P), None, ALU.mult))
                ch.link(dve.tensor_scalar(tmp[:], iota_e, 2.0, end[:, N_EXP - 1:N_EXP], ALU.mult, ALU.is_lt))
                ch.link(dve.tensor_reduce(col[:, 2:3], tmp[:], AX.X, ALU.add))
                ch.link(dve.tensor_copy(m.laps[:], col[:, 2:3]))
                ch.link(dve.tensor_tensor_scan(end[:], ones[:, 0:N_EXP], cnt[:], 0.0, ALU.mult, ALU.add))
                ch.link(dve.tensor_sub(base[:], end[:], cnt[:]))
                ch.link(dve.tensor_scalar(tmp[:], iota_e, col[:, 0:1], None, ALU.is_equal))
                ch.link(dve.tensor_mul(tmp[:], tmp[:], base[:]))
                ch.link(dve.tensor_reduce(col[:, 2:3], tmp[:], AX.X, ALU.add))
                ch.link(dve.scalar_tensor_tensor(out=col[:, 2:3], in0=col[:, 3:4], scalar=1.0, in1=col[:, 2:3],
                                                 op0=ALU.mult, op1=ALU.add))
                dve.tensor_copy(tab[:], col[:, 0:TAB]).then_inc(tab_ok, 1)
                for t in range(NT):
                    ch.link(dve.tensor_mul(wide[:], eq[:, t], row(base[:], TOP_K)))
                    ch.link(dve.tensor_reduce(addr[:, t, :], wide[:], AX.X, ALU.add))
                    ch.link(dve.tensor_add(addr[:, t, :], addr[:, t, :], pos8[:, t, :]))
                ch.link(dve.tensor_copy(m.y_row[:], addr[:]))


def experts(nc, m):
    with Tools(nc, "experts") as a:
        w_gu = a.sb("we_gu", [P, 2, KD, 2 * FF])
        w_dn = a.sb("we_dn", [P, 2, 2, D])
        idx = a.sb("idx_b", [P, 2, 1], U32)
        xg = a.sb("xg", [P, 2, D])
        xT = a.sb("xgT", [P, 2, KD, P])
        sg, hs, hsT = a.sb("sg_b", [P, 2, FF]), a.sb("hs_b", [P, 2, FF]), a.sb("hsT_b", [P, 2, FF])
        y = a.sb("y_b", [P, 2, D])
        ps_x = a.ps("ps_x", [P, 2, D])
        ps_gu = a.ps("ps_gu_b", [P, 2, 2 * FF])
        ps_y = a.ps("ps_y_b", [P, D])
        (gu_in, dn_in, idx_in, gathered, turned, xT_ok, gu_mm, sig_ok, mul_ok, hs_ok, hs_turned, hsT_ok, y_mm,
         y_store) = (a.ring(f"b_{n}", 2) for n in (
            "gu_in", "dn_in", "idx_in", "gathered", "turned", "xT_ok", "gu_mm", "sig_ok", "mul_ok", "hs_ok",
            "hs_turned", "hsT_ok", "y_mm", "y_store"))
        y_half_ok = [a.ring(f"b_y_half{c}_ok", 2) for c in range(2)]
        laps = lambda eng: eng.value_load(m.laps[0:1, 0:1], min_val=1, max_val=MAX_BLOCKS // 2)
        ident = m.const[:, 0:P]

        lists = m.list_dram.rearrange("(e b p) c -> e b p c", e=N_EXP, p=P)
        tick, tick_set = a.sb("tick", [P, 1]), a.sem("tick_set")
        with nc.Block() as block:

            @block.sync
            def _(sp):
                n = laps(sp)

                def entry(blk, c, top):
                    return sp.value_load(m.table[0:1, bass.ds(TAB * blk + c, 1)], min_val=0, max_val=top)

                def load_idx(b, blk, lap):
                    e, part = entry(blk, 0, N_EXP - 1), entry(blk, 1, NT - 1)
                    sp.wait_ge(gathered[b], 16 * lap)
                    sp.dma_start(idx[:, b, :], lists[bass.ds(e, 1), bass.ds(part, 1)].rearrange("a b p c -> (a b p) c")
                                 ).then_inc(idx_in[b], 16)

                for b in range(2):
                    load_idx(b, b, 0)
                def lap(i):
                    for b in range(2):
                        e = entry(2 * i + b, 0, N_EXP - 1)
                        w = lambda ap: ap[0][bass.ds(e, 1)]
                        sp.wait_ge(gu_mm[b], i)
                        sp.dma_start(w_gu[:, b, :, 0:FF], w(m.we_gate).rearrange("a (p k) n -> p (a k) n", k=KD)
                                     ).then_inc(gu_in[b], 16)
                        sp.dma_start(w_gu[:, b, :, FF:], w(m.we_up).rearrange("a (p k) n -> p (a k) n", k=KD)
                                     ).then_inc(gu_in[b], 16)
                        sp.wait_ge(y_mm[b], 2 * i)
                        sp.dma_start(w_dn[:, b], w(m.we_down).rearrange("a (k p) n -> p (a k) n", p=P)
                                     ).then_inc(dn_in[b], 16)
                        load_idx(b, 2 * i + 2 + b, i + 1)

                lap(0)
                with sp.Fori(1, n) as i:
                    lap(i)

            @block.gpsimd
            def _(pool):
                pool.memset(m.zero[:], 0.0).then_inc(tick_set, 1)
                n = laps(pool)

                def gather(b, lap):
                    pool.wait_ge(tick_set, 1 + 2 * lap + b)
                    pool.wait_ge(idx_in[b], 16 * lap + 16)
                    pool.tensor_add(tick[:], m.zero[:], m.zero[:]).then_inc(tick_set, 1)
                    pool.indirect_dma_start(xg[:, b, :], None, m.h2_dram,
                                            bass.IndirectOffsetOnAxis(ap=idx[:, b, :], axis=0)
                                            ).then_inc(gathered[b], 16)

                for b in range(2):
                    gather(b, 0)
                def lap(i):
                    for b in range(2):
                        pool.wait_ge(turned[b], i + 1)
                        gather(b, i + 1)
                    for b in range(2):
                        at = pool.value_load(m.table[0:1, bass.ds(TAB * (2 * i + b) + 2, 1)], min_val=0,
                                             max_val=T * TOP_K + T - P)
                        pool.wait_ge(y_store[1 - b], 16 * (i + b))
                        for c in range(2):
                            pool.wait_ge(y_half_ok[c][b], i + 1)
                        pool.dma_start(m.y_dram[bass.ds(at, P), :], y[:, b, :]).then_inc(y_store[b], 16)

                lap(0)
                with pool.Fori(1, n) as i:
                    lap(i)
                for b in range(2):
                    pool.wait_ge(gathered[b], 16 * n + 16)
                    pool.wait_ge(y_store[b], 16 * n)

            @block.tensor
            def _(pe):
                n = laps(pe)

                def turn(b, i):
                    pe.wait_ge(gathered[b], 16 * i + 16)
                    for k in range(KD):
                        mm = pe.transpose(ps_x[:, b, k * P:(k + 1) * P], xg[:, b, k::KD], ident)
                    mm.then_inc(turned[b], 1)

                for b in range(2):
                    turn(b, 0)

                def lap(i):
                    for b in range(2):
                        pe.wait_ge(xT_ok[b], i + 1)
                        pe.wait_ge(gu_in[b], 32 * i + 32)
                        pe.wait_ge(hsT_ok[b], i)
                        for k in range(KD):
                            mm = pe.matmul(ps_gu[:, b, :], xT[:, b, k, :], w_gu[:, b, k, :],
                                           start=(k == 0), stop=(k == KD - 1))
                        mm.then_inc(gu_mm[b], 1)
                    for b in range(2):
                        pe.wait_ge(hs_ok[b], i + 1)
                        for k in range(2):
                            mm = pe.transpose(ps_gu[:, b, k * P:(k + 1) * P], hs[:, b, k * P:(k + 1) * P], ident)
                        mm.then_inc(hs_turned[b], 1)
                        turn(b, i + 1)
                        pe.wait_ge(hsT_ok[b], i + 1)
                        pe.wait_ge(dn_in[b], 16 * i + 16)
                        for c in range(2):
                            pe.wait_ge(y_half_ok[c][1 - b], i + b)
                            for k in range(2):
                                mm = pe.matmul(ps_y[:, c * 512:(c + 1) * 512], hsT[:, b, k * P:(k + 1) * P],
                                               w_dn[:, b, k, c * 512:(c + 1) * 512], start=(k == 0), stop=(k == 1))
                            mm.then_inc(y_mm[b], 1)

                lap(0)
                with pe.Fori(1, n) as i:
                    lap(i)

            @block.scalar
            def _(act):
                n = laps(act)

                def copy_x(b, i):
                    act.wait_ge(turned[b], i + 1)
                    act.activation(xT[:, b].rearrange("p k t -> p (k t)"), ps_x[:, b, :], ACT.Copy
                                   ).then_inc(xT_ok[b], 1)

                for b in range(2):
                    copy_x(b, 0)

                def lap(i):
                    for b in range(2):
                        act.wait_ge(gu_mm[b], i + 1)
                        act.activation(sg[:, b, :], ps_gu[:, b, 0:FF], ACT.Sigmoid).then_inc(sig_ok[b], 1)
                    for b in range(2):
                        act.wait_ge(hs_turned[b], i + 1)
                        act.activation(hsT[:, b, :], ps_gu[:, b, 0:FF], ACT.Copy).then_inc(hsT_ok[b], 1)
                        copy_x(b, i + 1)
                        act.wait_ge(y_mm[b], 2 * i + 2)
                        act.wait_ge(y_store[b], 16 * i)
                        act.activation(y[:, b, 512:D], ps_y[:, 512:D], ACT.Copy).then_inc(y_half_ok[1][b], 1)

                lap(0)
                with act.Fori(1, n) as i:
                    lap(i)

            @block.vector
            def _(dve):
                n = laps(dve)

                def lap(i):
                    for b in range(2):
                        dve.wait_ge(sig_ok[b], i + 1)
                        dve.tensor_mul(hs[:, b, :], sg[:, b, :], ps_gu[:, b, 0:FF]).then_inc(mul_ok[b], 1)
                        dve.wait_ge(mul_ok[b], i + 1)
                        dve.tensor_mul(hs[:, b, :], hs[:, b, :], ps_gu[:, b, FF:]).then_inc(hs_ok[b], 1)
                    for b in range(2):
                        dve.wait_ge(y_mm[b], 2 * i + 1)
                        dve.wait_ge(y_store[b], 16 * i)
                        dve.tensor_copy(y[:, b, 0:512], ps_y[:, 0:512]).then_inc(y_half_ok[0][b], 1)

                lap(0)
                with dve.Fori(1, n) as i:
                    lap(i)


def combine(nc, m):
    RING = 6
    with Tools(nc, "combine") as a:
        rows = a.sb("rows_g", [P, RING, D])
        gate = a.sb("gate_f", [P, 2, D])
        gf = a.sb("g_final_b", [P, D])
        sq, out = a.sb("sq_f", [P, D]), a.sb("out_f", [P, 2, D])
        ss, rms = a.sb("ss_f", [P, NT]), a.sb("rms_f", [P, NT])
        got = a.ring("got", RING)
        vec_in, used, x_ok, ms_ok, sq_ok, rms_ok, out_ok, out_store, chain = a.sems(
            "f_vec_in", "f_used", "f_x_ok", "f_ms_ok", "f_sq_ok", "f_rms_ok", "f_out_ok", "f_out_store", "f_chain")
        with nc.Block() as block:

            @block.sync
            def _(sp):
                for g in range(2):
                    sp.dma_start(gate[:, g, :], m.mod_dram[g, 5:6, :].to_broadcast([P, D])).then_inc(vec_in, 16)
                sp.dma_start(gf[:], m.g_final.unsqueeze(0).to_broadcast([P, D])).then_inc(vec_in, 16)
                for t in range(NT):
                    sp.wait_ge(out_ok, t + 1)
                    if t >= 1:
                        sp.wait_ge(out_store, 16 * t)
                    to = m.y_sample[0, t * P:(t + 1) * P, :] if t < CTX else m.y_prompt[0]
                    sp.dma_start(to, out[:, t % 2, :]).then_inc(out_store, 16)
                sp.wait_ge(out_store, 16 * NT)

            @block.gpsimd
            def _(pool):
                for n in range(NT * TOP_K):
                    t, j = n // TOP_K, n % TOP_K
                    if n >= RING:
                        pool.wait_ge(used, n - RING + 1)
                    pool.indirect_dma_start(rows[:, n % RING, :], None, m.y_dram[0:T * TOP_K, :],
                                            bass.IndirectOffsetOnAxis(ap=m.y_row[:, t, j:j + 1], axis=0)
                                            ).then_inc(got[n % RING], 16)

            @block.scalar
            def _(act):
                for t in range(NT):
                    act.wait_ge(x_ok, t + 1)
                    act.activation(sq[:], m.x[:, t, :], ACT.Square, accum_out=ss[:, t:t + 1]).then_inc(sq_ok, 1)
                    act.wait_ge(ms_ok, t + 1)
                    act.activation(rms[:, t:t + 1], ss[:, t:t + 1], ACT.Sqrt).then_inc(rms_ok, 1)

            @block.vector
            def _(dve):
                ch = Chain(dve, chain)
                dve.wait_ge(vec_in, 48)
                for t in range(NT):
                    acc = m.acc[:, t, :]
                    for j in range(TOP_K):
                        n = t * TOP_K + j
                        dve.wait_ge(got[n % RING], 16 * (n // RING + 1))
                        dve.scalar_tensor_tensor(out=acc, in0=rows[:, n % RING, :], scalar=m.weight[:, t, j:j + 1],
                                                 in1=acc, op0=ALU.mult, op1=ALU.add).then_inc(used, 1)
                        dve.wait_ge(used, n + 1)
                    ch.link(dve.tensor_mul(acc, acc, gate[:, group(t), :]))
                    dve.tensor_add(m.x[:, t, :], m.x[:, t, :], acc).then_inc(x_ok, 1)
                    dve.wait_ge(sq_ok, t + 1)
                    dve.tensor_scalar(ss[:, t:t + 1], ss[:, t:t + 1], 1.0 / D, EPS, ALU.mult, ALU.add
                                      ).then_inc(ms_ok, 1)
                    dve.wait_ge(rms_ok, t + 1)
                    ch.link(dve.reciprocal(rms[:, t:t + 1], rms[:, t:t + 1]))
                    if t >= 2:
                        dve.wait_ge(out_store, 16 * (t - 1))
                    dve.scalar_tensor_tensor(out=out[:, t % 2, :], in0=m.x[:, t, :], scalar=rms[:, t:t + 1],
                                             in1=gf[:], op0=ALU.mult, op1=ALU.mult).then_inc(out_ok, 1)


def trunk_kernel(nc, dram):
    m = Stage()
    m.cond, m.lora, m.vectors, m.w_mix = (
        dram["cond"], dram["lora"], dram["vectors"], dram["w_mix"])
    m.w_merge, m.constants, m.route_constants, m.dft_channel = (
        dram["w_merge"], dram["constants"], dram["route_constants"], dram["dft_channel"])
    m.dft_lat, m.dft_ctx, m.x_prompt, m.x_sample = (
        dram["dft_lat"], dram["dft_ctx"], dram["x_prompt"], dram["x_sample"])
    m.state_rwkv, m.state_gla, m.w_mod, m.b_mod = (
        dram["state_rwkv"], dram["state_gla"], dram["w_mod"], dram["b_mod"])
    m.g_norm_mix, m.g_norm_ffn, m.rw_g_up, m.gla_a_up = (
        dram["g_norm_mix"], dram["g_norm_ffn"], dram["rw_g_up"], dram["gla_a_up"])
    m.w_out, m.w_router, m.b_router, m.we_gate = (
        dram["w_out"], dram["w_router"], dram["b_router"], dram["we_gate"])
    m.we_up, m.we_down, m.ws_gate, m.ws_up = (
        dram["we_up"], dram["we_down"], dram["ws_gate"], dram["ws_up"])
    m.ws_down, m.g_final, m.y_prompt, m.y_sample = (
        dram["ws_down"], dram["g_final"], dram["y_prompt"], dram["y_sample"])
    m.new_rwkv, m.new_gla = (
        dram["new_rwkv"], dram["new_gla"])
    scratch = lambda name, shape, dt=F32: nc.dram_tensor(name, shape, dt, kind="Internal").ap()
    m.mod_dram = scratch("mod_dram", [2, 6, D])
    m.hT_dram = scratch("hT_dram", [P, KD, T])
    m.h2_dram = scratch("h2_dram", [T, D])
    m.list_dram = scratch("list_dram", [N_EXP * T, 1], U32)
    m.tab_dram = scratch("tab_dram", [P, TAB], I32)
    m.y_dram = scratch("y_dram", [T * TOP_K + T, D])
    with Tools(nc, "trunk_kernel") as whole:
        m.const = whole.sb("const", [P, C_END * P])
        m.vec = whole.sb("vec", [P, N_VEC])
        m.zero = whole.sb("zero", [P, 1])
        with ExitStack() as branch_life:
            m.proj = branch_life.enter_context(nc.sbuf_tensor("proj", [P, N_MIX, T], F32, side="right"))
            norm_and_project(nc, m)
            m.branch = branch_life.enter_context(nc.sbuf_tensor("branch", [P, 2 * NB, T], F32, side="right"))
            fourier_and_conv(nc, m)
            rwkv(nc, m)
            gla(nc, m)
            m.merged = whole.sb("merged", [P, KD, T])
            merge_branches(nc, m)
        m.x = whole.sb("x", [P, NT, D])
        m.acc = whole.sb("acc", [P, NT, D])
        m.weight = whole.sb("weight", [P, NT, TOP_K])
        m.y_row = whole.sb("y_row", [P, NT, TOP_K], U32)
        m.laps = whole.sb("laps", [P, 1], I32)
        m.table = whole.sb("table", [1, TAB * P], I32)
        output_and_route(nc, m)
        experts(nc, m)
        combine(nc, m)


def constants():
    i, j = np.meshgrid(np.arange(P), np.arange(P), indexing="ij")
    blocks = [i == j, i // 64 == j // 64, i < j, i > j, i <= j, i >= j]
    for h in LEVELS:
        blocks.append((i // (2 * h) == j // (2 * h)) & (i % (2 * h) < h) & (j % (2 * h) >= h))
    for h in LEVELS:
        blocks.append((i // (2 * h) == j // (2 * h)) & (i % (2 * h) >= h) & (j % (2 * h) < h))
    blocks.append(i >= 0)
    for half in range(2):
        blocks.append(i // 32 == (j + P * half) // 64)
    out = np.concatenate([b.astype(np.float32) for b in blocks], axis=1)
    assert out.shape[1] == C_END * P
    return out


def fourier_constants():
    k = np.arange(64)
    one = np.exp(-2j * np.pi * np.outer(k, k) / 64)
    ch = np.kron(np.eye(2), one)
    channel = np.concatenate([ch.real, -ch.imag], axis=1)
    grid = np.kron(np.exp(-2j * np.pi * np.outer(np.arange(8), np.arange(8)) / 8), one) / np.sqrt(8 * 64 * 64)
    seq = np.exp(-2j * np.pi * np.outer(np.arange(P), np.arange(P)) / P) / np.sqrt(P * 64)
    lat = np.stack([grid.real, grid.imag], axis=0).reshape(2, 4, P, T_LAT).transpose(2, 1, 0, 3)
    ctx = np.stack([seq.real, seq.imag], axis=1)
    f = lambda v: np.ascontiguousarray(v.astype(np.float32))
    return f(channel), f(lat), f(ctx)


def pack_inputs(v):
    w = v["w_in"][0].reshape(P, KD, -1)
    zeros = lambda n: np.zeros((P, KD, n), np.float32)
    cols = lambda a, n: w[:, :, a:a + n]
    mix = np.concatenate([cols(0, 1152), cols(1152, 64), cols(1728, 16), zeros(16), cols(1744, 16), zeros(16),
                          cols(1216, 512), cols(1760, 1024)], axis=2)
    mix = mix.reshape(P, KD, N_MIX, P).transpose(2, 0, 1, 3).reshape(N_MIX, P, KD * P)
    merge = cols(2784, NB * D).reshape(P, KD, NB, KD, P).transpose(3, 2, 0, 1, 4)
    branch = v["w_branch"][0].reshape(NB, 2, P, KD, P).transpose(3, 0, 2, 1, 4)
    merge = np.concatenate([merge, branch], axis=3).reshape(KD * NB, P, (KD + 2) * P)
    col = lambda a: a.reshape(-1, P).T
    vectors = np.concatenate([col(v[n][0]) for n in (
        "rw_w0", "rw_a0", "rw_k_k", "rw_k_a", "rw_r_k", "rw_ln_w", "rw_ln_b", "gla_a_b", "gla_norm", "conv_w")], axis=1)
    cond = np.stack([v["c_ctx"].reshape(P, KD), v["c"].reshape(P, KD)], axis=2)
    lora = np.concatenate([v["rw_w_up"][0].reshape(64, BW), v["rw_a_up"][0].reshape(64, BW)], axis=0)
    c = np.ascontiguousarray
    return {"w_mix": c(mix), "w_merge": c(merge), "vectors": c(vectors), "cond": c(cond), "lora": c(lora)}


def route_constants():
    p = np.arange(P)[:, None]
    return np.concatenate([np.broadcast_to(np.arange(N_EXP), (P, N_EXP)), p, p + P * np.arange(NT)[None]],
                          axis=1).astype(np.float32)


_INS = ["x_prompt", "x_sample", "state_rwkv", "state_gla", "w_mod", "b_mod", "g_norm_mix", "g_norm_ffn",
        "rw_g_up", "gla_a_up", "w_out", "w_router", "b_router", "we_gate", "we_up", "we_down",
        "ws_gate", "ws_up", "ws_down", "g_final"]
_OUTS = [("y_prompt", (1, T_CTX, D)), ("y_sample", (1, T_LAT, D)), ("new_rwkv", (1, 1, 2, 4, 64, 64)),
         ("new_gla", (1, 1, 2, 4, 32, 64))]


def kernel(**inputs):
    import concourse.bacc as bacc
    from concourse.bass_utils import run_bass_kernel_spmd

    v = {name: np.asarray(a) for name, a in inputs.items()}
    arrays = {name: np.ascontiguousarray(v[name]) for name in _INS}
    arrays.update(pack_inputs(v))
    arrays["constants"] = constants()
    arrays["route_constants"] = route_constants()
    arrays["dft_channel"], arrays["dft_lat"], arrays["dft_ctx"] = fourier_constants()
    nc = bacc.Bacc("TRN2", target_bir_lowering=False, num_devices=1)
    dram = {name: nc.dram_tensor(name, a.shape, mybir.dt.from_np(a.dtype), kind="ExternalInput").ap()
            for name, a in arrays.items()}
    for name, shape in _OUTS:
        dram[name] = nc.dram_tensor(name, shape, F32, kind="ExternalOutput").ap()
    trunk_kernel(nc, dram)
    r = run_bass_kernel_spmd(nc, [arrays], core_ids=[0])
    return tuple(r.results[0][name] for name, _ in _OUTS)
```

```python
from contextlib import ExitStack

import numpy as np

import concourse.bass as bass
from concourse import mybir

F32, U32, I32 = mybir.dt.float32, mybir.dt.uint32, mybir.dt.int32
ALU = mybir.AluOpType
ACT = mybir.ActivationFunctionType
AX = mybir.AxisListType

P = 128
D = 1024
KD = D // P
T_LAT, T_CTX = 512, 128
T = T_LAT + T_CTX
NT = T // P
CTX = NT - 1
BW = 256
NB = 4
EPS = 1e-6

(U_, R_, K_, V_, WA, GDGA, GQ, GK, GV, GG, SB_, SC_, SX) = (0, 2, 4, 6, 8, 9, 10, 11, 12, 14, 16, 18, 20)
N_MIX = 22
GA = 64

(W0, A0, KK, KA, RK, LNW, LNB, GAB, GNORM, CONV) = (0, 4, 8, 10, 12, 14, 16, 18, 20, 22)
N_VEC = 28

LEVELS = (1, 2, 4, 8, 16, 32, 64)
(IDENT, HEADS, LT, GT, LE, GE, LEV_F, LEV_B) = (0, 1, 2, 3, 4, 5, 6, 13)
(ONES, GBLK, C_END) = (20, 21, 23)


class Chain:

    def __init__(self, eng, sem):
        self.eng, self.sem, self.base, self.k = eng, sem, 0, 0

    def link(self, ins):
        ins.then_inc(self.sem, 1)
        self.k += 1
        self.eng.wait_ge(self.sem, self.base + self.k)

    def laps(self, n, per):
        return _Laps(self, n, per)


class _Laps:
    def __init__(self, chain, n, per):
        self.chain, self.n, self.per = chain, n, per

    def __enter__(self):
        c = self.chain
        self.start = c.k
        self.fori = c.eng.Fori(0, self.n)
        i = self.fori.__enter__()
        c.base, c.k = i * self.per + self.start, 0
        return i

    def __exit__(self, *e):
        c = self.chain
        if e[0] is None:
            assert c.k == self.per, (c.k, self.per)
        c.base = 0
        c.k = self.start + self.n * self.per if isinstance(self.n, int) else 0
        return self.fori.__exit__(*e)


def flat(ap):
    rest = " ".join("abcd"[:len(ap.shape) - 1])
    return ap.rearrange(f"p {rest} -> p ({rest})")


class Tools:

    def __init__(self, nc, stage=""):
        self.nc, self.stage, self.ctx, self.used = nc, stage, ExitStack(), []

    def __enter__(self):
        return self

    def __exit__(self, *e):
        if e[0] is None and self.used:
            self.nc.clear_and_free_semaphores(self.used)
            self.nc.all_engine_barrier()
        return self.ctx.__exit__(*e)

    def sb(self, name, shape, dt=F32):
        return self.ctx.enter_context(self.nc.sbuf_tensor(name, shape, dt, allow_name_mangling=True))

    def ps(self, name, shape):
        return self.ctx.enter_context(self.nc.psum_tensor(name, shape, F32, allow_name_mangling=True))

    def sem(self, name):
        self.used.append(self.nc.alloc_semaphore(f"{self.stage}_{name}"))
        return self.used[-1]

    def sems(self, *names):
        return [self.sem(n) for n in names]

    def ring(self, name, n):
        return [self.sem(f"{name}{i}") for i in range(n)]


def norm_and_project(nc, m):
    RING = 4
    N_COL = 6 * D // 512
    N_FIRST = 2 * D // 512
    with Tools(nc, "norm_and_project") as a:
        hT = a.sb("hT", [P, KD, T])
        c_act, c_raw = a.sb("c_act", [P, KD, 2]), a.sb("c_raw", [P, KD, 2])
        wmod = a.sb("wmod", [P, RING, KD, 512])
        g_row = a.sb("g_row", [2, 2, D])
        rows = a.sb("mod_rows", [2, 6, D])
        w = a.sb("w_tiles", [P, 2, KD * P])
        mean_sq, rms, rstd = (a.sb(n, [P, NT]) for n in ("mean_sq", "rms", "rstd"))
        mod_c = a.sb("mod_c", [P, 2, KD, 2])
        spare = flat(m.proj[:])
        x = spare[:, 0:NT * D].rearrange("p (t d) -> p t d", t=NT)
        xn = spare[:, NT * D:(NT + 2) * D].rearrange("p (b d) -> p b d", b=2)
        square = spare[:, (NT + 2) * D:(NT + 3) * D]
        ps_mod = a.ps("ps_mod", [2, 2, 512])
        ps_cols = a.ps("ps_cols", [P, 2 * KD * 2])
        ps = a.ps("ps_turn_and_in", [P, 2, 1024])
        (vecs_in, rows_in, const_in, x_in, mod_mm, mod_added, mod_out, hT_out, act_chain, dve_chain, c_ready, ssq_ready,
         rms_ready, rows_ready, cols_mm, xn_ready, xn_turned, hT_ready) = a.sems(
            "vecs_in", "rows_in", "const_in", "x_in", "mod_mm", "mod_added", "mod_out", "hT_out", "act_chain", "dve_chain",
            "c_ready", "ssq_ready", "rms_ready", "rows_ready", "cols_mm", "xn_ready", "xn_turned", "hT_ready")
        wmod_in = a.ring("wmod_in", RING)
        w_in, done, out = a.ring("w_in", 2), a.ring("in_done", 2), a.ring("in_out", 2)
        w_mod = m.w_mod[0].rearrange("(p k) n -> p k n", k=KD)
        with nc.Block() as block:

            @block.sync
            def _(sp):
                def chunk(n):
                    sp.dma_start(wmod[:, n % RING], w_mod[:, :, n * 512:(n + 1) * 512]
                                 ).then_inc(wmod_in[n % RING], 16)

                def tile(i, b):
                    sp.dma_start(w[:, b, :], m.w_mix[bass.ds(i * 2 + b, 1)].rearrange("a p n -> (a p) n")
                                 ).then_inc(w_in[b], 16)

                sp.dma_start(c_raw[:], m.cond).then_inc(vecs_in, 16)
                chunk(0)
                sp.dma_start(flat(rows[:]), m.b_mod.to_broadcast([2, 6 * D])).then_inc(rows_in, 16)
                sp.dma_start(g_row[:, 0, :], m.g_norm_mix.to_broadcast([2, D])).then_inc(rows_in, 16)
                sp.dma_start(g_row[:, 1, :], m.g_norm_ffn.to_broadcast([2, D])).then_inc(rows_in, 16)
                chunk(1)
                sp.dma_start(x[:, 0:CTX, :], m.x_sample[0].rearrange("(t p) d -> p t d", p=P)).then_inc(x_in, 16)
                sp.dma_start(x[:, CTX, :], m.x_prompt[0]).then_inc(x_in, 16)
                chunk(2)
                chunk(3)
                sp.dma_start(m.const[:], m.constants).then_inc(const_in, 16)
                sp.dma_start(m.vec[:], m.vectors).then_inc(const_in, 16)
                for n in range(RING, N_COL):
                    sp.wait_ge(mod_mm, n - RING + 1)
                    chunk(n)
                    if n == N_COL - 2:
                        for b in range(2):
                            tile(0, b)
                sp.wait_ge(hT_ready, NT)
                sp.dma_start(m.hT_dram, hT[:]).then_inc(hT_out, 16)
                sp.wait_ge(rows_ready, 2)
                sp.dma_start(m.mod_dram, rows[:]).then_inc(mod_out, 16)
                with sp.Fori(1, N_MIX // 2) as i:
                    for b in range(2):
                        sp.wait_ge(done[b], i)
                        tile(i, b)
                sp.wait_ge(mod_out, 16)
                sp.wait_ge(hT_out, 16)

            @block.scalar
            def _(act):
                ch = Chain(act, act_chain)
                act.wait_ge(vecs_in, 16)
                act.activation(c_act[:], c_raw[:], ACT.Sigmoid).then_inc(c_ready, 1)
                act.wait_ge(x_in, 32)
                for t in range(NT):
                    ch.link(act.activation(square, x[:, t, :], ACT.Square, accum_out=mean_sq[:, t:t + 1]))
                act.activation(square[:, 0:1], mean_sq[:, 0:1], ACT.Copy).then_inc(ssq_ready, 1)
                act.wait_ge(ssq_ready, 2)
                act.activation(rms[:], mean_sq[:], ACT.Sqrt).then_inc(rms_ready, 1)
                with act.Fori(0, N_MIX // 2) as i:
                    for b in range(2):
                        act.wait_ge(done[b], i + 1)
                        act.activation(m.proj[:, bass.ds(i * 2 + b, 1), :].rearrange("p a t -> p (a t)"),
                                       ps[:, b, 0:T], ACT.Copy).then_inc(out[b], 1)

            @block.vector
            def _(dve):
                ch = Chain(dve, dve_chain)
                flat_rows = flat(rows[:])

                def add(n):
                    dve.wait_ge(mod_mm, n + 1)
                    cut = flat_rows[:, n * 512:(n + 1) * 512]
                    dve.tensor_add(cut, ps_mod[:, n % 2, :], cut).then_inc(mod_added, 1)

                def scaled(r, g):
                    ch.link(dve.tensor_scalar(rows[:, r, :], rows[:, r, :], 1.0, None, ALU.add))
                    dve.tensor_mul(rows[:, r, :], rows[:, r, :], g_row[:, g, :]).then_inc(rows_ready, 1)

                dve.wait_ge(c_ready, 1)
                dve.tensor_mul(c_act[:], c_act[:], c_raw[:]).then_inc(c_ready, 1)
                dve.wait_ge(rows_in, 48)
                dve.wait_ge(ssq_ready, 1)
                dve.tensor_scalar(mean_sq[:], mean_sq[:], 1.0 / D, EPS, ALU.mult, ALU.add).then_inc(ssq_ready, 1)
                dve.wait_ge(rms_ready, 1)
                ch.link(dve.reciprocal(rstd[:], rms[:]))
                for n in range(N_FIRST):
                    add(n)
                dve.wait_ge(mod_added, N_FIRST)
                scaled(1, 0)
                dve.wait_ge(cols_mm, 1)
                ch.link(dve.tensor_copy(mod_c[:].rearrange("p v k g -> p (v k g)"), ps_cols[:]))
                for t in range(NT + 1):
                    if t < NT:
                        if t >= 2:
                            dve.wait_ge(xn_turned, t - 1)
                        dve.tensor_scalar(xn[:, t % 2, :], x[:, t, :], rstd[:, t:t + 1], None, ALU.mult
                                          ).then_inc(xn_ready, 1)
                    if t >= 1:
                        u, g = t - 1, 0 if t - 1 == CTX else 1
                        dve.wait_ge(xn_turned, u + 1)
                        to = hT[:, :, u * P:(u + 1) * P]
                        ch.link(dve.tensor_mul(to, ps[:, u % 2, :].rearrange("p (k t) -> p k t", k=KD),
                                               mod_c[:, 1, :, g:g + 1].to_broadcast([P, KD, P])))
                        dve.tensor_add(to, to, mod_c[:, 0, :, g:g + 1].to_broadcast([P, KD, P])
                                       ).then_inc(hT_ready, 1)
                        add(N_FIRST + u)
                for n in range(N_FIRST + NT, N_COL):
                    add(n)
                dve.wait_ge(mod_added, N_COL)
                scaled(4, 1)

            @block.tensor
            def _(pe):
                def modulation(n):
                    pe.wait_ge(wmod_in[n % RING], 16 * (n // RING + 1))
                    if n >= 2:
                        pe.wait_ge(mod_added, n - 1)
                    for k in range(KD):
                        mm = pe.matmul(ps_mod[:, n % 2, :], c_act[:, k, :], wmod[:, n % RING, k, :],
                                       start=(k == 0), stop=(k == KD - 1))
                    mm.then_inc(mod_mm, 1)

                pe.wait_ge(c_ready, 2)
                for n in range(N_FIRST):
                    modulation(n)
                modulation(N_FIRST)
                pe.wait_ge(rows_ready, 1)
                pe.wait_ge(const_in, 32)
                for v in range(2):
                    for k in range(KD):
                        mm = pe.matmul(ps_cols[:, (v * KD + k) * 2:(v * KD + k) * 2 + 2], rows[:, v, k::KD],
                                       m.const[0:2, 0:2], start=True, stop=True)
                mm.then_inc(cols_mm, 1)
                for t in range(NT):
                    pe.wait_ge(xn_ready, t + 1)
                    if t >= 2:
                        pe.wait_ge(hT_ready, t - 1)
                    for k in range(KD):
                        mm = pe.transpose(ps[:, t % 2, k * P:(k + 1) * P], xn[:, t % 2, k::KD], m.const[:, 0:P])
                    mm.then_inc(xn_turned, 1)
                    modulation(N_FIRST + 1 + t)
                for n in range(N_FIRST + 1 + NT, N_COL):
                    modulation(n)
                pe.wait_ge(hT_ready, NT)

                def lap(i):
                    for b in range(2):
                        pe.wait_ge(w_in[b], 16 * i + 16)
                        pe.wait_ge(out[b], i)
                        for k in range(KD):
                            for lo, hi in ((0, 512), (512, T)):
                                mm = pe.matmul(ps[:, b, lo:hi], w[:, b, k * P:(k + 1) * P], hT[:, k, lo:hi],
                                               start=(k == 0), stop=(k == KD - 1))
                        mm.then_inc(done[b], 1)

                lap(0)
                with pe.Fori(1, N_MIX // 2) as i:
                    lap(i)


def fourier_and_conv(nc, m):
    with Tools(nc, "fourier_and_conv") as a:
        ch_dft = a.sb("ch_dft", [P, 2 * P])
        lat_dft = a.sb("lat_dft", [P, CTX, 2, T_LAT])
        ctx_dft = a.sb("ctx_dft", [P, 2, T_CTX])
        mixed = a.sb("ch_mixed", [P, NT, 2, 2 * P])
        z = a.sb("conv_z", [P, 2, T])
        y = a.sb("conv_y", [P, 2, T])
        ps_ch = a.ps("ps_ch", [P, 2, 512])
        ps_lat = a.ps("ps_lat", [P, 2, 512])
        ps_ctx = a.ps("ps_ctx", [P, 512])
        ch_in, tables_in, ch_mm, ch_out, tok_mm, conv = a.sems("ch_in", "tables_in", "ch_mm", "ch_out", "tok_mm", "conv")
        with nc.Block() as block:

            @block.sync
            def _(sp):
                sp.dma_start(ch_dft[:], m.dft_channel).then_inc(ch_in, 16)
                sp.dma_start(lat_dft[:], m.dft_lat).then_inc(tables_in, 16)
                sp.dma_start(ctx_dft[:], m.dft_ctx).then_inc(tables_in, 16)

            @block.tensor
            def _(pe):
                pe.wait_ge(ch_in, 16)
                for n in range(2 * NT):
                    t, c = n // 2, n % 2
                    if n >= 2:
                        pe.wait_ge(ch_out, n - 1)
                    pe.matmul(ps_ch[:, n % 2, 0:2 * P], m.proj[:, U_ + c, t * P:(t + 1) * P], ch_dft[:],
                              start=True, stop=True).then_inc(ch_mm, 1)
                pe.wait_ge(ch_out, 2 * NT)
                pe.wait_ge(tables_in, 32)
                for c in range(2):
                    for t in range(CTX):
                        for part in range(2):
                            mm = pe.matmul(ps_lat[:, c, :], mixed[:, t, c, part * P:(part + 1) * P],
                                           lat_dft[:, t, part, :], start=(t + part == 0),
                                           stop=(t == CTX - 1 and part == 1))
                    mm.then_inc(tok_mm, 1)
                for c in range(2):
                    for part in range(2):
                        mm = pe.matmul(ps_ctx[:, c * P:(c + 1) * P], mixed[:, CTX, c, part * P:(part + 1) * P],
                                       ctx_dft[:, part, :], start=(part == 0), stop=(part == 1))
                mm.then_inc(tok_mm, 1)

            @block.scalar
            def _(act):
                for n in range(2 * NT):
                    act.wait_ge(ch_mm, n + 1)
                    act.activation(mixed[:, n // 2, n % 2, :], ps_ch[:, n % 2, 0:2 * P], ACT.Copy).then_inc(ch_out, 1)
                for c in range(2):
                    act.wait_ge(tok_mm, c + 1)
                    act.activation(m.branch[:, c, 0:T_LAT], ps_lat[:, c, :], ACT.Copy)
                act.wait_ge(tok_mm, 3)
                act.activation(m.branch[:, 0:2, T_LAT:T], ps_ctx[:, 0:2 * P].rearrange("p (c t) -> p c t", c=2),
                               ACT.Copy)

            @block.vector
            def _(dve):
                ch = Chain(dve, conv)
                ch.link(dve.tensor_mul(z[:], m.proj[:, SC_:SC_ + 2, :], m.proj[:, SX:SX + 2, :]))
                w = lambda tap, c: m.vec[:, CONV + 2 * tap + c:CONV + 2 * tap + c + 1]
                for c in range(2):
                    ch.link(dve.tensor_scalar(y[:, c, :], z[:, c, :], w(1, c), None, ALU.mult))
                for lo, hi in ((0, T_LAT), (T_LAT, T)):
                    for c in range(2):
                        ch.link(dve.scalar_tensor_tensor(
                            out=y[:, c, lo + 1:hi], in0=z[:, c, lo:hi - 1], scalar=w(0, c),
                            in1=y[:, c, lo + 1:hi], op0=ALU.mult, op1=ALU.add))
                        ch.link(dve.scalar_tensor_tensor(
                            out=y[:, c, lo:hi - 1], in0=z[:, c, lo + 1:hi], scalar=w(2, c),
                            in1=y[:, c, lo:hi - 1], op0=ALU.mult, op1=ALU.add))
                dve.tensor_mul(m.branch[:, 6:8, :], y[:], m.proj[:, SB_:SB_ + 2, :])


def head_sum(pe, m, ps, src):
    for c in range(2):
        for lo, hi in ((0, 512), (512, T)):
            mm = pe.matmul(ps[:, c, lo:hi], m.const[:, HEADS * P:(HEADS + 1) * P], src[:, c, lo:hi],
                           start=True, stop=True)
    return mm


def rwkv_prepare(nc, m, r):
    C0 = -float(np.exp(-0.5))
    with Tools(nc, "rwkv_prepare") as a:
        lora = a.sb("lora_w", [P, BW])
        g_up = a.sb("g_up_w", [64, BW])
        keep = a.sb("keep", [P, T])
        kk, rec, sg, ag, L, b, ce, ci = (a.sb(n, [P, 2, T]) for n in ("kk", "rec", "sg", "ag", "L", "b", "ce", "ci"))
        bonus = a.sb("bonus", [P, 2, T])
        half = a.sb("half_tot", [P, 2, NT])
        zw = a.ps("ps_zw", [P, 2, 1024])
        za = a.ps("ps_za", [P, 2, 1024])
        (w_in, keep_set, squashed, sq, sq_mm, nrm, nrm_mul, zw_mm, za_mm, sg_ok, ag_ok, cum, kd_ok, exps, prods,
         bon, bon_mm, g_mm, act_chain, dve_chain) = a.sems(
            "w_in", "keep_set", "squashed", "sq", "sq_mm", "nrm", "nrm_mul", "zw_mm", "za_mm", "sg_ok", "ag_ok",
            "cum", "kd_ok", "exps", "prods", "bon", "bon_mm", "g_mm", "act_chain", "dve_chain")
        tiles = lambda ap: ap.rearrange("p c (t i) -> p c t i", i=P)
        pr = m.proj
        with nc.Block() as block:

            @block.sync
            def _(sp):
                sp.dma_start(lora[:], m.lora).then_inc(w_in, 16)
                sp.dma_start(g_up[:], m.rw_g_up[0]).then_inc(w_in, 16)

            @block.gpsimd
            def _(pool):
                pool.memset(keep[:], 1.0).then_inc(keep_set, 1)
                pool.wait_ge(keep_set, 1)
                pool.memset(keep[:, ::P], 0.0).then_inc(keep_set, 1)

            @block.scalar
            def _(act):
                ch = Chain(act, act_chain)
                act.activation(pr[0:64, WA, :], pr[0:64, WA, :], ACT.Tanh)
                act.activation(pr[0:64, GDGA, :], pr[0:64, GDGA, :], ACT.Sigmoid).then_inc(squashed, 1)
                act.wait_ge(sq_mm, 1)
                act.activation(rec[:], zw[:, :, 0:T], ACT.Sqrt).then_inc(nrm, 1)
                for d in range(2):
                    act.wait_ge(zw_mm, d + 1)
                    for c in range(2):
                        s = act.activation(sg[:, c, :], zw[:, c, 0:T], ACT.Sigmoid,
                                           bias=m.vec[:, W0 + 2 * d + c:W0 + 2 * d + c + 1])
                    s.then_inc(sg_ok, 1)
                    act.wait_ge(za_mm, d + 1)
                    for c in range(2):
                        s = act.activation(ag[:, c, :], za[:, c, 0:T], ACT.Sigmoid,
                                           bias=m.vec[:, A0 + 2 * d + c:A0 + 2 * d + c + 1])
                    s.then_inc(ag_ok, 1)
                    act.wait_ge(cum, d + 1)
                    act.activation(r.mid[d][:], half[:], ACT.Exp)
                    act.activation(L[:], ci[:], ACT.Exp, scale=-1.0)
                    act.activation(b[:], ce[:], ACT.Exp)
                    act.wait_ge(kd_ok, d + 1)
                    act.activation(ag[:], ci[:], ACT.Exp).then_inc(exps, 1)
                    act.wait_ge(prods, d + 1)
                act.wait_ge(g_mm, 1)
                act.wait_ge(prods, 2)
                act.activation(pr[:, K_:K_ + 2, :], za[:, :, 0:T], ACT.Copy)

            @block.vector
            def _(dve):
                ch = Chain(dve, dve_chain)
                dve.wait_ge(keep_set, 2)
                for c in range(2):
                    ch.link(dve.tensor_scalar(kk[:, c, :], pr[:, K_ + c, :], m.vec[:, KK + c:KK + c + 1], None,
                                              ALU.mult))
                dve.tensor_mul(b[:], kk[:], kk[:]).then_inc(sq, 1)
                dve.wait_ge(nrm, 1)
                ch.link(dve.tensor_scalar(rec[:], rec[:], 1e-12, None, ALU.max))
                ch.link(dve.reciprocal(rec[:], rec[:]))
                ch.link(dve.tensor_mul(kk[:], kk[:], rec[:]))
                for d in range(2):
                    dve.wait_ge(sg_ok, d + 1)
                    ch.link(dve.tensor_scalar(L[:], sg[:], C0, None, ALU.mult))
                    for c in range(2):
                        ch.link(dve.tensor_tensor_scan(b[:, c, :], keep[:], L[:, c, :], 0.0, ALU.mult, ALU.add))
                    ch.link(dve.tensor_scalar(half[:], tiles(b[:])[:, :, :, P - 1], 0.5, None, ALU.mult))
                    for c in range(2):
                        mid = half[:, c, :].unsqueeze(2).to_broadcast([P, NT, P])
                        bt = b[:, c, :].rearrange("p (t i) -> p t i", i=P)
                        if d == 0:
                            ch.link(dve.tensor_sub(ci[:, c, :].rearrange("p (t i) -> p t i", i=P), bt, mid))
                        else:
                            ch.link(dve.tensor_sub(ce[:, c, :].rearrange("p (t i) -> p t i", i=P), mid, bt))
                    if d == 0:
                        dve.tensor_sub(ce[:], ci[:], L[:]).then_inc(cum, 1)
                    else:
                        dve.tensor_add(ci[:], ce[:], L[:]).then_inc(cum, 1)
                    dve.wait_ge(ag_ok, d + 1)
                    ch.link(dve.tensor_mul(rec[:], kk[:], ag[:]))
                    for c in range(2):
                        ch.link(dve.tensor_scalar(sg[:, c, :], ag[:, c, :], 1.0, m.vec[:, KA + c:KA + c + 1],
                                                  ALU.subtract, ALU.mult))
                    ch.link(dve.scalar_tensor_tensor(out=sg[:], in0=sg[:], scalar=1.0, in1=pr[:, K_:K_ + 2, :],
                                                     op0=ALU.add, op1=ALU.mult))
                    if d == 0:
                        dve.tensor_copy(bonus[:], sg[:]).then_inc(kd_ok, 1)
                    else:
                        dve.tensor_add(bonus[:], bonus[:], sg[:]).then_inc(kd_ok, 1)
                    dve.wait_ge(exps, d + 1)
                    dve.tensor_mul(r.rt[d][:], pr[:, R_:R_ + 2, :], ag[:])
                    dve.tensor_mul(r.kt[d][:], sg[:], L[:])
                    dve.tensor_mul(r.bt[d][:], rec[:], L[:])
                    ch.link(dve.scalar_tensor_tensor(out=r.at[d][:], in0=kk[:], scalar=-1.0, in1=b[:],
                                                     op0=ALU.mult, op1=ALU.mult))
                    dve.tensor_copy(half[:, 0, 0:1], half[:, 0, 0:1]).then_inc(prods, 1)
                ch.link(dve.tensor_mul(bonus[:], bonus[:], pr[:, R_:R_ + 2, :]))
                for c in range(2):
                    s = dve.tensor_scalar(bonus[:, c, :], bonus[:, c, :], m.vec[:, RK + c:RK + c + 1], None, ALU.mult)
                s.then_inc(bon, 1)
                dve.wait_ge(bon_mm, 1)
                dve.tensor_mul(pr[:, R_:R_ + 2, :], zw[:, :, 0:T], pr[:, V_:V_ + 2, :])

            @block.tensor
            def _(pe):
                pe.wait_ge(sq, 1)
                head_sum(pe, m, zw, b).then_inc(sq_mm, 1)
                pe.wait_ge(w_in, 32)
                pe.wait_ge(squashed, 1)
                pe.wait_ge(nrm, 1)
                for d in range(2):
                    for ps, first, done, free in ((zw, 0, zw_mm, sg_ok), (za, 64, za_mm, ag_ok)):
                        pe.wait_ge(free, d)
                        at = first + 32 * d
                        for c in range(2):
                            for lo, hi in ((0, 512), (512, T)):
                                mm = pe.matmul(ps[:, c, lo:hi], lora[at:at + 32, c * P:(c + 1) * P],
                                               pr[at:at + 32, WA, lo:hi], start=True, stop=True)
                        mm.then_inc(done, 1)
                pe.wait_ge(ag_ok, 2)
                for c in range(2):
                    for lo, hi in ((0, 512), (512, T)):
                        mm = pe.matmul(za[:, c, lo:hi], g_up[:, c * P:(c + 1) * P], pr[0:64, GDGA, lo:hi],
                                       start=True, stop=True)
                mm.then_inc(g_mm, 1)
                pe.wait_ge(bon, 1)
                head_sum(pe, m, zw, bonus).then_inc(bon_mm, 1)


def turn_to_tokens(nc, m, items, name):
    with Tools(nc, f"turn_{name}") as a:
        ps = a.ps("ps_turn", [P, 8, 512])
        turned, out = a.sems(f"{name}_turned", f"{name}_out")
        with nc.Block() as block:

            @block.tensor
            def _(pe):
                for n, (_, src) in enumerate(items):
                    if n >= 8:
                        pe.wait_ge(out, n - 7)
                    pe.transpose(ps[:, n % 8, 0:P], src, m.const[:, 0:P]).then_inc(turned, 1)

            @block.scalar
            def _(act):
                for n, (dst, _) in enumerate(items):
                    act.wait_ge(turned, n + 1)
                    for k, (to, lo, hi) in enumerate(dst):
                        s = act.activation(to, ps[:, n % 8, lo:hi], ACT.Copy)
                    s.then_inc(out, 1)


def rwkv_scan(nc, m, r):
    NL = len(LEVELS) - 1
    H = 4
    tile_of = ((CTX, 0, 1, 2, 3), (CTX, 3, 2, 1, 0))
    cs = lambda n: m.const[:, n * P:(n + 1) * P]
    lev, strict, causal = (LEV_F, LEV_B), (LT, GT), (LE, GE)
    with Tools(nc, "rwkv_scan") as a:
        two = lambda n, shape: [a.sb(f"{n}_{d}", shape) for d in range(2)]
        X, XT, NTm, OFF, Y, MT, QB, QK, Upad = (two(n, [P, H, P]) for n in (
            "X", "XT", "NTm", "OFF", "Y", "MT", "QB", "QK", "Upad"))
        Rsb, Usb = two("Rsb", [P, BW]), two("Usb", [P, BW])
        S, Sc, S0, Snat = two("S", [P, 2, P]), two("Sc", [P, 2, P]), two("S0", [P, 2, P]), two("Snat", [P, 2, P])
        ps = [a.ps(f"ps_scan{d}", [P, 4, 512]) for d in range(2)]
        sem2 = lambda n: [a.sem(f"{n}_{d}") for d in range(2)]
        (sc_mm, m_mm, q_mm, Y_mm, dX_mm, R_mm, U_mm, S_mm, y_mm, x_set, m_set, q_set, X_upd, u_set, sc_set,
         Y_out, R_out, u_out, y_out, eye, off, S0_mm, S0_out, fin_mm, fin_out) = (sem2(n) for n in (
            "sc_mm", "m_mm", "q_mm", "Y_mm", "dX_mm", "R_mm", "U_mm", "S_mm", "y_mm", "x_set", "m_set", "q_set",
            "X_upd", "u_set", "sc_set", "Y_out", "R_out", "u_out", "y_out", "eye", "off", "S0_mm", "S0_out",
            "fin_mm", "fin_out"))
        zeroed, states_in, states_out, dve_chain = a.sems("zeroed", "states_in", "states_out", "dve_chain")
        split = lambda ap: ap.rearrange("p (hh par) t -> p par hh t", par=2)
        bank2 = lambda d, first, half: ps[d][:, first:first + 2, half * 256:half * 256 + 256].rearrange(
            "p b (hh t) -> p b hh t", hh=2)
        full = lambda d, b: ps[d][:, b, :].rearrange("p (h t) -> p h t", h=H)
        pair = lambda d, b, half=0: ps[d][:, b, half * 256:half * 256 + 256].rearrange("p (c v) -> p c v", c=2)
        many = lambda mask: mask.bitcast(U32).unsqueeze(1).unsqueeze(1).to_broadcast([P, 2, 2, P])
        with nc.Block() as block:

            @block.sync
            def _(sp):
                sp.wait_ge(zeroed, 1)
                for d in range(2):
                    for par in range(2):
                        sp.dma_start(Snat[d][64 * par:64 * par + 64, :, 64 * par:64 * par + 64],
                                     m.state_rwkv[0, 0, d, par::2].rearrange("h v k -> v h k")
                                     ).then_inc(states_in, 16)
                for d in range(2):
                    sp.wait_ge(fin_out[d], 1)
                    for par in range(2):
                        sp.dma_start(m.new_rwkv[0, 0, d, par::2].rearrange("h v k -> v h k"),
                                     Snat[d][64 * par:64 * par + 64, :, 64 * par:64 * par + 64]
                                     ).then_inc(states_out, 16)
                sp.wait_ge(states_out, 64)

            @block.gpsimd
            def _(pool):
                for d in range(2):
                    for t in (Snat, NTm, MT, QB, QK, Upad, Sc):
                        z = pool.memset(t[d][:], 0.0)
                z.then_inc(zeroed, 1)
                for s in range(NT):
                    for d in range(2):
                        pool.wait_ge(U_mm[d], s)
                        for t in (X, XT):
                            z = pool.tensor_copy(t[d][:], cs(IDENT).unsqueeze(1).to_broadcast([P, H, P]))
                        z.then_inc(eye[d], 1)
                    for li in range(1, NL + 1):
                        for d in range(2):
                            pool.wait_ge(x_set[d], s + 1)
                            pool.wait_ge(Y_mm[d], NL * s + li - 1)
                            pool.tensor_mul(OFF[d][:], NTm[d][:],
                                            cs(lev[d] + li).unsqueeze(1).to_broadcast([P, H, P])
                                            ).then_inc(off[d], 1)

            @block.tensor
            def _(pe):
                def head(d, arr, h, t):
                    lo = 64 * (h % 2)
                    return arr[d][lo:lo + 64, h // 2, t * P:(t + 1) * P]

                def scores(d, bank, half, lhs, rhs, t):
                    for h in range(H):
                        at = half * 256 + (h // 2) * P
                        mm = pe.matmul(ps[d][:, bank + h % 2, at:at + P], head(d, lhs, h, t), head(d, rhs, h, t),
                                       start=True, stop=True)
                    return mm

                pe.wait_ge(states_in, 64)
                for d in range(2):
                    for c in range(2):
                        mm = pe.transpose(ps[d][:, 3, c * P:(c + 1) * P], Snat[d][:, c, :], cs(IDENT))
                    mm.then_inc(S0_mm[d], 1)
                for s in range(NT):
                    for d in range(2):
                        t = tile_of[d][s]
                        pe.wait_ge(sc_set[d], s + 1)
                        pe.wait_ge(y_out[d], s)
                        scores(d, 0, 0, r.at, r.bt, t)
                        scores(d, 0, 1, r.bt, r.at, t).then_inc(sc_mm[d], 1)
                        pe.wait_ge(X_upd[d], NL * s)
                        pe.wait_ge(S0_out[d], 1)
                        pe.wait_ge(u_out[d], s)
                        pe.wait_ge(u_set[d], s)
                        scores(d, 2, 0, r.kt, r.at, t)
                        scores(d, 2, 1, r.bt, r.rt, t).then_inc(m_mm[d], 1)
                    for d in range(2):
                        pe.wait_ge(x_set[d], s + 1)
                        scores(d, 0, 0, r.kt, r.rt, tile_of[d][s]).then_inc(q_mm[d], 1)
                    for li in range(1, NL + 1):
                        n = NL * s + li
                        for d in range(2):
                            pe.wait_ge(off[d], n)
                            if li == 1:
                                pe.wait_ge(q_set[d], s + 1)
                            else:
                                pe.wait_ge(X_upd[d], n - 1)
                            for h in range(H):
                                mm = pe.matmul(full(d, 0)[:, h, :], OFF[d][:, h, :], X[d][:, h, :],
                                               start=True, stop=True)
                            mm.then_inc(Y_mm[d], 1)
                        for d in range(2):
                            pe.wait_ge(Y_out[d], n)
                            if li == 1:
                                pe.wait_ge(m_set[d], s + 1)
                            if li < NL:
                                for h in range(H):
                                    pe.matmul(full(d, 1)[:, h, :], XT[d][:, h, :], Y[d][:, h, :],
                                              start=True, stop=True)
                            for h in range(H):
                                mm = pe.matmul(full(d, 2)[:, h, :], Y[d][:, h, :], XT[d][:, h, :],
                                               start=True, stop=True)
                            mm.then_inc(dX_mm[d], 1)
                    for d in range(2):
                        t = tile_of[d][s]
                        for c in range(2):
                            for h in (2 * c, 2 * c + 1):
                                pe.matmul(ps[d][:, 3, 64 * h:64 * h + 64], MT[d][:, h, :],
                                          r.vtok[:, t, 64 * h:64 * h + 64], start=(h % 2 == 0), stop=False)
                            mm = pe.matmul(pair(d, 3)[:, c, :], r.at[d][:, c, t * P:(t + 1) * P], Sc[d][:, c, :],
                                           start=False, stop=True)
                        mm.then_inc(R_mm[d], 1)
                    for d in range(2):
                        pe.wait_ge(R_out[d], s + 1)
                        pe.wait_ge(X_upd[d], NL * s + NL)
                        for h in range(H):
                            mm = pe.matmul(ps[d][:, 3, 256 + 64 * h:320 + 64 * h], XT[d][:, h, :],
                                           Rsb[d][:, 64 * h:64 * h + 64], start=True, stop=True)
                        mm.then_inc(U_mm[d], 1)
                    for d in range(2):
                        t = tile_of[d][s]
                        pe.wait_ge(u_out[d], s + 1)
                        for c in range(2):
                            cols = slice(c * P, (c + 1) * P)
                            pe.matmul(pair(d, 0)[:, c, :], r.btok[d][:, t, cols], Usb[d][:, cols],
                                      start=True, stop=False)
                            mm = pe.matmul(pair(d, 0)[:, c, :], r.ktok[d][:, t, cols], r.vtok[:, t, cols],
                                           start=False, stop=True)
                        mm.then_inc(S_mm[d], 1)
                        pe.wait_ge(u_set[d], s + 1)
                        for c in range(2):
                            out = pair(d, 1)[:, c, :]
                            pe.matmul(out, Sc[d][:, c, :], r.rt[d][:, c, t * P:(t + 1) * P], start=True, stop=False)
                            for h in (2 * c, 2 * c + 1):
                                pe.matmul(out, r.vpad[:, t, h, :], QK[d][:, h, :], start=False, stop=False)
                                mm = pe.matmul(out, Upad[d][:, h, :], QB[d][:, h, :], start=False,
                                               stop=(h % 2 == 1))
                        mm.then_inc(y_mm[d], 1)
                for d in range(2):
                    for c in range(2):
                        mm = pe.transpose(ps[d][:, 3, c * P:(c + 1) * P], S[d][:, c, :], cs(IDENT))
                    mm.then_inc(fin_mm[d], 1)

            @block.scalar
            def _(act):
                for d in range(2):
                    act.wait_ge(S0_mm[d], 1)
                    act.activation(S0[d][:], pair(d, 3), ACT.Copy).then_inc(S0_out[d], 1)
                for s in range(NT):
                    for li in range(1, NL + 1):
                        for d in range(2):
                            act.wait_ge(Y_mm[d], NL * s + li)
                            act.wait_ge(dX_mm[d], NL * s + li - 1)
                            act.activation(Y[d][:], full(d, 0), ACT.Copy).then_inc(Y_out[d], 1)
                    for d in range(2):
                        act.wait_ge(R_mm[d], s + 1)
                        act.activation(Rsb[d][:], ps[d][:, 3, 0:BW], ACT.Copy).then_inc(R_out[d], 1)
                    for d in range(2):
                        act.wait_ge(U_mm[d], s + 1)
                        act.wait_ge(u_set[d], s)
                        act.activation(Usb[d][:], ps[d][:, 3, BW:2 * BW], ACT.Copy).then_inc(u_out[d], 1)
                    for d in range(2):
                        t = tile_of[d][s]
                        act.wait_ge(y_mm[d], s + 1)
                        act.activation(r.y[d][:, :, t * P:(t + 1) * P], pair(d, 1), ACT.Copy).then_inc(y_out[d], 1)
                for d in range(2):
                    act.wait_ge(fin_mm[d], 1)
                    act.activation(Snat[d][:], pair(d, 3), ACT.Copy).then_inc(fin_out[d], 1)

            @block.vector
            def _(dve):
                ch = Chain(dve, dve_chain)
                dve.wait_ge(zeroed, 1)
                for d in range(2):
                    dve.tensor_copy(S[d][:, 0, 0:1], cs(ONES)[:, 0:1]).then_inc(sc_set[d], 1)
                for s in range(NT):
                    for d in range(2):
                        dve.wait_ge(sc_mm[d], s + 1)
                        dve.wait_ge(eye[d], s + 1)
                        dve.wait_ge(off[d], NL * s)
                        dve.copy_predicated(split(X[d][:]), many(cs(lev[1 - d])), bank2(d, 0, 0))
                        dve.copy_predicated(split(XT[d][:]), many(cs(lev[d])), bank2(d, 0, 1))
                        dve.copy_predicated(split(NTm[d][:]), many(cs(strict[d])), bank2(d, 0, 1)
                                            ).then_inc(x_set[d], 1)
                        dve.wait_ge(m_mm[d], s + 1)
                        dve.wait_ge(y_mm[d], s)
                        dve.copy_predicated(split(MT[d][:]), many(cs(strict[d])), bank2(d, 2, 0))
                        dve.copy_predicated(split(QB[d][:]), many(cs(causal[d])), bank2(d, 2, 1)
                                            ).then_inc(m_set[d], 1)
                    for d in range(2):
                        dve.wait_ge(q_mm[d], s + 1)
                        dve.copy_predicated(split(QK[d][:]), many(cs(causal[d])), bank2(d, 0, 0)
                                            ).then_inc(q_set[d], 1)
                    for li in range(1, NL + 1):
                        for d in range(2):
                            dve.wait_ge(dX_mm[d], NL * s + li)
                            if li < NL:
                                dve.tensor_add(X[d][:], full(d, 1), X[d][:])
                            dve.tensor_add(XT[d][:], full(d, 2), XT[d][:]).then_inc(X_upd[d], 1)
                    for d in range(2):
                        dve.wait_ge(u_out[d], s + 1)
                        for par in range(2):
                            u = dve.tensor_copy(
                                Upad[d][:, par::2, 64 * par:64 * par + 64],
                                Usb[d][:].rearrange("p (hh par v) -> p par hh v", hh=2, par=2)[:, par])
                        u.then_inc(u_set[d], 1)
                    for d in range(2):
                        dve.wait_ge(S_mm[d], s + 1)
                        dve.wait_ge(y_mm[d], s + 1)
                        t = tile_of[d][s]
                        wide = lambda t: r.mid[d][:, :, t:t + 1].to_broadcast([P, 2, P])
                        ch.link(dve.tensor_mul(S0[d][:] if s else S[d][:], pair(d, 0),
                                               cs(HEADS).unsqueeze(1).to_broadcast([P, 2, P])))
                        if s == 0:
                            ch.link(dve.tensor_mul(S[d][:], S[d][:], wide(t)))
                            dve.wait_ge(S0_out[d], 1)
                            dve.tensor_mul(Sc[d][:], S0[d][:], wide(tile_of[d][1])).then_inc(sc_set[d], 1)
                        elif s < NT - 1:
                            ch.link(dve.tensor_add(Sc[d][:], Sc[d][:], S0[d][:]))
                            ch.link(dve.tensor_mul(Sc[d][:], Sc[d][:], wide(t)))
                            dve.tensor_mul(Sc[d][:], Sc[d][:], wide(tile_of[d][s + 1])).then_inc(sc_set[d], 1)


def rwkv_finish(nc, m, r):
    with Tools(nc, "rwkv_finish") as a:
        y, y2 = a.sb("y_sum", [P, 2, T]), a.sb("y_sq", [P, 2, T])
        ps = a.ps("ps_mean", [P, 2, 1024])
        ready, mm_s, rms, chain = a.sems("fin_ready", "fin_sum", "fin_rms", "fin_chain")
        with nc.Block() as block:

            @block.tensor
            def _(pe):
                pe.wait_ge(ready, 1)
                head_sum(pe, m, ps, y).then_inc(mm_s, 1)
                pe.wait_ge(ready, 2)
                head_sum(pe, m, ps, y2).then_inc(mm_s, 1)

            @block.scalar
            def _(act):
                act.wait_ge(ready, 3)
                act.activation(y2[:], y2[:], ACT.Sqrt).then_inc(rms, 1)

            @block.vector
            def _(dve):
                ch = Chain(dve, chain)
                dve.tensor_add(y[:], r.y[0][:], r.y[1][:]).then_inc(ready, 1)
                dve.wait_ge(mm_s, 1)
                dve.wait_ge(ready, 1)
                ch.link(dve.scalar_tensor_tensor(out=y[:], in0=ps[:, :, 0:T], scalar=-1.0 / 64, in1=y[:],
                                                 op0=ALU.mult, op1=ALU.add))
                dve.tensor_mul(y2[:], y[:], y[:]).then_inc(ready, 1)
                dve.wait_ge(mm_s, 2)
                dve.tensor_scalar(y2[:], ps[:, :, 0:T], 1.0 / 64, 64e-5, ALU.mult, ALU.add).then_inc(ready, 1)
                dve.wait_ge(rms, 1)
                ch.link(dve.reciprocal(y2[:], y2[:]))
                ch.link(dve.tensor_mul(y[:], y[:], y2[:]))
                for c in range(2):
                    ch.link(dve.tensor_scalar(y[:, c, :], y[:, c, :], m.vec[:, LNW + c:LNW + c + 1],
                                              m.vec[:, LNB + c:LNB + c + 1], ALU.mult, ALU.add))
                ch.link(dve.tensor_add(y[:], y[:], m.proj[:, R_:R_ + 2, :]))
                dve.tensor_mul(m.branch[:, 2:4, :], y[:], m.proj[:, K_:K_ + 2, :])


def rwkv(nc, m):
    spare = lambda lo, n: m.proj[:, lo:lo + n, :].rearrange("p a t -> p (a t)")
    with Tools(nc, "rwkv") as a:
        two = lambda n, shape: [a.sb(f"{n}{d}", shape) for d in range(2)]
        r = Stage()
        r.rt, r.kt, r.at, r.bt = (two(n, [P, 2, T]) for n in ("rt", "kt", "at", "bt"))
        r.mid = two("mid", [P, 2, NT])
        rwkv_prepare(nc, m, r)
        r.vtok = a.sb("vtok", [P, NT, BW])
        r.vpad = a.sb("vpad", [P, NT, 4, P])
        tok = lambda ap: ap.rearrange("p (t n) -> p t n", t=NT)
        r.ktok = [tok(spare(SB_, 2)), tok(spare(SC_, 2))]
        r.btok = [tok(spare(SX, 2)), tok(spare(U_, 2))]
        r.y = [m.branch[:, 2:4, :], m.branch[:, 4:6, :]]
        zero_pads(nc, a, r.vpad)
        items = []
        for t in range(NT):
            cut = slice(t * P, (t + 1) * P)
            for c in range(2):
                cols = slice(c * P, (c + 1) * P)
                items.append(([(r.vtok[:, t, cols], 0, P), (r.vpad[:, t, 2 * c, 0:64], 0, 64),
                               (r.vpad[:, t, 2 * c + 1, 64:P], 64, P)], m.proj[:, V_ + c, cut]))
                for d in range(2):
                    items.append(([(r.ktok[d][:, t, cols], 0, P)], r.kt[d][:, c, cut]))
                    items.append(([(r.btok[d][:, t, cols], 0, P)], r.bt[d][:, c, cut]))
        turn_to_tokens(nc, m, items, "rwkv")
        rwkv_scan(nc, m, r)
    with Tools(nc, "rwkv_end") as a:
        rwkv_finish(nc, m, r)


class Stage:
    pass


def zero_pads(nc, a, pad):
    cleared = a.sem("pads_cleared")
    with nc.Block() as block:

        @block.gpsimd
        def _(pool):
            pool.memset(pad[:], 0.0).then_inc(cleared, 1)
            pool.wait_ge(cleared, 1)


def gla_prepare(nc, m, r):
    with Tools(nc, "gla_prepare") as a:
        up = a.sb("gla_up", [P, P])
        keep = a.sb("gkeep", [P, T])
        x, l, b, tail, e1, e2 = (a.sb(f"g_{n}", [P, T]) for n in ("x", "l", "b", "tail", "e1", "e2"))
        ps = a.ps("ps_gate", [P, 2, 1024])
        w_in, keep_set, up_mm, soft, cum, exps, prods, act_chain, dve_chain = a.sems(
            "gw_in", "gkeep_set", "gup_mm", "gsoft", "gcum", "gexps", "gprods", "gact_chain", "gdve_chain")
        tiles = lambda ap: ap.rearrange("p (t i) -> p t i", i=P)
        with nc.Block() as block:

            @block.sync
            def _(sp):
                for d in range(2):
                    lo = GA + 32 * d
                    sp.dma_start(up[lo:lo + 16, :], m.gla_a_up[0, d]).then_inc(w_in, 16)

            @block.gpsimd
            def _(pool):
                pool.memset(keep[:], 1.0).then_inc(keep_set, 1)
                pool.wait_ge(keep_set, 1)
                pool.memset(keep[:, ::P], 0.0).then_inc(keep_set, 1)

            @block.tensor
            def _(pe):
                pe.wait_ge(w_in, 32)
                for d in range(2):
                    rows = slice(GA + 32 * d, GA + 32 * d + 16)
                    for lo, hi in ((0, 512), (512, T)):
                        mm = pe.matmul(ps[:, d, lo:hi], up[rows, :], m.proj[rows, GDGA, lo:hi], start=True, stop=True)
                    mm.then_inc(up_mm, 1)

            @block.scalar
            def _(act):
                ch = Chain(act, act_chain)
                for d in range(2):
                    act.wait_ge(up_mm, d + 1)
                    act.wait_ge(prods, d)
                    ch.link(act.activation(x[:], ps[:, d, 0:T], ACT.Identity, bias=m.vec[:, GAB + d:GAB + d + 1]))
                    ch.link(act.activation(l[:], x[:], ACT.Abs))
                    ch.link(act.activation(l[:], l[:], ACT.Exp, scale=-1.0))
                    act.activation(l[:], l[:], ACT.Ln, bias=1.0).then_inc(soft, 1)
                    act.wait_ge(cum, d + 1)
                    act.activation(e1[:], r.cum[d][:], ACT.Exp)
                    act.activation(r.end[d][:], r.end[d][:], ACT.Exp)
                    act.activation(e2[:], tail[:], ACT.Exp).then_inc(exps, 1)

            @block.vector
            def _(dve):
                ch = Chain(dve, dve_chain)
                dve.wait_ge(keep_set, 2)
                ch.link(dve.tensor_scalar(r.q[:], m.proj[:, GQ, :], 32.0 ** -0.5, None, ALU.mult))
                for d in range(2):
                    dve.wait_ge(soft, d + 1)
                    ch.link(dve.scalar_tensor_tensor(out=x[:], in0=x[:], scalar=0.0, in1=l[:], op0=ALU.min,
                                                     op1=ALU.subtract))
                    ch.link(dve.tensor_scalar(x[:], x[:], 1.0 / 16.0, None, ALU.mult))
                    ch.link(dve.tensor_tensor_scan(b[:], keep[:], x[:], 0.0, ALU.mult, ALU.add))
                    ch.link(dve.tensor_copy(r.end[d][:], tiles(b[:])[:, :, P - 1]))
                    whole = tiles(b[:])[:, :, P - 1:P].to_broadcast([P, NT, P])
                    if d == 0:
                        ch.link(dve.tensor_copy(r.cum[0][:], b[:]))
                        dve.tensor_sub(tiles(tail[:]), whole, tiles(b[:])).then_inc(cum, 1)
                    else:
                        ch.link(dve.tensor_sub(tail[:], b[:], x[:]))
                        dve.tensor_sub(tiles(r.cum[1][:]), whole, tiles(tail[:])).then_inc(cum, 1)
                    dve.wait_ge(exps, d + 1)
                    dve.tensor_mul(r.qd[d][:], r.q[:], e1[:])
                    dve.tensor_mul(r.kd[d][:], m.proj[:, GK, :], e2[:]).then_inc(prods, 1)


def gla_scores(nc, m, r):
    H, HP = 4, P // 2
    cs = lambda n: m.const[:, n * P:(n + 1) * P]
    top = len(LEVELS) - 1
    rounds = [(None, half, (0, 1)) for half in range(2)] + [
        (li, 1 - d, (d,)) for li in range(len(LEVELS)) for d in range(2)]
    NR, BUF = len(rounds), 3
    width = lambda n: LEVELS[top if rounds[n][0] is None else rounds[n][0]]
    asks = lambda ap, n: ap.rearrange("p (n two w) -> p n two w", two=2, w=width(n))[:, :, rounds[n][1], :]
    with Tools(nc, "gla_scores") as a:
        ring = lambda n: [a.sb(f"{n}_{b}", [P, T]) for b in range(BUF)]
        diff, kl = ring("diff"), ring("kl")
        ql = [a.sb(f"ql_{b}", [P, NT, H, HP]) for b in range(BUF)]
        ps = a.ps("ps_gsc", [P, 2, 4, 512])
        zeroed, from_mid, decay, ql_ok, kl_ok, sc_mm, copied, act_chain = a.sems(
            "gzeroed", "from_mid", "gdecay", "ql_ok", "kl_ok", "gsc_mm", "gcopied", "gs_act")
        with nc.Block() as block:

            @block.gpsimd
            def _(pool):
                for t in ql + r.sc:
                    z = pool.memset(t[:], 0.0)
                z.then_inc(zeroed, 1)
                for n in range(2, NR):
                    pool.wait_ge(decay, n - 1)
                    if n >= 2 + BUF:
                        pool.wait_ge(sc_mm, n - BUF + 1)
                    pool.tensor_mul(kl[n % BUF][:], m.proj[:, GK, :], diff[n % BUF][:]).then_inc(kl_ok, 1)

            @block.scalar
            def _(act):
                ch = Chain(act, act_chain)
                for n in range(2, NR):
                    act.wait_ge(from_mid, n - 1)
                    ch.link(act.activation(diff[n % BUF][:], diff[n % BUF][:], ACT.Abs))
                    act.activation(diff[n % BUF][:], diff[n % BUF][:], ACT.Exp, scale=-1.0).then_inc(decay, 1)

            @block.vector
            def _(dve):
                def start(n):
                    w, d = width(n), rounds[n][2][0]
                    if n >= 2 + BUF:
                        dve.wait_ge(ql_ok, n - BUF + 1)
                        dve.wait_ge(kl_ok, n - BUF - 1)
                    c = r.cum[d][:].rearrange("p (n w) -> p n w", w=2 * w)
                    at = w - 1 if d == 0 else w
                    dve.tensor_sub(diff[n % BUF][:].rearrange("p (n w) -> p n w", w=2 * w), c,
                                   c[:, :, at:at + 1].to_broadcast([P, T // (2 * w), 2 * w])).then_inc(from_mid, 1)

                def query(n):
                    if n >= 2:
                        dve.wait_ge(decay, n - 1)
                    if n >= BUF:
                        dve.wait_ge(sc_mm, n - BUF + 1)
                    for h in range(H):
                        rows = slice(32 * h, 32 * h + 32)
                        w = width(n)
                        to = ql[n % BUF][rows, :, h, :].rearrange("p t (n w) -> p t n w", w=w)
                        tiles = lambda ap: ap.rearrange("p (t n) w -> p t n w", t=NT)
                        if n < 2:
                            q = dve.tensor_copy(to, tiles(asks(r.q[rows], n)))
                        else:
                            q = dve.tensor_mul(to, tiles(asks(r.q[rows], n)), tiles(asks(diff[n % BUF][rows], n)))
                    q.then_inc(ql_ok, 1)

                def copy(n):
                    li, half, dirs = rounds[n]
                    w = width(n)
                    dve.wait_ge(sc_mm, n + 1)
                    if n >= 1:
                        dve.wait_ge(copied, n)
                    for d in dirs:
                        mask = asks(cs(IDENT if li is None else (LEV_F, LEV_B)[d] + li).bitcast(U32), n)
                        c = dve.copy_predicated(
                            asks(flat(r.sc[d][:]), n).rearrange("p (t n) w -> p t n w", t=NT * H),
                            mask.unsqueeze(1).to_broadcast([P, NT * H, HP // w, w]),
                            flat(ps[:, n % 2])[:, 0:NT * H * HP].rearrange("p (t n w) -> p t n w", n=HP // w, w=w))
                    c.then_inc(copied, 1)

                dve.wait_ge(zeroed, 1)
                query(0)
                query(1)
                for n in range(2, 2 + BUF):
                    start(n)
                for n in range(NR):
                    if n + 2 < NR:
                        query(n + 2)
                    if 2 + BUF <= n + BUF < NR:
                        start(n + BUF)
                    copy(n)

            @block.tensor
            def _(pe):
                for n in range(NR):
                    pe.wait_ge(ql_ok, n + 1)
                    if n >= 2:
                        pe.wait_ge(kl_ok, n - 1)
                        pe.wait_ge(copied, n - 1)
                    for t in range(NT):
                        cut = slice(t * P, (t + 1) * P)
                        keys = m.proj[:, GK, cut] if n < 2 else kl[n % BUF][:, cut]
                        mm = pe.matmul(flat(ps[:, n % 2])[:, t * H * HP:(t + 1) * H * HP], keys,
                                       ql[n % BUF][:, t].rearrange("p h i -> p (h i)"), start=True, stop=True)
                    mm.then_inc(sc_mm, 1)


def gla_scan(nc, m, r):
    tile_of = ((CTX, 0, 1, 2, 3), (CTX, 3, 2, 1, 0))
    with Tools(nc, "gla_scan") as a:
        two = lambda n, shape: [a.sb(f"{n}_{d}", shape) for d in range(2)]
        S, Sfin, inc = two("gS", [P, BW]), two("gSfin", [P, BW]), two("ginc", [P, BW])
        S0 = two("gS0", [P, BW])
        ps_o = [a.ps(f"ps_go{d}", [P, 2, P]) for d in range(2)]
        ps_S = [a.ps(f"ps_gS{d}", [P, BW]) for d in range(2)]
        sem2 = lambda n: [a.sem(f"{n}_{d}") for d in range(2)]
        o_mm, S_mm, S_set, o_out, ctx_ok = (sem2(n) for n in ("go_mm", "gS_mm", "gS_set", "go_out", "gctx"))
        zeroed, states_in, states_out, hT_in, chain = a.sems(
            "gs_zeroed", "gstates_in", "gstates_out", "hT_in", "gs_chain")
        mask = m.const[:, GBLK * P:(GBLK + 2) * P]
        with nc.Block() as block:

            @block.sync
            def _(sp):
                sp.wait_ge(zeroed, 1)
                for d in range(2):
                    for h in range(4):
                        sp.dma_start(S0[d][32 * h:32 * h + 32, 64 * h:64 * h + 64], m.state_gla[0, 0, d, h]
                                     ).then_inc(states_in, 16)
                sp.dma_start(m.hT_back[:], m.hT_dram).then_inc(hT_in, 16)
                for d in range(2):
                    sp.wait_ge(ctx_ok[d], 1)
                    for h in range(4):
                        sp.dma_start(m.new_gla[0, 0, d, h], Sfin[d][32 * h:32 * h + 32, 64 * h:64 * h + 64]
                                     ).then_inc(states_out, 16)
                sp.wait_ge(hT_in, 16)
                sp.wait_ge(states_out, 128)

            @block.gpsimd
            def _(pool):
                for d in range(2):
                    z = pool.memset(S0[d][:], 0.0)
                z.then_inc(zeroed, 1)

            @block.tensor
            def _(pe):
                for s in range(NT):
                    for d in range(2):
                        t = tile_of[d][s]
                        if s:
                            pe.wait_ge(S_set[d], s)
                        pe.matmul(ps_S[d][:], r.kdtok[d][:, t, :], r.vtok[:, t, :], start=True, stop=True
                                  ).then_inc(S_mm[d], 1)
                        pe.wait_ge(o_out[d], s)
                        for c in range(2):
                            if s:
                                pe.matmul(ps_o[d][:, c, :], S[d][:, c * P:(c + 1) * P],
                                          r.qd[d][:, t * P:(t + 1) * P], start=True, stop=False)
                            for h in (2 * c, 2 * c + 1):
                                mm = pe.matmul(ps_o[d][:, c, :], r.vpad[:, t, h, :], r.sc[d][:, t, h, :],
                                               start=(s == 0 and h % 2 == 0), stop=(h % 2 == 1))
                        mm.then_inc(o_mm[d], 1)

            @block.scalar
            def _(act):
                for s in range(NT):
                    for d in range(2):
                        t = tile_of[d][s]
                        act.wait_ge(o_mm[d], s + 1)
                        act.activation(r.o[d][:, :, t * P:(t + 1) * P], ps_o[d][:], ACT.Copy).then_inc(o_out[d], 1)

            @block.vector
            def _(dve):
                ch = Chain(dve, chain)
                for s in range(NT - 1):
                    for d in range(2):
                        t = tile_of[d][s]
                        dve.wait_ge(S_mm[d], s + 1)
                        if s == 0:
                            dve.tensor_mul(Sfin[d][:], ps_S[d][:], mask).then_inc(ctx_ok[d], 1)
                            dve.wait_ge(states_in, 128)
                            dve.tensor_copy(S[d][:], S0[d][:]).then_inc(S_set[d], 1)
                        else:
                            ch.link(dve.tensor_mul(inc[d][:], ps_S[d][:], mask))
                            dve.wait_ge(o_mm[d], s + 1)
                            dve.scalar_tensor_tensor(out=S[d][:], in0=S[d][:], scalar=r.end[d][:, t:t + 1],
                                                     in1=inc[d][:], op0=ALU.mult, op1=ALU.add
                                                     ).then_inc(S_set[d], 1)


def gla_finish(nc, m, r):
    with Tools(nc, "gla_finish") as a:
        o, o2, sg = (a.sb(n, [P, 2, T]) for n in ("o_sum", "o_sq", "o_gate"))
        ps = a.ps("ps_oms", [P, 2, 1024])
        ready, mm_s, rms, gate, chain = a.sems("gf_ready", "gf_sum", "gf_rms", "gf_gate", "gf_chain")
        with nc.Block() as block:

            @block.tensor
            def _(pe):
                pe.wait_ge(ready, 1)
                head_sum(pe, m, ps, o2).then_inc(mm_s, 1)

            @block.scalar
            def _(act):
                act.activation(sg[:], m.proj[:, GG:GG + 2, :], ACT.Sigmoid).then_inc(gate, 1)
                act.wait_ge(ready, 2)
                act.activation(o2[:], o2[:], ACT.Sqrt).then_inc(rms, 1)

            @block.vector
            def _(dve):
                ch = Chain(dve, chain)
                ch.link(dve.tensor_add(o[:], r.o[0][:], r.o[1][:]))
                dve.tensor_mul(o2[:], o[:], o[:]).then_inc(ready, 1)
                dve.wait_ge(gate, 1)
                ch.link(dve.tensor_mul(sg[:], sg[:], m.proj[:, GG:GG + 2, :]))
                for c in range(2):
                    ch.link(dve.tensor_scalar(sg[:, c, :], sg[:, c, :], m.vec[:, GNORM + c:GNORM + c + 1], None,
                                              ALU.mult))
                dve.wait_ge(mm_s, 1)
                dve.tensor_scalar(o2[:], ps[:, :, 0:T], 1.0 / 64, EPS, ALU.mult, ALU.add).then_inc(ready, 1)
                dve.wait_ge(rms, 1)
                ch.link(dve.reciprocal(o2[:], o2[:]))
                ch.link(dve.tensor_mul(o[:], o[:], o2[:]))
                dve.tensor_mul(m.branch[:, 4:6, :], o[:], sg[:])


def gla(nc, m):
    with Tools(nc, "gla") as a:
        two = lambda n, shape: [a.sb(f"{n}{d}", shape) for d in range(2)]
        r = Stage()
        r.q = a.sb("g_q", [P, T])
        r.cum, r.qd, r.kd = two("g_cum", [P, T]), two("g_qd", [P, T]), two("g_kd", [P, T])
        r.end = two("g_end", [P, NT])
        gla_prepare(nc, m, r)
        r.vtok, r.vpad = a.sb("g_vtok", [P, NT, BW]), a.sb("g_vpad", [P, NT, 4, P])
        r.kdtok = two("g_kdtok", [P, NT, P])
        r.sc = two("g_sc", [P, NT, 4, P])
        zero_pads(nc, a, r.vpad)
        items = []
        for t in range(NT):
            cut = slice(t * P, (t + 1) * P)
            for c in range(2):
                items.append(([(r.vtok[:, t, c * P:(c + 1) * P], 0, P), (r.vpad[:, t, 2 * c, 0:64], 0, 64),
                               (r.vpad[:, t, 2 * c + 1, 64:P], 64, P)], m.proj[:, GV + c, cut]))
            for d in range(2):
                items.append(([(r.kdtok[d][:, t, :], 0, P)], r.kd[d][:, cut]))
        turn_to_tokens(nc, m, items, "gla")
        gla_scores(nc, m, r)
        r.o = two("g_o", [P, 2, T])
        gla_scan(nc, m, r)
        gla_finish(nc, m, r)


def merge_branches(nc, m):
    with Tools(nc, "merge_branches") as a:
        hT = m.hT_back
        w = a.sb("w_merge_tiles", [P, 2, (KD + 2) * P])
        gate = a.sb("merge_gate", [P, 2, T])
        part = a.sb("merge_part", [P, 2, T])
        acc = a.sb("merge_acc", [P, T])
        ps_l = a.ps("ps_logit", [P, 2, 1024])
        ps_p = a.ps("ps_proj", [P, 2, 1024])
        w_in, ahead = a.ring("wm_in", 2), a.sem("out_ahead")
        done, gated, multiplied = a.ring("wm_done", 2), a.ring("wm_gate", 2), a.ring("wm_mul", 2)
        chain = a.sem("wm_chain")
        with nc.Block() as block:

            @block.sync
            def _(sp):
                def lap(i):
                    for b in range(2):
                        sp.wait_ge(done[b], i)
                        sp.dma_start(w[:, b, :], m.w_merge[bass.ds(2 * i + b, 1)].rearrange("a p n -> (a p) n")
                                     ).then_inc(w_in[b], 16)

                lap(0)
                sp.dma_start(m.w_out_sb, m.w_out[0].rearrange("(k p) n -> p k n", p=P)).then_inc(ahead, 16)
                sp.dma_start(m.x[:, 0:CTX, :], m.x_sample[0].rearrange("(t p) d -> p t d", p=P)).then_inc(ahead, 16)
                sp.dma_start(m.x[:, CTX, :], m.x_prompt[0]).then_inc(ahead, 16)
                with sp.Fori(1, KD * NB // 2) as i:
                    lap(i)
                sp.wait_ge(ahead, 48)

            @block.tensor
            def _(pe):
                def step(i):
                    for n in range(NB):
                        b, lap = n % 2, 2 * i + n // 2
                        pe.wait_ge(w_in[b], 16 * lap + 16)
                        pe.wait_ge(multiplied[b], lap)
                        for k in range(KD):
                            for lo, hi in ((0, 512), (512, T)):
                                pe.matmul(ps_l[:, b, lo:hi], w[:, b, k * P:(k + 1) * P], hT[:, k, lo:hi],
                                          start=(k == 0), stop=(k == KD - 1))
                        for k in range(2):
                            for lo, hi in ((0, 512), (512, T)):
                                mm = pe.matmul(ps_p[:, b, lo:hi], w[:, b, (KD + k) * P:(KD + k + 1) * P],
                                               m.branch[:, 2 * n + k, lo:hi], start=(k == 0), stop=(k == 1))
                        mm.then_inc(done[b], 1)

                step(0)
                with pe.Fori(1, KD) as i:
                    step(i)

            @block.scalar
            def _(act):
                def step(i):
                    for n in range(NB):
                        b, lap = n % 2, 2 * i + n // 2
                        act.wait_ge(done[b], lap + 1)
                        act.wait_ge(multiplied[b], lap)
                        act.activation(gate[:, b, :], ps_l[:, b, 0:T], ACT.Sigmoid).then_inc(gated[b], 1)

                step(0)
                with act.Fori(1, KD) as i:
                    step(i)

            @block.vector
            def _(dve):
                ch = Chain(dve, chain)
                with ch.laps(KD, 4) as i:
                    for n in range(NB):
                        b, lap = n % 2, 2 * i + n // 2
                        dve.wait_ge(gated[b], lap + 1)
                        dve.tensor_mul(part[:, b, :], gate[:, b, :], ps_p[:, b, 0:T]).then_inc(multiplied[b], 1)
                        dve.wait_ge(multiplied[b], lap + 1)
                        if n == 0:
                            ch.link(dve.tensor_copy(acc[:], part[:, b, :]))
                        elif n < NB - 1:
                            ch.link(dve.tensor_add(acc[:], acc[:], part[:, b, :]))
                        else:
                            ch.link(dve.tensor_add(m.merged[:, bass.ds(i, 1), :].rearrange("p a t -> p (a t)"),
                                                   acc[:], part[:, b, :]))


N_EXP, N_GRP, TOP_K, TOP_G, FF = 64, 8, 8, 4, 256
MAX_BLOCKS = N_EXP + T * TOP_K // P
TAB = 8
(B_EXPERT, B_PART, B_ROW, B_HALF, B_LOADS, U_EXPERT, U_BLOCK) = (0, 1, 2, 3, 4, 6, 7)


def group(t):
    return 0 if t == CTX else 1


def output_and_route(nc, m):
    with Tools(nc, "output_and_route") as a:
        w_out = m.w_out_sb
        w_r = a.sb("w_router_sb", [P, KD, N_EXP])
        w_gu = a.sb("ws_gu", [P, KD, 2 * FF])
        w_dn = a.sb("ws_dn", [P, 2, D])
        mod = a.sb("mod_rows_b", [P, 2, 3, D])
        sq = a.sb("sq_e", [P, D])
        h2 = a.sb("h2", [P, 2, D])
        h2T = [m.merged[:, :, t * P:(t + 1) * P] for t in range(NT)]
        ss, rms = a.sb("ss_e", [P, NT]), a.sb("rms_e", [P, NT])
        sg, hs, hsT = a.sb("sg_e", [P, FF]), a.sb("hs_e", [P, 2, FF]), a.sb("hsT_e", [P, 2, FF])
        bias = a.sb("b_router_b", [P, N_EXP])
        rc = a.sb("route_c", [P, N_EXP + 1 + NT])
        score = a.sb("score", [P, NT, N_EXP])
        sel, selm, chosen = a.sb("sel", [P, N_EXP]), a.sb("selm", [P, N_EXP]), a.sb("chosen", [P, NT, N_EXP])
        top, gs, g8, gm, pen = (a.sb(n, s) for n, s in (("top", [P, N_GRP, 8]), ("gs", [P, 8]), ("g8", [P, 8]),
                                                       ("gm", [P, 8]), ("pen", [P, 8])))
        idx_u, idx_g, eq_g = a.sb("idx_u", [P, 8], U32), a.sb("idx_g", [P, 8]), a.sb("eq_g", [P, TOP_G, N_GRP])
        e8, idx_e = a.sb("e8", [P, 8]), a.sb("idx_e", [P, NT, 8])
        eq = a.sb("eq_e", [P, NT, TOP_K, N_EXP])
        wide = a.sb("wide_e", [P, TOP_K, N_EXP])
        pos_in, pos8, addr = a.sb("pos_in", [P, N_EXP]), a.sb("pos8", [P, NT, 8]), a.sb("addr", [P, NT, 8])
        addr_u, tok_u = a.sb("addr_u", [P, NT, 8], U32), a.sb("tok_u", [P, NT], U32)
        zero_u = a.sb("zero_u", [P, N_EXP * T // P], U32)
        wsum = a.sb("wsum", [P, 1])
        cnt, nb, end, base, tmp = (a.sb(n, [P, N_EXP]) for n in ("cnt", "nblk", "end", "basee", "tmpe"))
        col = a.sb("col_e", [P, TAB])
        used, count = a.sb("used_e", [P, N_EXP]), a.sb("count_e", [P, N_EXP])
        ordinal, pairs, last, offset = (a.sb(n, [P, 1]) for n in ("ordinal", "pairs_e", "last_e", "offset_e"))
        tab = a.sb("tab", [P, TAB], I32)
        ps_mix, ps_t, ps_r = a.ps("ps_mix", [P, D]), a.ps("ps_t2", [P, D]), a.ps("ps_r", [P, 512])
        ps_gu, ps_y = a.ps("ps_gu", [P, 2 * FF]), a.ps("ps_y", [P, D])
        (w_in, r_in, mix_mm, mix_out, sq_ok, ms_ok, rms_ok, h2_ok, h2_store, turned, h2T_ok, r_mm, r_out, gu_mm, sig_ok,
         hs_ok, hs_turned, hsT_ok, y_mm, y_out, m_ok, pos_mm, pos_ok, zeroed, list_zero, addr_ok, scattered, cnt_mm,
         tab_ok, tab_store, tab_in, e_chain) = a.sems(*(f"e_{n}" for n in (
            "w_in", "r_in", "mix_mm", "mix_out", "sq_ok", "ms_ok", "rms_ok", "h2_ok", "h2_store", "turned", "h2T_ok", "r_mm",
            "r_out", "gu_mm", "sig_ok", "hs_ok", "hs_turned", "hsT_ok", "y_mm", "y_out", "m_ok", "pos_mm", "pos_ok",
            "zeroed", "list_zero", "addr_ok", "scattered", "cnt_mm", "tab_ok", "tab_store", "tab_in", "chain")))
        iota_e, iota_p = rc[:, 0:N_EXP], rc[:, N_EXP:N_EXP + 1]
        ident, ones, before = (m.const[:, n * P:(n + 1) * P] for n in (IDENT, ONES, LT))
        row = lambda ap, n: ap.unsqueeze(1).to_broadcast([P, n, ap.shape[1]])
        with nc.Block() as block:

            @block.sync
            def _(sp):
                for i, g in enumerate((0, 1)):
                    for j, r in enumerate((2, 3, 4)):
                        sp.dma_start(mod[:, g, j, :], m.mod_dram[g, r:r + 1, :].to_broadcast([P, D])
                                     ).then_inc(w_in, 16)
                sp.dma_start(w_r[:], m.w_router[0].rearrange("(p k) n -> p k n", k=KD)).then_inc(r_in, 16)
                sp.dma_start(bias[:], m.b_router.to_broadcast([P, N_EXP])).then_inc(r_in, 16)
                sp.dma_start(rc[:], m.route_constants).then_inc(r_in, 16)
                sp.dma_start(w_gu[:, :, 0:FF], m.ws_gate[0].rearrange("(p k) n -> p k n", k=KD)).then_inc(r_in, 16)
                sp.dma_start(w_gu[:, :, FF:], m.ws_up[0].rearrange("(p k) n -> p k n", k=KD)).then_inc(r_in, 16)
                sp.dma_start(w_dn[:], m.ws_down[0].rearrange("(k p) n -> p k n", p=P)).then_inc(r_in, 16)
                for t in range(NT):
                    sp.wait_ge(h2_ok, t + 1)
                    if t >= 1:
                        sp.wait_ge(h2_store, 16 * t)
                    sp.dma_start(m.h2_dram[t * P:(t + 1) * P, :], h2[:, t % 2, :]).then_inc(h2_store, 16)
                sp.wait_ge(tab_ok, 1)
                sp.dma_start(m.tab_dram, tab[:]).then_inc(tab_store, 16)
                sp.wait_ge(tab_store, 16)
                sp.dma_start(m.table[:], m.tab_dram.rearrange("b c -> (b c)").unsqueeze(0)).then_inc(tab_in, 16)
                sp.wait_ge(tab_in, 16)
                sp.wait_ge(h2_store, 16 * NT)

            @block.gpsimd
            def _(pool):
                pool.memset(zero_u[:], 0).then_inc(zeroed, 1)
                pool.wait_ge(zeroed, 1)
                pool.dma_start(m.list_dram.rearrange("(p n) a -> p (n a)", p=P), zero_u[:]).then_inc(list_zero, 16)
                pool.wait_ge(list_zero, 16)
                for t in range(NT):
                    pool.wait_ge(addr_ok, t + 1)
                    for j in range(TOP_K):
                        pool.indirect_dma_start(
                            m.list_dram, bass.IndirectOffsetOnAxis(ap=addr_u[:, t, j:j + 1], axis=0),
                            tok_u[:, t:t + 1], None).then_inc(scattered, 16)
                        pool.wait_ge(scattered, 16 * (t * TOP_K + j + 1))

            @block.tensor
            def _(pe):
                def mix(t):
                    pe.wait_ge(mix_out, t)
                    for n in range(2):
                        for k in range(KD):
                            mm = pe.matmul(ps_mix[:, n * 512:(n + 1) * 512], m.merged[:, k, t * P:(t + 1) * P],
                                           w_out[:, k, n * 512:(n + 1) * 512], start=(k == 0), stop=(k == KD - 1))
                    mm.then_inc(mix_mm, 1)

                def turn(t):
                    pe.wait_ge(h2_ok, t + 1)
                    if t >= 1:
                        pe.wait_ge(h2T_ok, t)
                    for k in range(KD):
                        mm = pe.transpose(ps_t[:, k * P:(k + 1) * P], h2[:, t % 2, k::KD], ident)
                    mm.then_inc(turned, 1)

                def route(t):
                    pe.wait_ge(h2T_ok, t + 1)
                    pe.wait_ge(pos_ok, t)
                    for k in range(KD):
                        mm = pe.matmul(ps_r[:, 0:N_EXP], h2T[t][:, k, :], w_r[:, k, :],
                                       start=(k == 0), stop=(k == KD - 1))
                    mm.then_inc(r_mm, 1)

                def gate_up(t):
                    pe.wait_ge(hs_ok, t)
                    for k in range(KD):
                        mm = pe.matmul(ps_gu[:], h2T[t][:, k, :], w_gu[:, k, :],
                                       start=(k == 0), stop=(k == KD - 1))
                    mm.then_inc(gu_mm, 1)

                def place(t):
                    pe.wait_ge(m_ok, t + 1)
                    pe.matmul(ps_r[:, 128:128 + N_EXP], before, chosen[:, t, :], start=True, stop=(t == 0))
                    for u in range(t):
                        pe.matmul(ps_r[:, 128:128 + N_EXP], ones, chosen[:, u, :], start=False, stop=(u == t - 1))
                    pe.matmul(ps_r[:, 256:257], ones, chosen[:, t, 0:1], start=True, stop=True).then_inc(pos_mm, 1)

                def down(t):
                    pe.wait_ge(hs_ok, t + 1)
                    pe.wait_ge(h2T_ok, NT)
                    for k in range(2):
                        mm = pe.transpose(ps_t[:, k * P:(k + 1) * P], hs[:, t % 2, k * P:(k + 1) * P], ident)
                    mm.then_inc(hs_turned, 1)
                    pe.wait_ge(hsT_ok, t + 1)
                    pe.wait_ge(y_out, t)
                    for n in range(2):
                        for k in range(2):
                            mm = pe.matmul(ps_y[:, n * 512:(n + 1) * 512], hsT[:, t % 2, k * P:(k + 1) * P],
                                           w_dn[:, k, n * 512:(n + 1) * 512], start=(k == 0), stop=(k == 1))
                    mm.then_inc(y_mm, 1)

                mix(0)
                mix(1)
                turn(0)
                pe.wait_ge(r_in, 16 * 6)
                for t in range(NT):
                    if t + 2 < NT:
                        mix(t + 2)
                    else:
                        gate_up(t + 2 - NT)
                    if t >= 1:
                        place(t - 1)
                    route(t)
                    if t + 1 < NT:
                        turn(t + 1)
                place(NT - 1)
                pe.wait_ge(pos_ok, NT)
                for t in range(NT):
                    mm = pe.matmul(ps_r[:, 0:N_EXP], ones, chosen[:, t, :], start=(t == 0), stop=(t == NT - 1))
                mm.then_inc(cnt_mm, 1)
                down(0)
                for t in range(1, NT):
                    if t + 1 < NT:
                        gate_up(t + 1)
                    down(t)

            @block.scalar
            def _(act):
                def norm(t):
                    act.wait_ge(mix_out, t + 1)
                    act.activation(sq[:], m.x[:, t, :], ACT.Square, accum_out=ss[:, t:t + 1]).then_inc(sq_ok, 1)
                    act.wait_ge(ms_ok, t + 1)
                    act.activation(rms[:, t:t + 1], ss[:, t:t + 1], ACT.Sqrt).then_inc(rms_ok, 1)

                def turn(t):
                    act.wait_ge(turned, t + 1)
                    act.activation(h2T[t], ps_t[:].rearrange("p (k t) -> p k t", k=KD), ACT.Copy
                                   ).then_inc(h2T_ok, 1)

                def down(t):
                    act.wait_ge(hs_turned, t + 1)
                    act.activation(hsT[:, t % 2, :], ps_t[:, 0:FF], ACT.Copy).then_inc(hsT_ok, 1)
                    act.wait_ge(y_mm, t + 1)
                    act.activation(m.acc[:, t, :], ps_y[:], ACT.Copy).then_inc(y_out, 1)

                def gate(t):
                    act.wait_ge(gu_mm, t + 1)
                    act.wait_ge(hs_ok, t)
                    act.activation(sg[:], ps_gu[:, 0:FF], ACT.Sigmoid).then_inc(sig_ok, 1)

                norm(0)
                norm(1)
                turn(0)
                for t in range(NT):
                    if t + 2 < NT:
                        norm(t + 2)
                    else:
                        gate(t + 2 - NT)
                    act.wait_ge(r_mm, t + 1)
                    act.activation(score[:, t, :], ps_r[:, 0:N_EXP], ACT.Sigmoid).then_inc(r_out, 1)
                    if t + 1 < NT:
                        turn(t + 1)
                down(0)
                for t in range(1, NT):
                    if t + 1 < NT:
                        gate(t + 1)
                    down(t)

            @block.vector
            def _(dve):
                ch = Chain(dve, e_chain)

                def residual(t):
                    g = group(t)
                    dve.wait_ge(mix_mm, t + 1)
                    if t >= 2:
                        dve.wait_ge(h2_store, 16 * (t - 1))
                        dve.wait_ge(turned, t - 1)
                    ch.link(dve.tensor_mul(h2[:, t % 2, :], ps_mix[:], mod[:, g, 0, :]))
                    dve.tensor_add(m.x[:, t, :], m.x[:, t, :], h2[:, t % 2, :]).then_inc(mix_out, 1)

                def norm(t):
                    g = group(t)
                    dve.wait_ge(sq_ok, t + 1)
                    dve.tensor_scalar(ss[:, t:t + 1], ss[:, t:t + 1], 1.0 / D, EPS, ALU.mult, ALU.add
                                      ).then_inc(ms_ok, 1)
                    dve.wait_ge(rms_ok, t + 1)
                    ch.link(dve.reciprocal(rms[:, t:t + 1], rms[:, t:t + 1]))
                    ch.link(dve.scalar_tensor_tensor(out=h2[:, t % 2, :], in0=m.x[:, t, :], scalar=rms[:, t:t + 1],
                                                     in1=mod[:, g, 2, :], op0=ALU.mult, op1=ALU.mult))
                    dve.tensor_add(h2[:, t % 2, :], h2[:, t % 2, :], mod[:, g, 1, :]).then_inc(h2_ok, 1)

                def silu(t):
                    dve.wait_ge(sig_ok, t + 1)
                    if t >= 2:
                        dve.wait_ge(hs_turned, t - 1)
                    ch.link(dve.tensor_mul(hs[:, t % 2, :], sg[:], ps_gu[:, 0:FF]))
                    dve.tensor_mul(hs[:, t % 2, :], hs[:, t % 2, :], ps_gu[:, FF:]).then_inc(hs_ok, 1)

                def choose(t):
                    dve.wait_ge(r_out, t + 1)
                    ch.link(dve.tensor_add(sel[:], score[:, t, :], bias[:]))
                    for g in range(N_GRP):
                        s = dve.max(top[:, g, :], sel[:, g * 8:(g + 1) * 8])
                    ch.link(s)
                    ch.link(dve.tensor_add(gs[:], top[:, :, 0], top[:, :, 1]))
                    ch.link(dve.max(g8[:], gs[:]))
                    ch.link(dve.max_index(idx_u[:], g8[:], gs[:]))
                    ch.link(dve.tensor_copy(idx_g[:], idx_u[:]))
                    ch.link(dve.tensor_tensor(eq_g[:], iota_e[:, 0:N_GRP].unsqueeze(1).to_broadcast([P, TOP_G, N_GRP]),
                                              idx_g[:, 0:TOP_G].unsqueeze(2).to_broadcast([P, TOP_G, N_GRP]),
                                              ALU.is_equal))
                    ch.link(dve.tensor_reduce(gm[:], eq_g[:].rearrange("p j g -> p g j"), AX.X, ALU.add))
                    ch.link(dve.tensor_scalar(pen[:], gm[:], 1.0, 1e30, ALU.subtract, ALU.mult))
                    members = lambda ap: ap.rearrange("p (g e) -> p g e", e=8)
                    of_group = lambda ap: ap.unsqueeze(2).to_broadcast([P, N_GRP, 8])
                    ch.link(dve.tensor_mul(members(selm[:]), members(sel[:]), of_group(gm[:])))
                    ch.link(dve.tensor_add(members(selm[:]), members(selm[:]), of_group(pen[:])))
                    ch.link(dve.max(e8[:], selm[:]))
                    ch.link(dve.max_index(idx_u[:], e8[:], selm[:]))
                    ch.link(dve.tensor_copy(idx_e[:, t, :], idx_u[:]))
                    ch.link(dve.tensor_tensor(eq[:, t], row(iota_e, TOP_K),
                                              idx_e[:, t, :].unsqueeze(2).to_broadcast([P, TOP_K, N_EXP]),
                                              ALU.is_equal))
                    dve.tensor_reduce(chosen[:, t, :], eq[:, t].rearrange("p j e -> p e j"), AX.X, ALU.add
                                      ).then_inc(m_ok, 1)
                    ch.link(dve.tensor_mul(wide[:], eq[:, t], row(score[:, t, :], TOP_K)))
                    ch.link(dve.tensor_reduce(m.weight[:, t, :], wide[:], AX.X, ALU.add))
                    ch.link(dve.tensor_reduce(wsum[:], m.weight[:, t, :], AX.X, ALU.add))
                    ch.link(dve.reciprocal(wsum[:], wsum[:]))
                    ch.link(dve.tensor_scalar(m.weight[:, t, :], m.weight[:, t, :], wsum[:], 2.5, ALU.mult, ALU.mult))

                def places(t):
                    dve.wait_ge(pos_mm, t + 1)
                    dve.tensor_copy(pos_in[:], ps_r[:, 128:128 + N_EXP]).then_inc(pos_ok, 1)
                    dve.wait_ge(pos_ok, t + 1)
                    ch.link(dve.tensor_mul(wide[:], eq[:, t], row(pos_in[:], TOP_K)))
                    ch.link(dve.tensor_reduce(pos8[:, t, :], wide[:], AX.X, ALU.add))
                    ch.link(dve.scalar_tensor_tensor(out=addr[:, t, :], in0=idx_e[:, t, :], scalar=float(T),
                                                     in1=pos8[:, t, :], op0=ALU.mult, op1=ALU.add))
                    dve.tensor_copy(addr_u[:, t, :], addr[:, t, :]).then_inc(addr_ok, 1)

                dve.wait_ge(w_in, 16 * 6)
                residual(0)
                norm(0)
                dve.wait_ge(r_in, 16 * 6)
                ch.link(dve.tensor_copy(tok_u[:], rc[:, N_EXP + 1:N_EXP + 1 + NT]))
                residual(1)
                norm(1)
                for t in range(NT):
                    if t + 2 < NT:
                        residual(t + 2)
                    if t >= 1:
                        places(t - 1)
                    if t + 2 < NT:
                        norm(t + 2)
                    elif t + 2 == NT:
                        silu(0)
                    choose(t)
                places(NT - 1)
                silu(1)
                dve.wait_ge(cnt_mm, 1)
                ch.link(dve.tensor_copy(cnt[:], ps_r[:, 0:N_EXP]))
                ch.link(dve.tensor_scalar(nb[:], cnt[:], 0.0, None, ALU.is_gt))
                for b in range(1, NT):
                    ch.link(dve.scalar_tensor_tensor(out=nb[:], in0=cnt[:], scalar=float(P * b), in1=nb[:],
                                                     op0=ALU.is_gt, op1=ALU.add))
                ch.link(dve.tensor_tensor_scan(end[:], ones[:, 0:N_EXP], nb[:], 0.0, ALU.mult, ALU.add))
                ch.link(dve.tensor_sub(base[:], end[:], nb[:]))
                def total(to):
                    ch.link(dve.tensor_reduce(to, tmp[:], AX.X, ALU.add))

                def take(to, of, expert):
                    ch.link(dve.tensor_scalar(tmp[:], iota_e, expert, None, ALU.is_equal))
                    ch.link(dve.tensor_mul(tmp[:], tmp[:], of))
                    total(to)

                c = lambda n: col[:, n:n + 1]
                ch.link(dve.tensor_scalar(tmp[:], end[:], iota_p, None, ALU.is_le))
                total(c(B_EXPERT))
                ch.link(dve.tensor_scalar(c(B_EXPERT), c(B_EXPERT), float(N_EXP - 1), None, ALU.min))
                take(c(B_PART), base[:], c(B_EXPERT))
                ch.link(dve.tensor_sub(c(B_PART), iota_p, c(B_PART)))
                ch.link(dve.tensor_scalar(c(B_PART), c(B_PART), 0.0, float(NT - 1), ALU.max, ALU.min))
                ch.link(dve.tensor_scalar(offset[:], c(B_PART), float(P), None, ALU.mult))
                ch.link(dve.tensor_scalar(tmp[:], iota_e, 2.0, end[:, N_EXP - 1:N_EXP], ALU.mult, ALU.is_lt))
                total(pairs[:])
                ch.link(dve.tensor_copy(m.laps[:, 0:1], pairs[:]))
                ch.link(dve.tensor_scalar(used[:], nb[:], 0.0, None, ALU.is_gt))
                ch.link(dve.tensor_tensor_scan(count[:], ones[:, 0:N_EXP], used[:], 0.0, ALU.mult, ALU.add))
                ch.link(dve.tensor_scalar(tmp[:], end[:], iota_p, None, ALU.is_le))
                ch.link(dve.tensor_mul(tmp[:], tmp[:], used[:]))
                total(ordinal[:])
                ch.link(dve.tensor_scalar(last[:], count[:, N_EXP - 1:N_EXP], 1.0, None, ALU.subtract))
                ch.link(dve.tensor_scalar(ordinal[:], ordinal[:], last[:], None, ALU.min))
                ch.link(dve.tensor_scalar(last[:], ordinal[:], 2.0, None, ALU.subtract))
                ch.link(dve.tensor_scalar(tmp[:], iota_e, 2.0, last[:], ALU.mult, ALU.is_le))
                total(pairs[:])
                ch.link(dve.tensor_scalar(last[:], pairs[:], -2.0, None, ALU.mult))
                ch.link(dve.tensor_add(c(B_HALF), last[:], ordinal[:]))
                ch.link(dve.tensor_scalar(c(B_LOADS), pairs[:], 1.0, 32.0, ALU.add, ALU.mult))
                ch.link(dve.tensor_add(c(B_LOADS + 1), pairs[:], c(B_HALF)))
                ch.link(dve.tensor_scalar(c(B_LOADS + 1), c(B_LOADS + 1), 1.0, 32.0, ALU.max, ALU.mult))
                ch.link(dve.tensor_scalar(tmp[:], count[:], iota_p, None, ALU.is_le))
                total(c(U_EXPERT))
                ch.link(dve.tensor_scalar(c(U_EXPERT), c(U_EXPERT), float(N_EXP - 1), None, ALU.min))
                take(c(U_BLOCK), base[:], c(U_EXPERT))
                ch.link(dve.tensor_scalar(tmp[:], iota_e, 2.0, count[:, N_EXP - 1:N_EXP], ALU.mult, ALU.is_lt))
                total(pairs[:])
                ch.link(dve.tensor_copy(m.laps[:, 1:2], pairs[:]))
                ch.link(dve.tensor_tensor_scan(end[:], ones[:, 0:N_EXP], cnt[:], 0.0, ALU.mult, ALU.add))
                ch.link(dve.tensor_sub(base[:], end[:], cnt[:]))
                take(c(B_ROW), base[:], c(B_EXPERT))
                ch.link(dve.tensor_add(c(B_ROW), c(B_ROW), offset[:]))
                dve.tensor_copy(tab[:], col[:]).then_inc(tab_ok, 1)
                ch.link(dve.scalar_tensor_tensor(out=last[:], in0=c(B_EXPERT), scalar=float(NT), in1=c(B_PART),
                                                 op0=ALU.mult, op1=ALU.add))
                ch.link(dve.tensor_copy(m.list_row[:], last[:]))
                for t in range(NT):
                    if t + 2 < NT:
                        silu(t + 2)
                    ch.link(dve.tensor_mul(wide[:], eq[:, t], row(base[:], TOP_K)))
                    ch.link(dve.tensor_reduce(addr[:, t, :], wide[:], AX.X, ALU.add))
                    ch.link(dve.tensor_add(addr[:, t, :], addr[:, t, :], pos8[:, t, :]))
                ch.link(dve.tensor_copy(m.y_row[:], addr[:]))


def experts(nc, m):
    with Tools(nc, "experts") as a:
        w_gu = a.sb("we_gu", [P, 2, KD, 2 * FF])
        w_dn = a.sb("we_dn", [P, 2, 2, D])
        idx = a.sb("idx_b", [P, 2, 1], U32)
        list_u, list_f, idx_all = a.sb("list_u", [P, P], U32), a.sb("list_f", [P, P]), a.sb("idx_all", [P, P], U32)
        xg = a.sb("xg", [P, 2, D])
        xT = a.sb("xgT", [P, 2, KD, P])
        sg, hs, hsT = a.sb("sg_b", [P, 2, FF]), a.sb("hs_b", [P, 2, FF]), a.sb("hsT_b", [P, 2, FF])
        y = a.sb("y_b", [P, 2, D])
        ps_x = a.ps("ps_x", [P, 2, D])
        ps_gu = a.ps("ps_gu_b", [P, 2, 2 * FF])
        ps_y = a.ps("ps_y_b", [P, D])
        (gu_in, dn_in, gathered, turned, xT_ok, sig_ok, mul_ok, hs_ok, hs_turned, hsT_ok,
         y_store) = (a.ring(f"b_{n}", 2) for n in (
            "gu_in", "dn_in", "gathered", "turned", "xT_ok", "sig_ok", "mul_ok", "hs_ok",
            "hs_turned", "hsT_ok", "y_store"))
        gu_mm, y_mm = a.sems("b_gu_mm", "b_y_mm")
        y_half_ok = [a.ring(f"b_y_half{c}_ok", 2) for c in range(2)]
        laps = lambda eng: eng.value_load(m.laps[0:1, 0:1], min_val=1, max_val=MAX_BLOCKS // 2)
        ident = m.const[:, 0:P]
        tick = a.sb("tick", [P, 1])
        pool_done, list_in, list_turn, list_ok = a.sems("b_pool_done", "b_list_in", "b_list_turn", "b_list_ok")

        def entry(eng, row, c, low, top):
            return eng.value_load(m.table[0:1, bass.ds(TAB * row + c, 1)], min_val=low, max_val=top)

        with nc.Block() as block:

            @block.sync
            def _(sp):
                n = sp.value_load(m.laps[0:1, 1:2], min_val=TOP_K // 2, max_val=N_EXP // 2)

                expert = lambda j: entry(sp, j, U_EXPERT, 0, N_EXP - 1)
                first = lambda j: entry(sp, j, U_BLOCK, 1, MAX_BLOCKS)
                of = lambda ap, e: ap[0][bass.ds(e, 1)]

                def load_gu(b, e):
                    for c, ap in enumerate((m.we_gate, m.we_up)):
                        sp.dma_start(w_gu[:, b, :, c * FF:(c + 1) * FF],
                                     of(ap, e).rearrange("a (p k) n -> p (a k) n", k=KD)).then_inc(gu_in[b], 16)

                def load_dn(b, e):
                    down = of(m.we_down, e).rearrange("a (k p) n -> k p (a n)", p=P)
                    for k in range(2):
                        sp.dma_start(w_dn[:, b, k, :], down[k]).then_inc(dn_in[b], 16)

                def pair(i):
                    e = [expert(2 * i + b) for b in range(2)]
                    blocks = [first(2 * i + b - 1) for b in range(2)]
                    for b in range(2):
                        sp.wait_ge(gu_mm, blocks[b])
                        load_gu(b, e[b])
                    for b in range(2):
                        sp.wait_ge(y_mm, 2 * blocks[b])
                        load_dn(b, e[b])

                e = [expert(b) for b in range(2)]
                for load in (load_gu, load_dn):
                    for b in range(2):
                        load(b, e[b])
                with sp.Fori(1, n) as i:
                    pair(i)

            @block.gpsimd
            def _(pool):
                pool.indirect_dma_start(list_u[:], None, m.list_dram.rearrange("(r p) c -> r (p c)", p=P),
                                        bass.IndirectOffsetOnAxis(ap=m.list_row[:], axis=0)).then_inc(list_in, 16)
                pool.memset(m.zero[:], 0.0).then_inc(pool_done, 1)
                n = laps(pool)
                pool.wait_ge(list_ok, 1)

                def gather(b, i):
                    pool.wait_ge(pool_done, 4 * i + 2 * b + 1)
                    pool.tensor_copy(idx[:, b, :], idx_all[:, bass.ds(2 * i + b, 1)]).then_inc(pool_done, 1)
                    pool.wait_ge(pool_done, 4 * i + 2 * b + 2)
                    pool.tensor_add(tick[:], m.zero[:], m.zero[:]).then_inc(pool_done, 1)
                    pool.indirect_dma_start(xg[:, b, :], None, m.h2_dram,
                                            bass.IndirectOffsetOnAxis(ap=idx[:, b, :], axis=0)
                                            ).then_inc(gathered[b], 16)

                for b in range(2):
                    gather(b, 0)

                def lap(i):
                    for b in range(2):
                        pool.wait_ge(turned[b], i + 1)
                        gather(b, i + 1)
                    for b in range(2):
                        at = entry(pool, 2 * i + b, B_ROW, 0, T * TOP_K + T - P)
                        pool.wait_ge(y_store[1 - b], 16 * (i + b))
                        for c in range(2):
                            pool.wait_ge(y_half_ok[c][b], i + 1)
                        pool.dma_start(m.y_dram[bass.ds(at, P), :], y[:, b, :]).then_inc(y_store[b], 16)

                lap(0)
                with pool.Fori(1, n) as i:
                    lap(i)
                for b in range(2):
                    pool.wait_ge(gathered[b], 16 * n + 16)
                    pool.wait_ge(y_store[b], 16 * n)

            @block.tensor
            def _(pe):
                n = laps(pe)
                pe.wait_ge(list_turn, 1)
                pe.transpose(ps_gu[:, 0, 0:P], list_f[:], ident).then_inc(list_turn, 1)

                def turn(b, i):
                    pe.wait_ge(gathered[b], 16 * i + 16)
                    for k in range(KD):
                        mm = pe.transpose(ps_x[:, b, k * P:(k + 1) * P], xg[:, b, k::KD], ident)
                    mm.then_inc(turned[b], 1)

                for b in range(2):
                    turn(b, 0)

                def lap(i):
                    half, loads = [0, 0], [0, 0]
                    for b in range(2):
                        blk = 2 * i + b
                        half[b] = entry(pe, blk, B_HALF, 0, 1)
                        loads[b] = [entry(pe, blk, B_LOADS + c, 32, 16 * N_EXP) for c in range(2)]
                        pe.wait_ge(xT_ok[b], i + 1)
                        for c in range(2):
                            pe.wait_ge(gu_in[c], loads[b][c])
                        pe.wait_ge(hsT_ok[b], i)
                        for k in range(KD):
                            mm = pe.matmul(ps_gu[:, b, :], xT[:, b, k, :],
                                           w_gu[:, bass.ds(half[b], 1), k, :].rearrange("p a n -> p (a n)"),
                                           start=(k == 0), stop=(k == KD - 1))
                        mm.then_inc(gu_mm, 1)
                    def turn_hs(b):
                        pe.wait_ge(hs_ok[b], i + 1)
                        for k in range(2):
                            mm = pe.transpose(ps_gu[:, b, k * P:(k + 1) * P], hs[:, b, k * P:(k + 1) * P], ident)
                        mm.then_inc(hs_turned[b], 1)

                    def down(b, c):
                        pe.wait_ge(hsT_ok[b], i + 1)
                        pe.wait_ge(dn_in[0], loads[b][0])
                        pe.wait_ge(dn_in[1], loads[b][1])
                        pe.wait_ge(y_half_ok[c][1 - b], i + b)
                        for k in range(2):
                            mm = pe.matmul(ps_y[:, c * 512:(c + 1) * 512], hsT[:, b, k * P:(k + 1) * P],
                                           w_dn[:, bass.ds(half[b], 1), k, c * 512:(c + 1) * 512
                                                ].rearrange("p a n -> p (a n)"), start=(k == 0), stop=(k == 1))
                        mm.then_inc(y_mm, 1)

                    turn_hs(0)
                    turn(0, i + 1)
                    down(0, 0)
                    turn_hs(1)
                    down(0, 1)
                    turn(1, i + 1)
                    down(1, 0)
                    down(1, 1)

                lap(0)
                with pe.Fori(1, n) as i:
                    lap(i)
                pairs = pe.value_load(m.laps[0:1, 1:2], min_val=1, max_val=N_EXP // 2)
                for c in range(2):
                    pe.wait_ge(gu_in[c], 32 * pairs)
                    pe.wait_ge(dn_in[c], 32 * pairs)

            @block.scalar
            def _(act):
                n = laps(act)

                def copy_x(b, i):
                    act.wait_ge(turned[b], i + 1)
                    act.activation(xT[:, b].rearrange("p k t -> p (k t)"), ps_x[:, b, :], ACT.Copy
                                   ).then_inc(xT_ok[b], 1)

                for b in range(2):
                    copy_x(b, 0)

                def lap(i):
                    for b in range(2):
                        act.wait_ge(gu_mm, 2 * i + b + 1)
                        act.activation(sg[:, b, :], ps_gu[:, b, 0:FF], ACT.Sigmoid).then_inc(sig_ok[b], 1)
                    def copy_hs(b):
                        act.wait_ge(hs_turned[b], i + 1)
                        act.activation(hsT[:, b, :], ps_gu[:, b, 0:FF], ACT.Copy).then_inc(hsT_ok[b], 1)

                    def copy_y(b):
                        act.wait_ge(y_mm, 4 * i + 2 * b + 2)
                        act.wait_ge(y_store[b], 16 * i)
                        act.activation(y[:, b, 512:D], ps_y[:, 512:D], ACT.Copy).then_inc(y_half_ok[1][b], 1)

                    copy_hs(0)
                    copy_x(0, i + 1)
                    copy_hs(1)
                    copy_y(0)
                    copy_x(1, i + 1)
                    copy_y(1)

                lap(0)
                with act.Fori(1, n) as i:
                    lap(i)

            @block.vector
            def _(dve):
                n = laps(dve)
                dve.wait_ge(list_in, 16)
                dve.tensor_copy(list_f[:], list_u[:]).then_inc(list_turn, 1)
                dve.wait_ge(list_turn, 2)
                dve.tensor_copy(idx_all[:], ps_gu[:, 0, 0:P]).then_inc(list_ok, 1)

                def lap(i):
                    for b in range(2):
                        dve.wait_ge(sig_ok[b], i + 1)
                        dve.tensor_mul(hs[:, b, :], sg[:, b, :], ps_gu[:, b, 0:FF]).then_inc(mul_ok[b], 1)
                        dve.wait_ge(mul_ok[b], i + 1)
                        dve.tensor_mul(hs[:, b, :], hs[:, b, :], ps_gu[:, b, FF:]).then_inc(hs_ok[b], 1)
                    for b in range(2):
                        dve.wait_ge(y_mm, 4 * i + 2 * b + 1)
                        dve.wait_ge(y_store[b], 16 * i)
                        dve.tensor_copy(y[:, b, 0:512], ps_y[:, 0:512]).then_inc(y_half_ok[0][b], 1)

                lap(0)
                with dve.Fori(1, n) as i:
                    lap(i)


def combine(nc, m):
    RING, ON_PE = TOP_K, 5
    with Tools(nc, "combine") as a:
        rows = a.sb("rows_g", [P, RING, D])
        gate = a.sb("gate_f", [P, 2, D])
        gf = a.sb("g_final_b", [P, D])
        diag = a.sb("diag_w", [P, 2, ON_PE, P])
        order = [0, 5, 1, 2, 6, 3, 7, 4]
        ps = a.ps("ps_sum", [P, 2, D])
        sq, out = a.sb("sq_f", [P, D]), a.sb("out_f", [P, 2, D])
        ss, rms = a.sb("ss_f", [P, NT]), a.sb("rms_f", [P, NT])
        got = a.ring("got", RING)
        (vec_in, used, added, diag_ok, summed, x_ok, ms_ok, sq_ok, rms_ok, out_ok, out_store, chain) = a.sems(
            "f_vec_in", "f_used", "f_added", "f_diag_ok", "f_summed", "f_x_ok", "f_ms_ok", "f_sq_ok", "f_rms_ok",
            "f_out_ok", "f_out_store", "f_chain")
        with nc.Block() as block:

            @block.sync
            def _(sp):
                for g in range(2):
                    sp.dma_start(gate[:, g, :], m.mod_dram[g, 5:6, :].to_broadcast([P, D])).then_inc(vec_in, 16)
                sp.dma_start(gf[:], m.g_final.unsqueeze(0).to_broadcast([P, D])).then_inc(vec_in, 16)
                for t in range(NT):
                    sp.wait_ge(out_ok, t + 1)
                    if t >= 1:
                        sp.wait_ge(out_store, 16 * t)
                    to = m.y_sample[0, t * P:(t + 1) * P, :] if t < CTX else m.y_prompt[0]
                    sp.dma_start(to, out[:, t % 2, :]).then_inc(out_store, 16)
                sp.wait_ge(out_store, 16 * NT)

            @block.gpsimd
            def _(pool):
                for n in range(NT * TOP_K):
                    t, j = n // TOP_K, order[n % TOP_K]
                    if t >= 1 and j < ON_PE:
                        pool.wait_ge(used, (t - 1) * ON_PE + j + 1)
                    elif t >= 1:
                        pool.wait_ge(added, (t - 1) * (TOP_K - ON_PE) + j - ON_PE + 1)
                    pool.indirect_dma_start(rows[:, j, :], None, m.y_dram[0:T * TOP_K, :],
                                            bass.IndirectOffsetOnAxis(ap=m.y_row[:, t, j:j + 1], axis=0)
                                            ).then_inc(got[j], 16)

            @block.tensor
            def _(pe):
                for t in range(NT):
                    pe.wait_ge(diag_ok, t + 1)
                    if t >= 2:
                        pe.wait_ge(summed, t - 1)
                    for j in range(ON_PE):
                        pe.wait_ge(got[j], 16 * (t + 1))
                        for c in range(2):
                            cut = slice(c * 512, (c + 1) * 512)
                            mm = pe.matmul(ps[:, t % 2, cut], diag[:, t % 2, j, :], rows[:, j, cut],
                                           start=(j == 0), stop=(j == ON_PE - 1))
                        mm.then_inc(used, 1)

            @block.scalar
            def _(act):
                for t in range(NT):
                    act.wait_ge(x_ok, t + 1)
                    act.activation(sq[:], m.x[:, t, :], ACT.Square, accum_out=ss[:, t:t + 1]).then_inc(sq_ok, 1)
                    act.wait_ge(ms_ok, t + 1)
                    act.activation(rms[:, t:t + 1], ss[:, t:t + 1], ACT.Sqrt).then_inc(rms_ok, 1)

            @block.vector
            def _(dve):
                ch = Chain(dve, chain)
                dve.wait_ge(vec_in, 48)
                def diagonals(t):
                    dve.tensor_mul(diag[:, t % 2], m.const[:, 0:P].unsqueeze(1).to_broadcast([P, ON_PE, P]),
                                   m.weight[:, t, 0:ON_PE].unsqueeze(2).to_broadcast([P, ON_PE, P])).then_inc(diag_ok, 1)

                diagonals(0)
                diagonals(1)
                for t in range(NT):
                    acc = m.acc[:, t, :]
                    for j in range(ON_PE, TOP_K):
                        dve.wait_ge(got[j], 16 * (t + 1))
                        dve.scalar_tensor_tensor(out=acc, in0=rows[:, j, :], scalar=m.weight[:, t, j:j + 1],
                                                 in1=acc, op0=ALU.mult, op1=ALU.add).then_inc(added, 1)
                        dve.wait_ge(added, t * (TOP_K - ON_PE) + j - ON_PE + 1)
                    dve.wait_ge(used, (t + 1) * ON_PE)
                    if t + 2 < NT:
                        diagonals(t + 2)
                    dve.tensor_add(acc, acc, ps[:, t % 2, :]).then_inc(summed, 1)
                    dve.wait_ge(summed, t + 1)
                    ch.link(dve.tensor_mul(acc, acc, gate[:, group(t), :]))
                    dve.tensor_add(m.x[:, t, :], m.x[:, t, :], acc).then_inc(x_ok, 1)
                    dve.wait_ge(sq_ok, t + 1)
                    dve.tensor_scalar(ss[:, t:t + 1], ss[:, t:t + 1], 1.0 / D, EPS, ALU.mult, ALU.add
                                      ).then_inc(ms_ok, 1)
                    dve.wait_ge(rms_ok, t + 1)
                    ch.link(dve.reciprocal(rms[:, t:t + 1], rms[:, t:t + 1]))
                    if t >= 2:
                        dve.wait_ge(out_store, 16 * (t - 1))
                    dve.scalar_tensor_tensor(out=out[:, t % 2, :], in0=m.x[:, t, :], scalar=rms[:, t:t + 1],
                                             in1=gf[:], op0=ALU.mult, op1=ALU.mult).then_inc(out_ok, 1)


def trunk_kernel(nc, dram):
    m = Stage()
    m.cond, m.lora, m.vectors, m.w_mix = (
        dram["cond"], dram["lora"], dram["vectors"], dram["w_mix"])
    m.w_merge, m.constants, m.route_constants, m.dft_channel = (
        dram["w_merge"], dram["constants"], dram["route_constants"], dram["dft_channel"])
    m.dft_lat, m.dft_ctx, m.x_prompt, m.x_sample = (
        dram["dft_lat"], dram["dft_ctx"], dram["x_prompt"], dram["x_sample"])
    m.state_rwkv, m.state_gla, m.w_mod, m.b_mod = (
        dram["state_rwkv"], dram["state_gla"], dram["w_mod"], dram["b_mod"])
    m.g_norm_mix, m.g_norm_ffn, m.rw_g_up, m.gla_a_up = (
        dram["g_norm_mix"], dram["g_norm_ffn"], dram["rw_g_up"], dram["gla_a_up"])
    m.w_out, m.w_router, m.b_router, m.we_gate = (
        dram["w_out"], dram["w_router"], dram["b_router"], dram["we_gate"])
    m.we_up, m.we_down, m.ws_gate, m.ws_up = (
        dram["we_up"], dram["we_down"], dram["ws_gate"], dram["ws_up"])
    m.ws_down, m.g_final, m.y_prompt, m.y_sample = (
        dram["ws_down"], dram["g_final"], dram["y_prompt"], dram["y_sample"])
    m.new_rwkv, m.new_gla = (
        dram["new_rwkv"], dram["new_gla"])
    scratch = lambda name, shape, dt=F32: nc.dram_tensor(name, shape, dt, kind="Internal").ap()
    m.mod_dram = scratch("mod_dram", [2, 6, D])
    m.hT_dram = scratch("hT_dram", [P, KD, T])
    m.h2_dram = scratch("h2_dram", [T, D])
    m.list_dram = scratch("list_dram", [N_EXP * T, 1], U32)
    m.tab_dram = scratch("tab_dram", [P, TAB], I32)
    m.y_dram = scratch("y_dram", [T * TOP_K + T, D])
    with Tools(nc, "trunk_kernel") as whole:
        m.const = whole.sb("const", [P, C_END * P])
        m.vec = whole.sb("vec", [P, N_VEC])
        m.zero = whole.sb("zero", [P, 1])
        with ExitStack() as branch_life:
            m.proj = branch_life.enter_context(nc.sbuf_tensor("proj", [P, N_MIX, T], F32, side="right"))
            norm_and_project(nc, m)
            m.branch = branch_life.enter_context(nc.sbuf_tensor("branch", [P, 2 * NB, T], F32, side="right"))
            fourier_and_conv(nc, m)
            rwkv(nc, m)
            with nc.sbuf_tensor("hT_back", [P, KD, T], F32, side="right") as m.hT_back:
                gla(nc, m)
                m.merged = whole.sb("merged", [P, KD, T])
                spare = flat(m.proj[:])
                m.w_out_sb = spare[:, 0:KD * D].rearrange("p (k n) -> p k n", k=KD)
                m.x = spare[:, KD * D:KD * D + NT * D].rearrange("p (t d) -> p t d", t=NT)
                m.acc = flat(m.branch[:]).rearrange("p (t d) -> p t d", t=NT)
                merge_branches(nc, m)
            m.weight = whole.sb("weight", [P, NT, TOP_K])
            m.y_row = whole.sb("y_row", [P, NT, TOP_K], U32)
            m.list_row = whole.sb("list_row", [P, 1], U32)
            m.laps = whole.sb("laps", [P, 2], I32)
            m.table = whole.sb("table", [1, TAB * P], I32)
            output_and_route(nc, m)
            experts(nc, m)
            combine(nc, m)


def constants():
    i, j = np.meshgrid(np.arange(P), np.arange(P), indexing="ij")
    blocks = [i == j, i // 64 == j // 64, i < j, i > j, i <= j, i >= j]
    for h in LEVELS:
        blocks.append((i // (2 * h) == j // (2 * h)) & (i % (2 * h) < h) & (j % (2 * h) >= h))
    for h in LEVELS:
        blocks.append((i // (2 * h) == j // (2 * h)) & (i % (2 * h) >= h) & (j % (2 * h) < h))
    blocks.append(i >= 0)
    for half in range(2):
        blocks.append(i // 32 == (j + P * half) // 64)
    out = np.concatenate([b.astype(np.float32) for b in blocks], axis=1)
    assert out.shape[1] == C_END * P
    return out


def fourier_constants():
    k = np.arange(64)
    one = np.exp(-2j * np.pi * np.outer(k, k) / 64)
    ch = np.kron(np.eye(2), one)
    channel = np.concatenate([ch.real, -ch.imag], axis=1)
    grid = np.kron(np.exp(-2j * np.pi * np.outer(np.arange(8), np.arange(8)) / 8), one) / np.sqrt(8 * 64 * 64)
    seq = np.exp(-2j * np.pi * np.outer(np.arange(P), np.arange(P)) / P) / np.sqrt(P * 64)
    lat = np.stack([grid.real, grid.imag], axis=0).reshape(2, 4, P, T_LAT).transpose(2, 1, 0, 3)
    ctx = np.stack([seq.real, seq.imag], axis=1)
    f = lambda v: np.ascontiguousarray(v.astype(np.float32))
    return f(channel), f(lat), f(ctx)


def pack_inputs(v):
    w = v["w_in"][0].reshape(P, KD, -1)
    zeros = lambda n: np.zeros((P, KD, n), np.float32)
    cols = lambda a, n: w[:, :, a:a + n]
    mix = np.concatenate([cols(0, 1152), cols(1152, 64), cols(1728, 16), zeros(16), cols(1744, 16), zeros(16),
                          cols(1216, 512), cols(1760, 1024)], axis=2)
    mix = mix.reshape(P, KD, N_MIX, P).transpose(2, 0, 1, 3).reshape(N_MIX, P, KD * P)
    merge = cols(2784, NB * D).reshape(P, KD, NB, KD, P).transpose(3, 2, 0, 1, 4)
    branch = v["w_branch"][0].reshape(NB, 2, P, KD, P).transpose(3, 0, 2, 1, 4)
    merge = np.concatenate([merge, branch], axis=3).reshape(KD * NB, P, (KD + 2) * P)
    col = lambda a: a.reshape(-1, P).T
    vectors = np.concatenate([col(v[n][0]) for n in (
        "rw_w0", "rw_a0", "rw_k_k", "rw_k_a", "rw_r_k", "rw_ln_w", "rw_ln_b", "gla_a_b", "gla_norm", "conv_w")], axis=1)
    cond = np.stack([v["c_ctx"].reshape(P, KD), v["c"].reshape(P, KD)], axis=2)
    lora = np.concatenate([v["rw_w_up"][0].reshape(64, BW), v["rw_a_up"][0].reshape(64, BW)], axis=0)
    c = np.ascontiguousarray
    return {"w_mix": c(mix), "w_merge": c(merge), "vectors": c(vectors), "cond": c(cond), "lora": c(lora)}


def route_constants():
    p = np.arange(P)[:, None]
    return np.concatenate([np.broadcast_to(np.arange(N_EXP), (P, N_EXP)), p, p + P * np.arange(NT)[None]],
                          axis=1).astype(np.float32)


_INS = ["x_prompt", "x_sample", "state_rwkv", "state_gla", "w_mod", "b_mod", "g_norm_mix", "g_norm_ffn",
        "rw_g_up", "gla_a_up", "w_out", "w_router", "b_router", "we_gate", "we_up", "we_down",
        "ws_gate", "ws_up", "ws_down", "g_final"]
_OUTS = [("y_prompt", (1, T_CTX, D)), ("y_sample", (1, T_LAT, D)), ("new_rwkv", (1, 1, 2, 4, 64, 64)),
         ("new_gla", (1, 1, 2, 4, 32, 64))]


def kernel(**inputs):
    import concourse.bacc as bacc
    from concourse.bass_utils import run_bass_kernel_spmd

    v = {name: np.asarray(a) for name, a in inputs.items()}
    arrays = {name: np.ascontiguousarray(v[name]) for name in _INS}
    arrays.update(pack_inputs(v))
    arrays["constants"] = constants()
    arrays["route_constants"] = route_constants()
    arrays["dft_channel"], arrays["dft_lat"], arrays["dft_ctx"] = fourier_constants()
    nc = bacc.Bacc("TRN2", target_bir_lowering=False, num_devices=1)
    dram = {name: nc.dram_tensor(name, a.shape, mybir.dt.from_np(a.dtype), kind="ExternalInput").ap()
            for name, a in arrays.items()}
    for name, shape in _OUTS:
        dram[name] = nc.dram_tensor(name, shape, F32, kind="ExternalOutput").ap()
    trunk_kernel(nc, dram)
    r = run_bass_kernel_spmd(nc, [arrays], core_ids=[0])
    return tuple(r.results[0][name] for name, _ in _OUTS)
```
